# Optimizing a Trainium2 kernel written in Bass

```python
import jax, jax.numpy as jnp
from jax import lax
import numpy as np
import math

D_MODEL = 1024
BATCH = 1
SEQ = 256
DEPTH = 1

CONV_DIM = 512
CONV_WIDTH = 31
GLA_HEADS = 4
GLA_DK = 128
GLA_DV = 256
GLA_LOWRANK = 16
GLA_TAU = 16.0
GLA_CHUNK = 64
QK_DIM = GLA_HEADS * GLA_DK
V_DIM = GLA_HEADS * GLA_DV
N_BRANCH = 2
N_GROUPS = 4
EXPERTS_PER_GROUP = 8
N_EXPERTS = N_GROUPS * EXPERTS_PER_GROUP
TOP_K = 2
D_EXPERT = 512
EPS = 1e-6
N_MOD = 6
IN_SIZES = (2 * CONV_DIM, QK_DIM, QK_DIM, V_DIM, V_DIM, GLA_LOWRANK, N_BRANCH * D_MODEL)
IN_DIM = 2 * CONV_DIM + 2 * QK_DIM + 2 * V_DIM + GLA_LOWRANK + N_BRANCH * D_MODEL


def rmsnorm(x, g):
    x32 = x.astype(jnp.float32)
    y = x32 * lax.rsqrt(jnp.mean(x32 * x32, axis=-1, keepdims=True) + EPS)
    return (y * g.astype(jnp.float32)).astype(x.dtype)

def layernorm(x, g, b):
    x32 = x.astype(jnp.float32)
    mu = jnp.mean(x32, axis=-1, keepdims=True)
    xc = x32 - mu
    var = jnp.mean(xc * xc, axis=-1, keepdims=True)
    y = xc * lax.rsqrt(var + EPS) * g.astype(jnp.float32) + b.astype(jnp.float32)
    return y.astype(x.dtype)

def modulate(x, shift, scale):
    return x * (1.0 + scale[:, None, :]) + shift[:, None, :]

def conv_module(u, w_dw, b_dw, ln_g, ln_b, w_pw, b_pw):
    a, gt = jnp.split(u, 2, axis=-1)
    z = a * jax.nn.sigmoid(gt)
    z = lax.conv_general_dilated(
        z, w_dw, window_strides=(1,), padding=[(CONV_WIDTH - 1, 0)],
        dimension_numbers=("NWC", "WIO", "NWC"), feature_group_count=CONV_DIM) + b_dw
    z = jax.nn.silu(layernorm(z, ln_g, ln_b))
    return z @ w_pw + b_pw

def gla_chunked(q, k, v, logg):
    B, S, H, _ = q.shape
    n_chunks = S // GLA_CHUNK

    def to_chunks(t):
        return t.reshape(B, n_chunks, GLA_CHUNK, H, t.shape[-1]).transpose(1, 0, 3, 2, 4)

    causal = jnp.tril(jnp.ones((GLA_CHUNK, GLA_CHUNK), dtype=bool))[:, :, None]

    def step(state, inp):
        qc, kc, vc, gc = inp
        b = jnp.cumsum(gc, axis=2)
        o_inter = jnp.einsum("bhcd,bhde->bhce", qc * jnp.exp(b), state)
        diff = b[:, :, :, None, :] - b[:, :, None, :, :]
        decay = jnp.exp(jnp.where(causal, diff, -jnp.inf))
        attn = jnp.einsum("bhid,bhijd,bhjd->bhij", qc, decay, kc)
        o_intra = jnp.einsum("bhij,bhje->bhie", attn, vc)
        b_last = b[:, :, -1:, :]
        new_state = (jnp.exp(b_last[:, :, 0, :])[..., None] * state
                     + jnp.einsum("bhcd,bhce->bhde", kc * jnp.exp(b_last - b), vc))
        return new_state, o_inter + o_intra

    state0 = jnp.zeros((B, H, q.shape[-1], v.shape[-1]), jnp.float32)
    _, outs = lax.scan(step, state0, (to_chunks(q), to_chunks(k), to_chunks(v), to_chunks(logg)))
    return outs.transpose(1, 0, 3, 2, 4).reshape(B, S, H, v.shape[-1])

def hybrid_mixer(u, w_in, w_dw, b_dw, g_conv_ln, b_conv_ln, w_conv_pw, b_conv_pw,
                 w_a2, b_a2, g_gla_norm, w_gla_o, w_out):
    B, S, _ = u.shape
    proj = u @ w_in
    offs = np.cumsum(IN_SIZES)[:-1].tolist()
    p_conv, q, k, v, r, a1, gates = jnp.split(proj, offs, axis=-1)
    y_conv = conv_module(p_conv, w_dw, b_dw, g_conv_ln, b_conv_ln, w_conv_pw, b_conv_pw)
    q = q.reshape(B, S, GLA_HEADS, GLA_DK).astype(jnp.float32) * (GLA_DK ** -0.5)
    k = k.reshape(B, S, GLA_HEADS, GLA_DK).astype(jnp.float32)
    v = v.reshape(B, S, GLA_HEADS, GLA_DV).astype(jnp.float32)
    logg = jax.nn.log_sigmoid((a1 @ w_a2 + b_a2).astype(jnp.float32)) / GLA_TAU
    logg = logg.reshape(B, S, GLA_HEADS, GLA_DK)
    o = gla_chunked(q, k, v, logg)
    o = rmsnorm(o, g_gla_norm.reshape(GLA_HEADS, GLA_DV)).reshape(B, S, V_DIM).astype(u.dtype)
    y_gla = (o * jax.nn.silu(r)) @ w_gla_o
    gt = jax.nn.sigmoid(gates).reshape(B, S, N_BRANCH, D_MODEL)
    merged = gt[:, :, 0, :] * y_conv + gt[:, :, 1, :] * y_gla
    return merged @ w_out

def hierarchical_moe(h, w_rg, b_rg, w_re, b_re, w1, w3, w2):
    B, S, D = h.shape
    t = h.reshape(B * S, D)
    lg = (t @ w_rg + b_rg).astype(jnp.float32)
    pg = jax.nn.softmax(lg, axis=-1)
    _, gsel = lax.top_k(lg, 1)
    wg = jnp.take_along_axis(pg, gsel, axis=1)
    le = (t @ w_re + b_re).astype(jnp.float32).reshape(-1, N_GROUPS, EXPERTS_PER_GROUP)
    le_sel = jnp.take_along_axis(le, gsel[:, :, None], axis=1)[:, 0, :]
    top_v, top_i = lax.top_k(le_sel, TOP_K)
    w = jax.nn.softmax(top_v, axis=-1) * wg
    eid = gsel * EXPERTS_PER_GROUP + top_i
    comb = jnp.einsum("tk,tke->te", w, jax.nn.one_hot(eid, N_EXPERTS, dtype=jnp.float32))
    y = jnp.zeros((B * S, D), jnp.float32)
    for e in range(N_EXPERTS):
        hid = jax.nn.silu(t @ w1[e]) * (t @ w3[e])
        y = y + comb[:, e:e + 1] * (hid @ w2[e]).astype(jnp.float32)
    return y.astype(h.dtype).reshape(B, S, D)

def first_inputs(seed: int = 0) -> dict:
    key = jax.random.key(seed)
    ks = jax.random.split(key, 32)
    f32 = jnp.float32
    L, D = DEPTH, D_MODEL

    def nrm(k, shape, scale):
        return jax.random.normal(k, shape, f32) * scale

    def gain(k, shape):
        return 1.0 + 0.05 * jax.random.normal(k, shape, f32)

    return {
        "x": jax.random.normal(ks[0], (BATCH, SEQ, D), f32),
        "c": jax.random.normal(ks[1], (BATCH, D), f32),
        "w_ada": nrm(ks[2], (L, D, N_MOD * D), 0.5 * D ** -0.5),
        "b_ada": nrm(ks[3], (L, N_MOD * D), 0.02),
        "g_norm1": gain(ks[4], (L, D)),
        "w_in": nrm(ks[5], (L, D, IN_DIM), D ** -0.5),
        "w_dw": nrm(ks[6], (L, CONV_WIDTH, 1, CONV_DIM), CONV_WIDTH ** -0.5),
        "b_dw": nrm(ks[7], (L, CONV_DIM), 0.02),
        "g_conv_ln": gain(ks[8], (L, CONV_DIM)),
        "b_conv_ln": nrm(ks[9], (L, CONV_DIM), 0.02),
        "w_conv_pw": nrm(ks[10], (L, CONV_DIM, D), CONV_DIM ** -0.5),
        "b_conv_pw": nrm(ks[11], (L, D), 0.02),
        "w_a2": nrm(ks[12], (L, GLA_LOWRANK, QK_DIM), GLA_LOWRANK ** -0.5),
        "b_a2": nrm(ks[13], (L, QK_DIM), 0.02),
        "g_gla_norm": gain(ks[14], (L, V_DIM)),
        "w_gla_o": nrm(ks[15], (L, V_DIM, D), V_DIM ** -0.5),
        "w_out": nrm(ks[16], (L, D, D), D ** -0.5),
        "g_norm2": gain(ks[17], (L, D)),
        "w_router_g": nrm(ks[18], (L, D, N_GROUPS), D ** -0.5),
        "b_router_g": nrm(ks[19], (L, N_GROUPS), 0.01),
        "w_router_e": nrm(ks[20], (L, D, N_EXPERTS), D ** -0.5),
        "b_router_e": nrm(ks[21], (L, N_EXPERTS), 0.01),
        "w1": nrm(ks[22], (L, N_EXPERTS, D, D_EXPERT), D ** -0.5),
        "w3": nrm(ks[23], (L, N_EXPERTS, D, D_EXPERT), D ** -0.5),
        "w2": nrm(ks[24], (L, N_EXPERTS, D_EXPERT, D), D_EXPERT ** -0.5),
        "w_ada_f": nrm(ks[25], (D, 2 * D), 0.5 * D ** -0.5),
        "b_ada_f": nrm(ks[26], (2 * D,), 0.02),
        "g_final": gain(ks[27], (D,)),
    }

def first_block(x, c, w_ada, b_ada, g_norm1, w_in, w_dw, b_dw, g_conv_ln, b_conv_ln,
              w_conv_pw, b_conv_pw, w_a2, b_a2, g_gla_norm, w_gla_o, w_out, g_norm2,
              w_router_g, b_router_g, w_router_e, b_router_e, w1, w3, w2,
              w_ada_f, b_ada_f, g_final):
    h = x
    c_act = jax.nn.silu(c)
    for l in range(DEPTH):
        mod = c_act @ w_ada[l] + b_ada[l]
        sh1, sc1, ga1, sh2, sc2, ga2 = jnp.split(mod, N_MOD, axis=-1)
        u = modulate(rmsnorm(h, g_norm1[l]), sh1, sc1)
        y = hybrid_mixer(u, w_in[l], w_dw[l], b_dw[l], g_conv_ln[l], b_conv_ln[l],
                         w_conv_pw[l], b_conv_pw[l], w_a2[l], b_a2[l], g_gla_norm[l],
                         w_gla_o[l], w_out[l])
        h = h + ga1[:, None, :] * y
        u2 = modulate(rmsnorm(h, g_norm2[l]), sh2, sc2)
        y2 = hierarchical_moe(u2, w_router_g[l], b_router_g[l], w_router_e[l], b_router_e[l],
                              w1[l], w3[l], w2[l])
        h = h + ga2[:, None, :] * y2
    modf = c_act @ w_ada_f + b_ada_f
    shf, scf = jnp.split(modf, 2, axis=-1)
    return modulate(rmsnorm(h, g_final), shf, scf)


ATTN_GROUPS = ((128, 1), (512, 4), (2048, 16))
N_ATTN_GROUPS = len(ATTN_GROUPS)
HEADS_PER_GROUP = 6
ATTN_HEADS = N_ATTN_GROUPS * HEADS_PER_GROUP
HEAD_DIM = 64
ATTN_WIDTH = ATTN_HEADS * HEAD_DIM
ATTN_OUT_WIDTH = HEADS_PER_GROUP * HEAD_DIM
REL_BUCKETS = 32
REL_MAX_DISTANCE = 2048
POOL_WINDOWS = (2, 4, 8, 16)
POOL_WIDTH = D_MODEL
POOL_GROUP = POOL_WIDTH // len(POOL_WINDOWS)
SSD_INNER = D_MODEL
SSD_HEAD_DIM = 64
SSD_HEADS = SSD_INNER // SSD_HEAD_DIM
SSD_GROUPS = 2
SSD_STATE = 128
SSD_CONV = 4
SSD_CHUNK = 128
SSD_XBC = SSD_INNER + 2 * SSD_GROUPS * SSD_STATE
D_FF = 2816
FFN_CONV = 3
N_BRANCH_2 = 3
NORM_EPS = 1e-6
IN_SPLIT_SIZES = (ATTN_WIDTH, ATTN_WIDTH, ATTN_WIDTH, POOL_WIDTH, SSD_INNER, SSD_XBC, SSD_HEADS, N_BRANCH_2 * D_MODEL)
IN_WIDTH = sum(IN_SPLIT_SIZES)


def rmsnorm_2(x, g):
    xf = x.astype(jnp.float32)
    y = xf * lax.rsqrt(jnp.mean(xf * xf, axis=-1, keepdims=True) + NORM_EPS)
    return (y * g.astype(jnp.float32)).astype(x.dtype)

def causal_dwconv(x, w, b):
    K = w.shape[0]
    s = x.shape[1]
    xp = jnp.pad(x, ((0, 0), (K - 1, 0), (0, 0)))
    y = xp[:, 0:s] * w[0]
    for k in range(1, K):
        y = y + xp[:, k:k + s] * w[k]
    return y + b

def t5_bucket(dist):
    max_exact = REL_BUCKETS // 2
    is_small = dist < max_exact
    nf = jnp.maximum(dist, 1).astype(jnp.float32)
    large = max_exact + (jnp.log(nf / max_exact) / math.log(REL_MAX_DISTANCE / max_exact)
                         * (REL_BUCKETS - max_exact)).astype(jnp.int32)
    large = jnp.minimum(large, REL_BUCKETS - 1)
    return jnp.where(is_small, dist, large)

def dilated_group_attention(q, k, v, bias_table, dilation, steps):
    b, s, h, dh = q.shape
    L = s // dilation
    W = steps
    nb = -(-L // W)
    Lp = nb * W
    bd = b * dilation

    def to_res(t):
        return t.reshape(b, L, dilation, h, dh).transpose(0, 2, 3, 1, 4).reshape(bd, h, L, dh)

    qb = jnp.pad(to_res(q), ((0, 0), (0, 0), (0, Lp - L), (0, 0))).reshape(bd, h, nb, W, dh)
    kr = jnp.pad(to_res(k), ((0, 0), (0, 0), (W, Lp - L), (0, 0))).reshape(bd, h, nb + 1, W, dh)
    vr = jnp.pad(to_res(v), ((0, 0), (0, 0), (W, Lp - L), (0, 0))).reshape(bd, h, nb + 1, W, dh)
    kb = jnp.concatenate([kr[:, :, :-1], kr[:, :, 1:]], axis=3)
    vb = jnp.concatenate([vr[:, :, :-1], vr[:, :, 1:]], axis=3)

    qi = jnp.arange(W)[:, None]
    kk = jnp.arange(2 * W)[None, :]
    rel = qi + W - kk
    band = (rel >= 0) & (rel <= W)
    kabs = jnp.arange(nb)[:, None, None] * W + kk[None] - W
    valid = band[None] & (kabs >= 0)
    bucket = t5_bucket(jnp.clip(rel, 0, None) * dilation)
    bias = bias_table[bucket].transpose(2, 0, 1).astype(jnp.float32)

    scale = 1.0 / math.sqrt(dh)
    scores = jnp.einsum("bhnqd,bhnkd->bhnqk", qb, kb).astype(jnp.float32) * scale + bias[:, None]
    scores = jnp.where(valid[None, None], scores, -jnp.inf)
    m = jnp.max(scores, axis=-1, keepdims=True)
    p = jnp.exp(scores - m)
    l = jnp.sum(p, axis=-1)
    o = jnp.einsum("bhnqk,bhnkd->bhnqd", p, vb.astype(jnp.float32)) / l[..., None]
    lse = m[..., 0] + jnp.log(l)

    o = o.reshape(bd, h, Lp, dh)[:, :, :L].reshape(b, dilation, h, L, dh)
    o = o.transpose(0, 3, 1, 2, 4).reshape(b, s, h, dh)
    lse = lse.reshape(bd, h, Lp)[:, :, :L].reshape(b, dilation, h, L)
    lse = lse.transpose(0, 3, 1, 2).reshape(b, s, h)
    return o, lse

def dilated_attention_mixer(q, k, v, rel_bias):
    b, s = q.shape[:2]
    outs, lses = [], []
    for gi, (window, dilation) in enumerate(ATTN_GROUPS):
        hs = slice(gi * HEADS_PER_GROUP, (gi + 1) * HEADS_PER_GROUP)
        o, lse = dilated_group_attention(q[:, :, hs], k[:, :, hs], v[:, :, hs],
                                         rel_bias[:, hs], dilation, window // dilation)
        outs.append(o)
        lses.append(lse)
    o = jnp.stack(outs, axis=0)
    alpha = jax.nn.softmax(jnp.stack(lses, axis=0), axis=0)
    o = jnp.sum(alpha[..., None] * o, axis=0)
    return o.reshape(b, s, ATTN_OUT_WIDTH).astype(q.dtype)

def pool_mixer(u, w_grp, scale):
    b, s, _ = u.shape
    uf = u.astype(jnp.float32)
    cs = jnp.cumsum(uf, axis=1)
    pos = (jnp.arange(s) + 1)[None, :, None]
    outs = []
    for gi, w in enumerate(POOL_WINDOWS):
        sl = slice(gi * POOL_GROUP, (gi + 1) * POOL_GROUP)
        c = cs[..., sl]
        shifted = jnp.pad(c, ((0, 0), (w, 0), (0, 0)))[:, :s]
        cnt = jnp.minimum(pos, w).astype(jnp.float32)
        outs.append((c - shifted) / cnt - uf[..., sl])
    d = jnp.stack(outs, axis=2).astype(u.dtype)
    y = jnp.einsum("bsgc,gcd->bsgd", d, w_grp).reshape(b, s, POOL_WIDTH)
    return y * scale

def ssd_scan(x, dt, A, Bm, Cm):
    b, s, h, p = x.shape
    g, n = Bm.shape[2:]
    e = h // g
    l = SSD_CHUNK
    c = s // l
    xc = (x * dt[..., None]).reshape(b, c, l, g, e, p)
    a = (dt * A).reshape(b, c, l, h).transpose(0, 3, 1, 2)
    a_cs = jnp.cumsum(a, axis=-1)
    Bc = Bm.reshape(b, c, l, g, n)
    Cc = Cm.reshape(b, c, l, g, n)
    causal = jnp.tril(jnp.ones((l, l), dtype=bool))
    seg = a_cs[..., :, None] - a_cs[..., None, :]
    Lmat = jnp.exp(jnp.where(causal, seg, -jnp.inf)).reshape(b, g, e, c, l, l)
    cb = jnp.einsum("bclgn,bcsgn->bcgls", Cc, Bc)
    y_diag = jnp.einsum("bcgls,bgecls,bcsgep->bclgep", cb, Lmat, xc)
    decay = jnp.exp(a_cs[..., -1:] - a_cs).reshape(b, g, e, c, l)
    states = jnp.einsum("bclgn,bgecl,bclgep->bcgepn", Bc, decay, xc)
    chunk_decay = jnp.exp(a_cs[..., -1]).reshape(b, g, e, c)

    def step(carry, inp):
        st, dec = inp
        return carry * dec[..., None, None] + st, carry

    init = jnp.zeros((b, g, e, p, n), dtype=x.dtype)
    _, prev = lax.scan(step, init, (states.transpose(1, 0, 2, 3, 4, 5), chunk_decay.transpose(3, 0, 1, 2)))
    prev = prev.transpose(1, 0, 2, 3, 4, 5)
    out_decay = jnp.exp(a_cs).reshape(b, g, e, c, l)
    y_off = jnp.einsum("bclgn,bcgepn,bgecl->bclgep", Cc, prev, out_decay)
    return (y_diag + y_off).reshape(b, s, h, p)

def ssd_mixer(z, xbc, dt_raw, conv_w, conv_b, dt_bias, a_log, d_skip, norm_w):
    b, s, _ = z.shape
    xbc = jax.nn.silu(causal_dwconv(xbc, conv_w, conv_b))
    xs = xbc[..., :SSD_INNER].reshape(b, s, SSD_HEADS, SSD_HEAD_DIM).astype(jnp.float32)
    Bm = xbc[..., SSD_INNER:SSD_INNER + SSD_GROUPS * SSD_STATE].reshape(b, s, SSD_GROUPS, SSD_STATE).astype(jnp.float32)
    Cm = xbc[..., SSD_INNER + SSD_GROUPS * SSD_STATE:].reshape(b, s, SSD_GROUPS, SSD_STATE).astype(jnp.float32)
    dt = jax.nn.softplus(dt_raw.astype(jnp.float32) + dt_bias.astype(jnp.float32))
    A = -jnp.exp(a_log.astype(jnp.float32))
    y = ssd_scan(xs, dt, A, Bm, Cm) + d_skip.astype(jnp.float32)[:, None] * xs
    y = y.reshape(b, s, SSD_INNER) * jax.nn.silu(z.astype(jnp.float32))
    yg = y.reshape(b, s, SSD_GROUPS, SSD_INNER // SSD_GROUPS)
    yg = yg * lax.rsqrt(jnp.mean(yg * yg, axis=-1, keepdims=True) + NORM_EPS)
    y = yg.reshape(b, s, SSD_INNER) * norm_w.astype(jnp.float32)
    return y.astype(z.dtype)

def conv_ffn(u, w_up, conv_w, conv_b, w_down):
    h = causal_dwconv(u @ w_up, conv_w, conv_b)
    a, v = h[..., :D_FF], h[..., D_FF:]
    return (jax.nn.silu(a) * v) @ w_down

def second_inputs(seed: int = 0) -> dict:
    key = jax.random.key(seed)
    ks = jax.random.split(key, 24)
    f32 = jnp.float32

    def nrm(k, shape, scale):
        return jax.random.normal(k, shape, dtype=f32) * scale

    dt0 = jnp.exp(jax.random.uniform(ks[10], (DEPTH, SSD_HEADS), dtype=f32)
                  * (math.log(0.1) - math.log(0.001)) + math.log(0.001))
    return {
        "x": nrm(ks[0], (BATCH, SEQ, D_MODEL), 1.0),
        "rel_bias": nrm(ks[1], (REL_BUCKETS, ATTN_HEADS), 0.1),
        "ln1_g": 1.0 + nrm(ks[2], (DEPTH, D_MODEL), 0.02),
        "w_in": nrm(ks[3], (DEPTH, D_MODEL, IN_WIDTH), D_MODEL ** -0.5),
        "b_gate": nrm(ks[4], (DEPTH, N_BRANCH_2 * D_MODEL), 0.02),
        "w_a": nrm(ks[5], (DEPTH, ATTN_OUT_WIDTH, D_MODEL), ATTN_OUT_WIDTH ** -0.5),
        "pool_w": nrm(ks[6], (DEPTH, len(POOL_WINDOWS), POOL_GROUP, POOL_GROUP), POOL_GROUP ** -0.5),
        "pool_scale": 1.0 + nrm(ks[7], (DEPTH, POOL_WIDTH), 0.1),
        "w_b": nrm(ks[8], (DEPTH, POOL_WIDTH, D_MODEL), POOL_WIDTH ** -0.5),
        "ssd_conv_w": nrm(ks[9], (DEPTH, SSD_CONV, SSD_XBC), SSD_CONV ** -0.5),
        "ssd_conv_b": nrm(ks[11], (DEPTH, SSD_XBC), 0.02),
        "ssd_dt_bias": dt0 + jnp.log(-jnp.expm1(-dt0)),
        "ssd_a_log": jnp.log(jax.random.uniform(ks[12], (DEPTH, SSD_HEADS), dtype=f32, minval=1.0, maxval=16.0)),
        "ssd_d": 1.0 + nrm(ks[13], (DEPTH, SSD_HEADS), 0.1),
        "ssd_norm_w": 1.0 + nrm(ks[14], (DEPTH, SSD_INNER), 0.02),
        "w_c": nrm(ks[15], (DEPTH, SSD_INNER, D_MODEL), SSD_INNER ** -0.5),
        "w_o": nrm(ks[16], (DEPTH, D_MODEL, D_MODEL), D_MODEL ** -0.5),
        "ln2_g": 1.0 + nrm(ks[17], (DEPTH, D_MODEL), 0.02),
        "ffn_w_up": nrm(ks[18], (DEPTH, D_MODEL, 2 * D_FF), D_MODEL ** -0.5),
        "ffn_conv_w": nrm(ks[19], (DEPTH, FFN_CONV, 2 * D_FF), FFN_CONV ** -0.5),
        "ffn_conv_b": nrm(ks[20], (DEPTH, 2 * D_FF), 0.02),
        "ffn_w_down": nrm(ks[21], (DEPTH, D_FF, D_MODEL), D_FF ** -0.5),
        "final_g": 1.0 + nrm(ks[22], (D_MODEL,), 0.02),
    }

def second_block(x, rel_bias, ln1_g, w_in, b_gate, w_a, pool_w, pool_scale, w_b,
              ssd_conv_w, ssd_conv_b, ssd_dt_bias, ssd_a_log, ssd_d, ssd_norm_w, w_c,
              w_o, ln2_g, ffn_w_up, ffn_conv_w, ffn_conv_b, ffn_w_down, final_g):
    b, s, _ = x.shape
    split_idx = []
    acc = 0
    for sz in IN_SPLIT_SIZES[:-1]:
        acc += sz
        split_idx.append(acc)
    for i in range(DEPTH):
        u = rmsnorm_2(x, ln1_g[i])
        proj = u @ w_in[i]
        q, k, v, pool_in, z, xbc, dt_raw, gate_pre = jnp.split(proj, split_idx, axis=-1)
        q = q.reshape(b, s, ATTN_HEADS, HEAD_DIM)
        k = k.reshape(b, s, ATTN_HEADS, HEAD_DIM)
        v = v.reshape(b, s, ATTN_HEADS, HEAD_DIM)
        y_a = dilated_attention_mixer(q, k, v, rel_bias) @ w_a[i]
        y_b = pool_mixer(pool_in, pool_w[i], pool_scale[i]) @ w_b[i]
        y_c = ssd_mixer(z, xbc, dt_raw, ssd_conv_w[i], ssd_conv_b[i], ssd_dt_bias[i],
                        ssd_a_log[i], ssd_d[i], ssd_norm_w[i]) @ w_c[i]
        gates = jax.nn.sigmoid(gate_pre + b_gate[i]).reshape(b, s, N_BRANCH_2, D_MODEL)
        merged = gates[:, :, 0] * y_a + gates[:, :, 1] * y_b + gates[:, :, 2] * y_c
        x = x + merged @ w_o[i]
        x = x + conv_ffn(rmsnorm_2(x, ln2_g[i]), ffn_w_up[i], ffn_conv_w[i], ffn_conv_b[i], ffn_w_down[i])
    return rmsnorm_2(x, final_g)


def setup_inputs(seed=0):
    out = dict(first_inputs(seed))
    for name, value in second_inputs(seed + 1).items():
        if name != "x":
            out[name + "_2"] = value
    return out


def reference(
    x, c, w_ada, b_ada, g_norm1, w_in, w_dw, b_dw, g_conv_ln, b_conv_ln, w_conv_pw, b_conv_pw,
    w_a2, b_a2, g_gla_norm, w_gla_o, w_out, g_norm2, w_router_g, b_router_g, w_router_e,
    b_router_e, w1, w3, w2, w_ada_f, b_ada_f, g_final, rel_bias_2, ln1_g_2, w_in_2, b_gate_2,
    w_a_2, pool_w_2, pool_scale_2, w_b_2, ssd_conv_w_2, ssd_conv_b_2, ssd_dt_bias_2,
    ssd_a_log_2, ssd_d_2, ssd_norm_w_2, w_c_2, w_o_2, ln2_g_2, ffn_w_up_2, ffn_conv_w_2,
    ffn_conv_b_2, ffn_w_down_2, final_g_2,
):
    x = first_block(
        x, c, w_ada, b_ada, g_norm1, w_in, w_dw, b_dw, g_conv_ln, b_conv_ln, w_conv_pw,
        b_conv_pw, w_a2, b_a2, g_gla_norm, w_gla_o, w_out, g_norm2, w_router_g, b_router_g,
        w_router_e, b_router_e, w1, w3, w2, w_ada_f, b_ada_f, g_final,
    )
    return second_block(
        x, rel_bias_2, ln1_g_2, w_in_2, b_gate_2, w_a_2, pool_w_2, pool_scale_2, w_b_2,
        ssd_conv_w_2, ssd_conv_b_2, ssd_dt_bias_2, ssd_a_log_2, ssd_d_2, ssd_norm_w_2, w_c_2,
        w_o_2, ln2_g_2, ffn_w_up_2, ffn_conv_w_2, ffn_conv_b_2, ffn_w_down_2, final_g_2,
    )


_drawn_inputs = setup_inputs


def setup_inputs(seed=0):
    import zlib

    import numpy as np

    out = dict(_drawn_inputs(seed))
    spreads = {}
    factors = {'g_norm1': 3.339,
     'b_dw': 8.0,
     'g_conv_ln': 6.402,
     'b_conv_ln': 8.0,
     'b_conv_pw': 8.0,
     'b_a2': 8.0,
     'g_gla_norm': 6.684,
     'g_norm2': 2.878,
     'b_router_g': 8.0,
     'b_router_e': 8.0,
     'rel_bias_2': 7.733,
     'ln1_g_2': 3.582,
     'b_gate_2': 8.0,
     'ssd_conv_b_2': 4.74,
     'ssd_norm_w_2': 6.52,
     'ln2_g_2': 4.694,
     'ffn_conv_b_2': 4.837,
     'final_g_2': 25.873,
     'ssd_d_2': 49.206}
    for name, (base, spread) in spreads.items():
        noise = np.random.default_rng([zlib.crc32(name.encode()), seed]).standard_normal(out[name].shape)
        drawn = base * np.exp(spread * noise) if base else spread * noise
        out[name] = __import__('jax').numpy.asarray(drawn.astype(out[name].dtype))
    for name, factor in factors.items():
        out[name] = (out[name] * factor).astype(out[name].dtype)
    return out
```

```python
from contextlib import ExitStack

import concourse.bass as bass
from concourse import mybir
import numpy as np

F32 = mybir.dt.float32
U32 = mybir.dt.uint32
ALU = mybir.AluOpType
ACT = mybir.ActivationFunctionType
AX = mybir.AxisListType.X

P = 128
S = 256
D = 1024
KT = D // P
NE = 32
NS = 4
SLOT = 4096
LEVELS = (32, 16, 8, 4, 2, 1)
WINDOWS = (2, 4, 8, 16)

IN1 = dict(a=0, gt=512, q=1024, k=1536, v=2048, r=3072, a1=4096, gates=4112)
IN2 = dict(q=0, k=1152, v=2304, pool=3456, z=4480, xbc=5504, dt=7040, gates=7056)

COLS = [("g_norm1", 8), ("g_norm2", 8), ("g_final", 8), ("c", 8), ("b_ada", 48), ("b_ada_f", 16),
        ("w_dw", 124), ("b_dw", 4), ("g_conv_ln", 4), ("b_conv_ln", 4), ("b_conv_pw", 8), ("g_gla_norm", 8),
        ("ln1_g_2", 8), ("b_gate_2", 24), ("pool_scale_2", 8), ("ssd_conv_w_2", 48), ("ssd_conv_b_2", 12),
        ("ssd_d_2", 8), ("ssd_norm_w_2", 8), ("ln2_g_2", 8), ("ffn_conv_w_2", 132), ("ffn_conv_b_2", 44),
        ("final_g_2", 8), ("router_b", 36), ("dt_bias", 16), ("a_log", 16), ("eps", 1)]
CONSTS = [("ident", 128), ("ones", 128), ("u64", 128), ("u128", 128), ("masks", 7 * 128), ("invcnt", 4 * 256),
          ("oh", 3 * 384), ("iota8", 8)]


def spans(table):
    at, out = 0, {}
    for name, n in table:
        out[name] = (at, n)
        at += n
    return out, at


COL_AT, NCOLS = spans(COLS)
CONST_AT, NCONST = spans(CONSTS)


def constants():
    c = np.zeros((P, NCONST), np.float32)

    def put(name, v):
        at, n = CONST_AT[name]
        c[:v.shape[0], at:at + n] = v

    i = np.arange(P)
    put("ident", np.eye(P))
    put("ones", np.ones((P, P)))
    le = i[:, None] <= i[None, :]
    same = i[:, None] // 64 == i[None, :] // 64
    put("u64", (le & same) / 16.0)
    put("u128", le * 1.0)
    ms = []
    for m in LEVELS:
        blk = i[:, None] // (2 * m) == i[None, :] // (2 * m)
        ms.append(blk & (i[:, None] % (2 * m) < m) & (i[None, :] % (2 * m) >= m))
    ms.append(i[:, None] == i[None, :])
    put("masks", np.concatenate(ms, 1) * 1.0)
    t = np.arange(S) + 1
    put("invcnt", np.broadcast_to(np.concatenate([1.0 / np.minimum(t, w) for w in WINDOWS]), (P, 4 * S)))
    dist = 255 - np.arange(384)
    nf = np.maximum(dist, 1).astype(np.float32)
    large = 16 + (np.log(nf / np.float32(16)) / np.float32(np.log(2048 / 16)) * np.float32(16)).astype(np.int32)
    bucket = np.where(dist < 16, np.maximum(dist, 0), np.minimum(large, 31))
    oh = np.zeros((33, 3, 384))
    for g, (w, dil) in enumerate(((128, 1), (512, 4), (2048, 16))):
        ok = (dist >= 0) & (dist <= w) & (dist % dil == 0)
        oh[bucket[ok], g, np.arange(384)[ok]] = 1.0
        oh[32, g, ~ok] = -1e30
    put("oh", oh.reshape(33, -1))
    put("iota8", np.broadcast_to(np.arange(8), (P, 8)))
    return c


class Tok:
    def __init__(self, eng, at):
        self.eng, self.at, self.used = eng, at, False


class Landed:
    def __init__(self, sem, value):
        self.sem, self.value = sem, value


def build(nc, T, out, scratch, dbg=None):
    ctx = ExitStack()
    engines = ("tensor", "vector", "scalar", "gpsimd", "sync")
    queue = {e: [] for e in engines}

    def flat(ws):
        for w in ws:
            if isinstance(w, (list, tuple)):
                yield from flat(w)
            elif w is not None:
                yield w

    def op(eng, fn, *waits, sem=None):
        tok = Tok(eng, len(queue[eng]))
        queue[eng].append((fn, list(flat(waits)), tok, sem))
        return tok

    with ctx:
        sem_n = [0]

        def new_sem(name):
            sem_n[0] += 1
            return ctx.enter_context(nc.semaphore(f"{name}{sem_n[0]}"))

        ARENA = 53000
        arena = ctx.enter_context(nc.sbuf_tensor("arena", [P, ARENA], F32))
        banks = [ctx.enter_context(nc.psum_tensor(f"bank{i}", [P, 512], F32)) for i in range(8)]
        idxb = ctx.enter_context(nc.sbuf_tensor("idxb", [P, 16], U32))
        done = {e: new_sem("done_" + e) for e in engines}

        top = [0]

        def buf(n, shape=None, at=None):
            if at is None:
                at = top[0]
                top[0] += n
            assert at + n <= ARENA, (at, n)
            v = arena[:, at:at + n]
            if shape is not None:
                names = "abcd"[:len(shape)]
                v = v.rearrange(f"p ({' '.join(names)}) -> p {' '.join(names)}", **dict(zip(names, shape)))
            return v

        def view(ap, *shape):
            names = "abcd"[:len(shape)]
            return ap.rearrange(f"p ({' '.join(names)}) -> p {' '.join(names)}", **dict(zip(names, shape)))

        def mm(o, l, r, start, stop, *w, skip=False):
            return op("tensor", lambda e: e.matmul(o, l, r, start=start, stop=stop, skip_group_check=skip), *w)

        def tp(o, i, idn, *w):
            return op("tensor", lambda e: e.transpose(o, i, idn), *w)

        def act(o, i, f, *w, bias=0.0, scale=1.0, accum=None):
            if accum is not None:
                return op("scalar", lambda e: e.activation(o, i, f, bias=bias, scale=scale, accum_out=accum), *w)
            return op("scalar", lambda e: e.activation(o, i, f, bias=bias, scale=scale), *w)

        def tt(o, a, b, f, *w, eng="vector"):
            return op(eng, lambda e: e.tensor_tensor(o, a, b, f), *w)

        def ts(o, a, s1, f1, s2, f2, *w, eng="vector"):
            if f2 is None:
                return op(eng, lambda e: e.tensor_scalar(o, a, s1, None, f1), *w)
            return op(eng, lambda e: e.tensor_scalar(o, a, s1, s2, f1, f2), *w)

        def stt(o, a, s, b, f1, f2, *w):
            return op("vector", lambda e: e.scalar_tensor_tensor(out=o, in0=a, scalar=s, in1=b, op0=f1, op1=f2), *w)

        def copy(o, i, *w, eng="vector"):
            return op(eng, lambda e: e.tensor_copy(o, i), *w)

        def recip(o, i, *w):
            return op("vector", lambda e: e.reciprocal(o, i), *w)

        def fill(o, v, *w, eng="gpsimd"):
            return op(eng, lambda e: e.memset(o, v), *w)

        def dma(o, i, *w):
            s = new_sem("d")
            op("sync", lambda e: e.dma_start(o, i), *w, sem=s)
            return Landed(s, 16)

        ring = [buf(SLOT) for _ in range(NS)]
        ring_sem = [new_sem("ring") for _ in range(NS)]
        ring_free = [None] * NS
        ring_n = [0]

        def load(src, kt, n):
            s = ring_n[0] % NS
            ring_n[0] += 1
            dst = view(ring[s][:, 0:kt * n], kt, n)
            op("sync", lambda e: e.dma_start(dst, src), ring_free[s], sem=ring_sem[s])
            return dst, Landed(ring_sem[s], 16 * ((ring_n[0] - 1) // NS + 1)), s

        def wcols(w, c0, n):
            return load(w[:, c0:c0 + n].rearrange("(t p) n -> p t n", p=P), w.shape[0] // P, n)

        def wrows(w, t0, t1):
            return load(w[t0 * P:t1 * P, :].rearrange("(t p) n -> p t n", p=P), t1 - t0, w.shape[1])

        bank_free = [None] * 8
        bank_set = [list(range(8))]
        bank_n = [0]

        def take():
            b = bank_set[0][bank_n[0] % len(bank_set[0])]
            bank_n[0] += 1
            return b, banks[b], bank_free[b]

        cols = buf(NCOLS)
        consts = buf(NCONST)
        t_cols = dma(cols, T["cols"])
        xbase = top[0]
        xT = buf(2048, (2, 1024))
        t_x = dma(xT, T["x"].rearrange("o (t p) d -> p (o t) d", p=P))
        t_consts = dma(consts, T["consts"])

        def col(name, i=0, n=1):
            at = COL_AT[name][0] + i
            return cols[:, at:at + n]

        def const(name):
            at, n = CONST_AT[name]
            return consts[:, at:at + n]

        ident, ones, u64, u128 = (const(n) for n in ("ident", "ones", "u64", "u128"))
        masks = view(const("masks"), 7, 128)
        invcnt = view(const("invcnt"), 4, 256)
        oh = view(const("oh"), 3, 384)
        iota8 = const("iota8")
        eps = col("eps")

        rtab = buf(18)
        t_rtab1 = dma(rtab[0:32, :], T["rel_bias_2"])
        one_row = CONST_AT["ones"][0]
        t_rtab2 = dma(rtab[32:33, :], T["consts"][0:1, one_row:one_row + 18])
        wa2 = buf(512)
        t_wa2 = dma(wa2[0:16, :], T["w_a2"][0])
        t_ba2 = dma(wa2[16:17, :], T["b_a2"])
        wr = buf(8 * 36, (8, 36))
        t_wr1 = dma(wr[:, :, 0:4], T["w_router_g"][0].rearrange("(t p) n -> p t n", p=P))
        t_wr2 = dma(wr[:, :, 4:36], T["w_router_e"][0].rearrange("(t p) n -> p t n", p=P))
        wa1 = buf(128, (8, 16))
        t_wa1 = dma(wa1, T["w_in"][0][:, IN1["a1"]:IN1["a1"] + 16].rearrange("(t p) n -> p t n", p=P))
        wdt = buf(128, (8, 16))
        t_wdt = dma(wdt, T["w_in_2"][0][:, IN2["dt"]:IN2["dt"] + 16].rearrange("(t p) n -> p t n", p=P))

        h = buf(2048, (8, 256))
        u = buf(2048, (8, 256))
        mod = buf(64)
        am = buf(24)
        cact = buf(8)
        rstd = buf(256)
        base = top[0]

        def project(wget, kts, rhs, m_list, evac, *deps):
            last = None
            for j0 in range(0, len(m_list), 2):
                pair = m_list[j0:j0 + 2]
                b, bank, free = take()
                for j, m in enumerate(pair):
                    for k in range(kts):
                        w, wt = wget(m, k)
                        last = mm(bank[:, j * 256:j * 256 + 256], w, rhs(k), k == 0, k == kts - 1, free, wt, deps)
                bank_free[b] = [evac(m, bank[:, j * 256:j * 256 + 256], last) for j, m in enumerate(pair)]
            return last

        def project_cols(w, c0, n, rhs, evac, *deps, chunk=512):
            m0 = 0
            for c in range(0, n, chunk):
                k = min(chunk, n - c)
                slot, landed, s = wcols(w, c0 + c, k)
                last = project(lambda m, kt, slot=slot, m0=m0: (slot[:, kt, (m - m0) * P:(m - m0) * P + P], landed),
                               w.shape[0] // P, rhs, list(range(m0, m0 + k // P)), evac, *deps)
                ring_free[s] = last
                m0 += k // P

        t_h = []
        for tc in range(2):
            for g in range(2):
                b, bank, free = take()
                for j in range(4):
                    last = tp(bank[:, j * P:j * P + P], xT[:, tc, (4 * g + j) * P:(4 * g + j + 1) * P], ident,
                              free, t_x, t_consts)
                t = copy(h[:, 4 * g:4 * g + 4, tc * P:tc * P + P], view(bank[:, :], 4, P), last)
                bank_free[b] = t
                t_h.append(t)

        t_cact = act(cact, col("c", 0, 8), ACT.Silu, t_cols)
        mod_bank = 7
        bank_set[0] = list(range(7))

        def ada(w, c0, n, m0):
            for c in range(0, n, 512):
                slot, landed, s = wcols(w, c0 + c, 512)
                for m in range(4):
                    at = m0 + c // P + m
                    for k in range(KT):
                        last = mm(banks[mod_bank][:, at:at + 1], slot[:, k, m * P:m * P + P], cact[:, k:k + 1],
                                  k == 0, k == KT - 1, landed, t_cact, bank_free[mod_bank])
                ring_free[s] = last
            return last

        def ada_out(m0, n, bias, last):
            t = tt(mod[:, m0:m0 + n], banks[mod_bank][:, m0:m0 + n], bias, ALU.add, last, t_cols)
            bank_free[mod_bank] = t
            return t

        w_ada = T["w_ada"][0]
        t_mod = ada_out(0, 16, col("b_ada", 0, 16), ada(w_ada, 0, 2048, 0))

        def gain(i, g, sc, t):
            return stt(am[:, 8 * i:8 * i + 8], mod[:, sc:sc + 8], 1.0, col(g, 0, 8), ALU.add, ALU.mult, t)

        t_am = gain(0, "g_norm1", 8, t_mod)

        def norm(x, t_x, t_sq_free, sq, scale_col, shift_col, o, t_o_free, *t_ab):
            t_sq = [act(sq[:, 0:4, :], x[:, 0:4, :], ACT.Square, t_x, t_sq_free),
                    tt(sq[:, 4:8, :], x[:, 4:8, :], x[:, 4:8, :], ALU.mult, t_x, t_sq_free)]
            b, bank, free = take()
            for k in range(KT):
                last = mm(bank[:, 0:256], ones, sq[:, k, :], k == 0, k == KT - 1, free, t_sq[k // 4], t_consts)
            t = act(rstd, bank[:, 0:256], ACT.Sqrt, last, bias=eps, scale=1.0 / D)
            bank_free[b] = t
            t_r = recip(rstd, rstd, t)
            toks = []
            for g in range(2):
                t = tt(sq[:, 4 * g:4 * g + 4, :], x[:, 4 * g:4 * g + 4, :],
                       rstd.rearrange("p (o n) -> p o n", o=1).to_broadcast([P, 4, 256]), ALU.mult, t_r, last)
                for k in range(4 * g, 4 * g + 4):
                    if shift_col is None:
                        if k % 2:
                            toks.append(act(o[:, k, :], sq[:, k, :], ACT.Identity, t, t_ab, t_o_free, scale=scale_col(k)))
                        else:
                            toks.append(ts(o[:, k, :], sq[:, k, :], scale_col(k), ALU.mult, None, None, t, t_ab, t_o_free))
                    elif k % 2:
                        toks.append(act(o[:, k, :], sq[:, k, :], ACT.Identity, t, t_ab, t_o_free,
                                        scale=scale_col(k), bias=shift_col(k)))
                    else:
                        toks.append(ts(o[:, k, :], sq[:, k, :], scale_col(k), ALU.mult, shift_col(k), ALU.add,
                                       t, t_ab, t_o_free))
            return toks

        rhs_u = lambda k: u[:, k, :]

        scr = buf(5120)
        sq = view(scr[:, 0:2048], 8, 256)
        zp = buf(4 * 286, (4, 286))
        cacc = buf(1024, (4, 256))
        sig = buf(1024, (4, 256))
        q = buf(1024, (4, 256))
        kk = buf(1024, (4, 256))
        v = buf(2048, (2, 1024))
        rbase = top[0]
        r = buf(2048, (8, 256))
        gates = buf(4096, (16, 256))
        bcs = buf(1024, (4, 256))
        attn = buf(1024, (2, 4, 128), at=xbase)
        tmpm = buf(512)
        qb = buf(1024, (4, 256), at=xbase + 1024)
        kdT = buf(1024, (2, 4, 128))
        St = buf(3072, (3, 4, 256))
        a1 = buf(256)
        small = buf(64)

        rep = buf(18 * 384, (18, 384), at=rbase)
        t_rep = []
        for i in range(18):
            b, bank, free = take()
            last = mm(bank[:, 0:384], rtab[0:33, i:i + 1].to_broadcast([33, P]), oh[0:33, i // 6, :], True, True,
                      free, t_rtab1, t_rtab2, t_consts)
            t = copy(rep[:, i, :], bank[:, 0:384], last)
            bank_free[b] = t
            t_rep.append(t)
        t_rep_out = dma(scratch.rearrange("(p n) -> p n", n=18 * 384), rep.rearrange("p a b -> p (a b)"), t_rep)

        t_u = norm(h, t_h, None, sq, lambda k: am[:, k:k + 1], lambda k: mod[:, k:k + 1], u, None, t_am, t_mod)

        w_in = T["w_in"][0]
        t_a1one = fill(a1[0:17, :], 1.0)
        t_zpad = fill(zp[:, :, 0:30], 0.0)

        t_sig = {}
        project_cols(w_in, IN1["gt"], 512, rhs_u,
                     lambda m, ps, t: t_sig.setdefault(m, act(sig[:, m, :], ps, ACT.Sigmoid, t)), t_u)
        t_z = {}
        project_cols(w_in, IN1["a"], 512, rhs_u,
                     lambda m, ps, t: t_z.setdefault(m, tt(zp[:, m, 30:286], ps, sig[:, m, :], ALU.mult, t, t_sig[m])), t_u)

        b, bank, free = take()
        for k in range(KT):
            last = mm(bank[0:16, 0:256], wa1[:, k, :], u[:, k, :], k == 0, k == KT - 1, free, t_wa1, t_u)
        t_a1 = copy(a1[0:16, :], bank[0:16, 0:256], last, t_a1one)
        bank_free[b] = t_a1
        lgT = view(scr[:, 2048:3072], 2, 512)
        lx = view(scr[:, 3072:4096], 2, 512)
        t_lg = []
        for tc in range(2):
            b, bank, free = take()
            last = mm(bank[:, :], a1[0:17, tc * P:tc * P + P], wa2[0:17, :], True, True, free, t_a1, t_wa2, t_ba2)
            t = act(lx[:, tc, :], bank[:, :], ACT.Abs, last)
            t = act(lx[:, tc, :], lx[:, tc, :], ACT.Exp, t, scale=-1.0)
            t = act(lx[:, tc, :], lx[:, tc, :], ACT.Ln, t, bias=1.0)
            t = stt(lgT[:, tc, :], bank[:, :], 0.0, lx[:, tc, :], ALU.min, ALU.subtract, t)
            bank_free[b] = t
            t_lg.append(t)
        t_b = []
        for hh in range(4):
            b, bank, free = take()
            for tc in range(2):
                last = mm(bank[:, tc * P:tc * P + P], lgT[:, tc, hh * P:hh * P + P], u64, True, True, free, t_lg[tc])
            t = copy(bcs[:, hh, :], bank[:, 0:256], last, t_rep_out)
            bank_free[b] = t
            t_b.append(t)

        t_q, t_k = {}, {}
        project_cols(w_in, IN1["q"], 512, rhs_u,
                     lambda m, ps, t: t_q.setdefault(m, act(q[:, m, :], ps, ACT.Copy, t, scale=128.0 ** -0.5)), t_u)
        project_cols(w_in, IN1["k"], 512, rhs_u,
                     lambda m, ps, t: t_k.setdefault(m, act(kk[:, m, :], ps, ACT.Copy, t)), t_u)
        t_q, t_k = list(t_q.values()), list(t_k.values())

        t_v = []
        for c in range(2):
            slot, landed, s = wcols(w_in, IN1["v"] + 512 * c, 512)
            for tc in range(2):
                b, bank, free = take()
                for k in range(KT):
                    last = mm(bank[:, :], u[:, k, tc * P:tc * P + P], slot[:, k, :], k == 0, k == KT - 1, free, landed, t_u)
                t = act(v[:, tc, c * 512:c * 512 + 512], bank[:, :], ACT.Copy, last)
                bank_free[b] = t
                t_v.append(t)
            ring_free[s] = last

        tl = []
        for m in range(4):
            tl.append(ts(cacc[:, m, :], zp[:, m, 0:256], col("w_dw", m * 31), ALU.mult, col("b_dw", m), ALU.add,
                         t_z[m], t_zpad, t_cols))
        for j in range(1, 31):
            for m in range(4):
                tl[m] = stt(cacc[:, m, :], zp[:, m, j:j + 256], col("w_dw", m * 31 + j), cacc[:, m, :],
                            ALU.mult, ALU.add, tl[m])
        t_conv = tl

        dq, e1, e2, qe, ke = (scr[:, 1024 * i:1024 * i + 1024] for i in range(5))
        qf, kf, bf = (x.rearrange("p a b -> p (a b)") for x in (q, kk, bcs))
        t_attn = [None, None]
        t_free = [t_b]
        for li in range(7):
            if li < 6:
                m = LEVELS[li]
                n = 1024 // (2 * m)
                b3 = view(bf, n, 2 * m)
                t = tt(view(dq, n, 2 * m), b3, b3[:, :, m - 1:m].to_broadcast([P, n, 2 * m]), ALU.subtract, t_b, t_free)
                ta = ts(e1, dq, 0.0, ALU.min, None, None, t, t_free)
                tb = ts(e2, dq, 0.0, ALU.max, None, None, t, t_free)
                ta = act(e1, e1, ACT.Exp, ta)
                tb = act(e2, e2, ACT.Exp, tb, scale=-1.0)
                ta = tt(qe, qf, e1, ALU.mult, ta, t_q, t_free)
                tb = tt(ke, kf, e2, ALU.mult, tb, t_k, t_free, eng="gpsimd")
                qs, ks = view(qe, 4, 256), view(ke, 4, 256)
                t_in = [ta, tb]
            else:
                qs, ks, t_in = q, kk, [t_q, t_k]
            t_free = []
            for tc in range(2):
                b, bank, free = take()
                for hh in range(4):
                    last = mm(bank[:, hh * P:hh * P + P], ks[:, hh, tc * P:tc * P + P], qs[:, hh, tc * P:tc * P + P],
                              True, True, free, t_in)
                t_free.append(last)
                mk = masks[:, li:li + 1, :].to_broadcast([P, 4, P])
                if li == 0:
                    t = tt(attn[:, tc, :, :], view(bank[:, :], 4, P), mk, ALU.mult, last, t_consts)
                    bank_free[b] = t
                else:
                    t = tt(view(tmpm, 4, P), view(bank[:, :], 4, P), mk, ALU.mult, last, t_attn)
                    bank_free[b] = t
                    t = tt(attn[:, tc, :, :], attn[:, tc, :, :], view(tmpm, 4, P), ALU.add, t)
                t_attn[tc] = t
        t_lev = t_free

        t = act(e1, bf, ACT.Exp, t_b, t_lev)
        t_qb = tt(qb.rearrange("p a b -> p (a b)"), qf, e1, ALU.mult, t, t_q)
        b3 = view(bf, 16, 64)
        t = tt(view(dq, 16, 64), b3, b3[:, :, 63:64].to_broadcast([P, 16, 64]), ALU.subtract, t_b, t_lev)
        t = act(e2, dq, ACT.Exp, t, scale=-1.0)
        t_kd = tt(ke, kf, e2, ALU.mult, t, t_k, t_lev)
        dec = small[:, 0:16]
        t_dec = act(dec, b3[:, :, 63], ACT.Exp, t_b)
        dec3 = view(dec, 4, 4)
        ke3 = view(ke, 4, 256)
        t_kdT = []
        for tc in range(2):
            b, bank, free = take()
            for hh in range(4):
                last = tp(bank[:, hh * P:hh * P + P], ke3[:, hh, tc * P:tc * P + P], ident, free, t_kd)
            t = act(kdT[:, tc, :, :], view(bank[:, :], 4, P), ACT.Copy, last)
            bank_free[b] = t
            t_kdT.append(t)
        t_S = []
        for c in range(3):
            tc, s0 = c // 2, 64 * (c % 2)
            row = []
            for g in range(2):
                b, bank, free = take()
                for j in range(2):
                    hh = 2 * g + j
                    last = mm(bank[:, j * 256:j * 256 + 256], kdT[s0:s0 + 64, tc, hh, :],
                              v[s0:s0 + 64, tc, hh * 256:hh * 256 + 256], True, True, free, t_kdT[tc], t_v)
                for j in range(2):
                    hh = 2 * g + j
                    ps = bank[:, j * 256:j * 256 + 256]
                    if c == 0:
                        t = copy(St[:, c, hh, :], ps, last)
                    else:
                        t = stt(St[:, c, hh, :], St[:, c - 1, hh, :], dec3[:, hh, c:c + 1], ps, ALU.mult, ALU.add,
                                last, t_dec, t_S[c - 1][hh])
                    row.append(t)
                bank_free[b] = t
            t_S.append(row)

        ss = small[:, 16:24]
        rs = small[:, 24:32]
        on = view(scr[:, 1024:3072], 2, 1024)
        junk = tmpm
        t_on = []
        obanks = []
        t_ss = None
        for tc in range(2):
            for g in range(2):
                b, bank, free = take()
                for j in range(2):
                    hh = 2 * g + j
                    last = mm(bank[:, j * 256:j * 256 + 256], attn[:, tc, hh, :], v[:, tc, hh * 256:hh * 256 + 256],
                              True, False, free, t_attn[tc], t_v, skip=True)
                    for s in range(2):
                        c = 2 * tc + s
                        if c:
                            last = mm(bank[64 * s:64 * s + 64, j * 256:j * 256 + 256], qb[:, hh, c * 64:c * 64 + 64],
                                      St[:, c - 1, hh, :], False, True, t_qb, t_S[c - 1][hh], skip=True)
                for j in range(2):
                    i = tc * 4 + 2 * g + j
                    t = t_ss = act(junk[:, 0:256], bank[:, j * 256:j * 256 + 256], ACT.Square, last, t_ss, t_attn,
                            accum=ss[:, i:i + 1])
                obanks.append((b, bank, tc, g, t))
        t = act(rs, ss, ACT.Sqrt, t, bias=eps, scale=1.0 / 256)
        t_rs = recip(rs, rs, t)
        for b, bank, tc, g, t0 in obanks:
            for j in range(2):
                hh = 2 * g + j
                t = ts(on[:, tc, hh * 256:hh * 256 + 256], bank[:, j * 256:j * 256 + 256],
                       rs[:, tc * 4 + hh:tc * 4 + hh + 1], ALU.mult, None, None, t_rs, t_lev, t_kdT, t_qb)
            bank_free[b] = t
            t_on.append(t)

        t_r = {}

        def silu_r(m, ps, t):
            t_r[m] = act(r[:, m, :], ps, ACT.Silu, t, t_rep_out)
            return t_r[m]
        project_cols(w_in, IN1["r"], 1024, rhs_u, silu_r, t_u)
        t_og = []
        for tc in range(2):
            for g in range(2):
                b, bank, free = take()
                for j in range(4):
                    m = 4 * g + j
                    last = tp(bank[:, j * P:j * P + P], on[:, tc, m * P:m * P + P], ident, free, t_on)
                for j in range(4):
                    m = 4 * g + j
                    t = stt(r[:, m, tc * P:tc * P + P], bank[:, j * P:j * P + P], col("g_gla_norm", m),
                            r[:, m, tc * P:tc * P + P], ALU.mult, ALU.mult, last, t_r[m])
                bank_free[b] = t
                t_og.append(t)
        t_g = {}

        def gate(m, ps, t):
            t_g[m] = act(gates[:, m, :], ps, ACT.Sigmoid, t, t_rep_out)
            return t_g[m]
        project_cols(w_in, IN1["gates"], 2048, rhs_u, gate, t_u)

        b, bank, free = take()
        for m in range(4):
            last = mm(bank[:, 0:256], ones, cacc[:, m, :], m == 0, m == 3, free, t_conv[m])
        mu = scr[:, 4096:4352]
        t = ts(mu, bank[:, 0:256], 1.0 / 512, ALU.mult, None, None, last, t_kdT)
        bank_free[b] = t
        t_c = tt(cacc, cacc, mu.rearrange("p (o n) -> p o n", o=1).to_broadcast([P, 4, 256]), ALU.subtract, t, last)
        t_s2 = act(sig, cacc, ACT.Square, t_c, list(t_z.values()))
        b, bank, free = take()
        for m in range(4):
            last = mm(bank[:, 0:256], ones, sig[:, m, :], m == 0, m == 3, free, t_s2)
        t = act(mu, bank[:, 0:256], ACT.Sqrt, last, t_c, bias=eps, scale=1.0 / 512)
        bank_free[b] = t
        t = recip(mu, mu, t)
        t = tt(cacc, cacc, mu.rearrange("p (o n) -> p o n", o=1).to_broadcast([P, 4, 256]), ALU.mult, t, t_s2)
        t_cs = [act(sig[:, m, :], cacc[:, m, :], ACT.Silu, t, last, scale=col("g_conv_ln", m), bias=col("b_conv_ln", m))
                for m in range(4)]

        t_mg = {}

        def y_conv(m, ps, t):
            t_mg[m] = stt(gates[:, m, :], ps, col("b_conv_pw", m), gates[:, m, :], ALU.add, ALU.mult, t, t_g[m])
            return t_mg[m]
        for c in range(2):
            slot, landed, s = wcols(T["w_conv_pw"][0], 512 * c, 512)
            ring_free[s] = project(lambda m, k: (slot[:, k, (m - 4 * c) * P:(m - 4 * c) * P + P], landed), 4,
                                   lambda k: sig[:, k, :], list(range(4 * c, 4 * c + 4)), y_conv, t_cs)

        def y_gla(m, ps, t):
            t1 = tt(gates[:, 8 + m, :], ps, gates[:, 8 + m, :], ALU.mult, t, t_g[8 + m])
            t_mg[m] = tt(gates[:, m, :], gates[:, m, :], gates[:, 8 + m, :], ALU.add, t1, t_mg[m])
            return t1
        project_cols(T["w_gla_o"][0], 0, 1024, lambda k: r[:, k, :], y_gla, t_og)

        t_mod = ada_out(16, 8, col("b_ada", 16, 8), ada(w_ada, 2048, 1024, 16))

        t_h1 = {}

        def add_h(m, ps, t):
            t_h1[m] = stt(h[:, m, :], ps, mod[:, 16 + m:17 + m], h[:, m, :], ALU.mult, ALU.add, t, t_mod)
            return t_h1[m]
        t_mgl = list(t_mg.values())
        project_cols(T["w_out"][0], 0, 1024, lambda k: gates[:, k, :], add_h, t_mgl)
        t_h = list(t_h1.values())

        t_mod = ada_out(24, 24, col("b_ada", 24, 24), ada(w_ada, 3072, 3072, 24))
        t_am = gain(1, "g_norm2", 32, t_mod)
        t_u = norm(h, t_h, None, sq, lambda k: am[:, 8 + k:9 + k], lambda k: mod[:, 24 + k:25 + k], u, None, t_am, t_mod)
        end1 = t_u

        top[0] = base
        sq_moe = buf(2048, (8, 256))
        combB = buf(8192, (32, 256))
        hid = buf(2048, (2, 4, 256))
        s1 = buf(1024, (2, 512))
        lg = buf(72, (2, 36))
        rt = buf(256)
        comb = buf(64, (2, 32))
        combT = buf(256)

        b, bank, free = take()
        lgps = bank[:, 0:72].rearrange("p (a b) -> p a b", a=2)
        for tc in range(2):
            for k in range(KT):
                last = mm(lgps[:, tc, :], u[:, k, tc * P:tc * P + P], wr[:, k, :], k == 0, k == KT - 1,
                          free, t_u, t_wr1, t_wr2)
        t_l = tt(lg, lgps, col("router_b", 0, 36).rearrange("p (o n) -> p o n", o=1).to_broadcast([P, 2, 36]),
                 ALU.add, last, t_cols, end1)
        bank_free[b] = t_l
        t_comb = []
        for tc in range(2):
            w = rt[:, 128 * tc:128 * tc + 128]
            l4 = lg[:, tc, 0:4]
            le = lg[:, tc, 4:36]
            gm, wg, oh4, prev = w[:, 0:1], w[:, 1:2], w[:, 4:8], w[:, 8:9]
            ex, sel, tmp = w[:, 12:16], w[:, 16:24], w[:, 24:56]
            m8, oi, o1, o2, ws = w[:, 56:64], w[:, 64:66], w[:, 72:80], w[:, 80:88], w[:, 96:104]
            ix = idxb[:, 8 * tc:8 * tc + 8]
            t_gm = op("vector", lambda e, gm=gm, l4=l4: e.reduce_max(gm, l4, AX), t_l)
            t = ts(ex, l4, gm, ALU.subtract, None, None, t_gm)
            t = act(ex, ex, ACT.Exp, t, accum=wg)
            t_wg = recip(wg, wg, t)
            t_o = ts(oh4, l4, gm, ALU.is_equal, None, None, t_gm)
            t = copy(prev, oh4[:, 0:1], t_o)
            for i in range(1, 4):
                t_o = tt(tmp[:, 0:1], oh4[:, i:i + 1], prev, ALU.is_gt, t, t_o)
                t = tt(prev, prev, oh4[:, i:i + 1], ALU.max, t_o)
                t_o = copy(oh4[:, i:i + 1], tmp[:, 0:1], t)
            t = tt(view(tmp, 4, 8), view(le, 4, 8),
                   oh4.rearrange("p (g o) -> p g o", o=1).to_broadcast([P, 4, 8]), ALU.mult, t_o)
            t = op("vector", lambda e, sel=sel, tmp=tmp: e.reduce_sum(sel, tmp.rearrange("p (g e) -> p e g", g=4), AX), t)
            t = op("vector", lambda e, m8=m8, sel=sel: e.max(m8, sel), t)
            t_m8 = t
            t = op("vector", lambda e, ix=ix, m8=m8, sel=sel: e.max_index(ix, m8, sel), t)
            t = copy(oi, ix[:, 0:2], t)
            t1 = ts(o1, iota8, oi[:, 0:1], ALU.is_equal, None, None, t, t_consts)
            t2 = ts(o2, iota8, oi[:, 1:2], ALU.is_equal, None, None, t)
            t = tt(ws[:, 0:1], m8[:, 1:2], m8[:, 0:1], ALU.subtract, t_m8)
            t_e = act(ws[:, 1:2], ws[:, 0:1], ACT.Exp, t)
            t = ts(ws[:, 2:3], ws[:, 1:2], 1.0, ALU.add, None, None, t_e)
            t = recip(ws[:, 3:4], ws[:, 2:3], t)
            t = tt(ws[:, 4:5], ws[:, 3:4], wg, ALU.mult, t, t_wg)
            t = tt(ws[:, 5:6], ws[:, 4:5], ws[:, 1:2], ALU.mult, t)
            t = ts(o1, o1, ws[:, 4:5], ALU.mult, None, None, t, t1)
            t = stt(o1, o2, ws[:, 5:6], o1, ALU.mult, ALU.add, t, t2)
            t = tt(view(comb[:, tc, :], 4, 8), oh4.rearrange("p (g o) -> p g o", o=1).to_broadcast([P, 4, 8]),
                   o1.rearrange("p (o e) -> p o e", o=1).to_broadcast([P, 4, 8]), ALU.mult, t, t_o)
            t_comb.append(t)
        b, bank, free = take()
        for tc in range(2):
            last = tp(bank[0:32, tc * P:tc * P + P], comb[:, tc, :], ident, free, t_comb)
        t_cT = copy(combT[0:32, :], bank[0:32, 0:256], last)
        bank_free[b] = t_cT
        t_cB = []
        for e0 in range(0, NE, 2):
            b, bank, free = take()
            for j in range(2):
                last = mm(bank[:, j * 256:j * 256 + 256], ident[0:32, e0 + j:e0 + j + 1].to_broadcast([32, P]),
                          combT[0:32, :], True, True, free, t_cT)
            t = copy(combB[:, e0:e0 + 2, :], view(bank[:, :], 2, 256), last, end1)
            bank_free[b] = t
            t_cB.append(t)

        acc_free = [bank_free[i] for i in range(4, 8)]
        bank_set[0] = [0, 1, 2, 3]
        t_down = [None, None]
        t_s1 = [None, None]
        for e in range(NE):
            hb = e % 2
            w1, l1, n1 = wcols(T["w1"][0, e], 0, 512)
            w3, l3, n3 = wcols(T["w3"][0, e], 0, 512)
            w2, l2, n2 = wrows(T["w2"][0, e], 0, 4)
            t_hid = []
            for g in range(2):
                b1, bank1, free1 = take()
                for j in range(2):
                    m = 2 * g + j
                    for k in range(KT):
                        last1 = mm(bank1[:, j * 256:j * 256 + 256], w1[:, k, m * P:m * P + P], u[:, k, :],
                                   k == 0, k == KT - 1, free1, l1, t_u)
                b3, bank3, free3 = take()
                for j in range(2):
                    m = 2 * g + j
                    for k in range(KT):
                        last3 = mm(bank3[:, j * 256:j * 256 + 256], w3[:, k, m * P:m * P + P], u[:, k, :],
                                   k == 0, k == KT - 1, free3, l3)
                ta = act(s1[:, g, :], bank1[:, :], ACT.Silu, last1, t_s1[g], end1)
                bank_free[b1] = ta
                hv = hid[:, hb, 2 * g:2 * g + 2, :]
                tb = tt(hv, view(s1[:, g, :], 2, 256), view(bank3[:, :], 2, 256), ALU.mult, ta, last3, t_down[hb])
                bank_free[b3] = tb
                t_s1[g] = tb
                t_hid.append(tt(hv, hv, combB[:, e:e + 1, :].to_broadcast([P, 2, 256]), ALU.mult, tb, t_cB[e // 2]))
            ring_free[n1], ring_free[n3] = last1, last3
            for m in range(8):
                o = banks[4 + m // 2][:, (m % 2) * 256:(m % 2) * 256 + 256]
                for k in range(4):
                    last = mm(o, w2[:, k, m * P:m * P + P], hid[:, hb, k, :], e == 0 and k == 0 and m % 2 == 0,
                              e == NE - 1 and k == 3, l2, t_hid[k // 2], acc_free if e == 0 else None, skip=True)
            t_down[hb] = last
            ring_free[n2] = last
        t_h = []
        for m in range(8):
            o = banks[4 + m // 2][:, (m % 2) * 256:(m % 2) * 256 + 256]
            t = stt(h[:, m, :], o, mod[:, 40 + m:41 + m], h[:, m, :], ALU.mult, ALU.add, last, t_mod)
            t_h.append(t)
            bank_free[4 + m // 2] = t
        bank_set[0] = list(range(7))

        t_mod = ada_out(48, 16, col("b_ada_f", 0, 16), ada(T["w_ada_f"], 0, 2048, 48))
        t_am = gain(2, "g_final", 56, t_mod)
        t_h = norm(h, t_h, None, sq_moe, lambda k: am[:, 16 + k:17 + k], lambda k: mod[:, 48 + k:49 + k], h, None,
                   t_am, t_mod)
        bank_set[0] = list(range(8))

        top[0] = base
        sq = buf(2048, (8, 256))
        merged = buf(2048, (8, 256))
        gate_b = buf(2048, (8, 256))
        base2 = top[0]
        t_u = norm(h, t_h, t_h, sq, lambda k: col("ln1_g_2", k), None, u, None, t_cols)
        end2 = t_u
        w_in = T["w_in_2"][0]

        t_gb = {}

        def branch_gate(i, *w):
            def evac(m, ps, t):
                t_gb[m] = act(gate_b[:, m, :], ps, ACT.Sigmoid, t, w, bias=col("b_gate_2", 8 * i + m))
                return t_gb[m]
            project_cols(w_in, IN2["gates"] + 1024 * i, 1024, rhs_u, evac, t_u)

        q = buf(2304, (9, 256))
        kk = buf(2304, (9, 256))
        vT = buf(2304, (2, 1152))
        toep = buf(18 * 256, (18, 256))
        sc = buf(768)
        pT = buf(768)
        ya = buf(768, (2, 384))
        yaF = buf(768, (3, 256))
        sm = buf(64)

        skew = 18 * 384 - 1
        t_toep = dma(toep, bass.AP(scratch.tensor, 127, [[skew, P], [384, 18], [1, 256]]), t_rep_out, end2)

        t_q, t_k = {}, {}

        def put_q(m, ps, t):
            t_q[m] = act(q[:, m, :], ps, ACT.Copy, t, end2, scale=0.125)
            return t_q[m]

        def put_k(m, ps, t):
            t_k[m] = act(kk[:, m, :], ps, ACT.Copy, t, end2)
            return t_k[m]
        project_cols(w_in, IN2["q"], 1152, rhs_u, put_q, t_u)
        project_cols(w_in, IN2["k"], 1152, rhs_u, put_k, t_u)
        t_v = []
        for c in range(3):
            slot, landed, s = wcols(w_in, IN2["v"] + 384 * c, 384)
            for tc in range(2):
                b, bank, free = take()
                for k in range(KT):
                    last = mm(bank[:, 0:384], u[:, k, tc * P:tc * P + P], slot[:, k, :], k == 0, k == KT - 1,
                              free, landed, t_u)
                t = act(vT[:, tc, c * 384:c * 384 + 384], bank[:, 0:384], ACT.Copy, last, end2)
                bank_free[b] = t
                t_v.append(t)
            ring_free[s] = last

        t_pT = t_sc = t_pv = None
        t_ya = []
        lsum = sm[:, 16:28]
        for ic in range(2):
            nk = P * (ic + 1)
            bank_set[0] = list(range(6))
            ob = 6 + ic
            for hh in range(6):
                t_s = []
                toep4 = toep.rearrange("p (g h) n -> p g h n", g=3)
                for gs in ((0, 1), (2,)):
                    b, bank, free = take()
                    for g in gs:
                        hd = 6 * g + hh
                        p0 = 64 * (hd % 2)
                        last = mm(bank[:, (g % 2) * nk:(g % 2) * nk + nk], q[p0:p0 + 64, hd // 2, ic * P:ic * P + P],
                                  kk[p0:p0 + 64, hd // 2, 0:nk], True, True, free, t_q[hd // 2], t_k[hd // 2])
                    n = len(gs)
                    t = tt(view(sc[:, gs[0] * nk:(gs[0] + n) * nk], n, nk), view(bank[:, 0:n * nk], n, nk),
                           toep4[:, gs[0]:gs[0] + n, hh, 256 - nk:256], ALU.add, last, t_toep, t_sc)
                    bank_free[b] = t
                    t_s.append(t)
                mx, lv = sm[:, hh:hh + 1], lsum[:, 6 * ic + hh:6 * ic + hh + 1]
                t = op("vector", lambda e, mx=mx, i=sc[:, 0:3 * nk]: e.reduce_max(mx, i, AX), t_s, t_sc)
                t = ts(mx, mx, -1.0, ALU.mult, None, None, t)
                t_e = act(sc[:, 0:3 * nk], sc[:, 0:3 * nk], ACT.Exp, t, bias=mx, accum=lv)
                nb = 3 * (ic + 1)
                t_p = []
                for j0 in range(0, nb, 4):
                    n = min(4, nb - j0)
                    b, bank, free = take()
                    for j in range(n):
                        last = tp(bank[:, j * P:j * P + P], sc[:, (j0 + j) * P:(j0 + j + 1) * P], ident, free, t_e)
                    t = act(pT[:, j0 * P:(j0 + n) * P], bank[:, 0:n * P], ACT.Copy, last, t_pv)
                    bank_free[b] = t
                    t_p.append(t)
                t_sc = last
                o = banks[ob][:, hh * 64:hh * 64 + 64]
                for j in range(nb):
                    g, jc = j // (ic + 1), j % (ic + 1)
                    hd = 6 * g + hh
                    t_pv = mm(o, pT[:, j * P:j * P + P], vT[:, jc, hd * 64:hd * 64 + 64], j == 0, j == nb - 1,
                              t_p, t_v, bank_free[ob])
            t = recip(lsum[:, 6 * ic:6 * ic + 6], lsum[:, 6 * ic:6 * ic + 6], t_e)
            t = tt(view(ya[:, ic, :], 6, 64), view(banks[ob][:, 0:384], 6, 64),
                   lsum[:, 6 * ic:6 * ic + 6].rearrange("p (a o) -> p a o", o=1).to_broadcast([P, 6, 64]),
                   ALU.mult, t, t_pv)
            bank_free[ob] = t
            t_ya.append(t)
        bank_set[0] = list(range(8))
        t_yaF = []
        for tc in range(2):
            b, bank, free = take()
            for j in range(3):
                last = tp(bank[:, j * P:j * P + P], ya[:, tc, j * P:j * P + P], ident, free, t_ya[tc])
            t = copy(yaF[:, :, tc * P:tc * P + P], view(bank[:, 0:384], 3, P), last)
            bank_free[b] = t
            t_yaF.append(t)
        branch_gate(0, end2)
        t_m = {}

        def first_branch(m, ps, t):
            t_m[m] = tt(merged[:, m, :], ps, gate_b[:, m, :], ALU.mult, t, t_gb[m], end2)
            return t_m[m]
        slot, landed, s = wrows(T["w_a_2"][0], 0, 3)
        ring_free[s] = project(lambda m, k: (slot[:, k, m * P:m * P + P], landed), 3, lambda k: yaF[:, k, :],
                               list(range(8)), first_branch, t_yaF)
        end_a = list(t_m.values())

        def next_branch(m, ps, t):
            t1 = tt(gate_b[:, m, :], ps, gate_b[:, m, :], ALU.mult, t, t_gb[m])
            t_m[m] = tt(merged[:, m, :], merged[:, m, :], gate_b[:, m, :], ALU.add, t1, t_m[m])
            return t1

        top[0] = base2
        p0, p1, p2 = (buf(8 * 264, (8, 264)) for _ in range(3))
        pd = buf(2048, (8, 256))
        py = buf(2048, (8, 256))
        t_pad = [fill(x[:, :, 0:8], 0.0, end_a, t_toep) for x in (p0, p1, p2)]
        t_p0 = {}

        def put_p(m, ps, t):
            t_p0[m] = act(p0[:, m, 8:264], ps, ACT.Copy, t, end_a, t_toep)
            return t_p0[m]
        project_cols(w_in, IN2["pool"], 1024, rhs_u, put_p, t_u)
        t = tt(p1[:, :, 8:264], p0[:, :, 8:264], p0[:, :, 7:263], ALU.add, list(t_p0.values()), t_pad, end_a)
        t = tt(p2[:, 2:8, 8:264], p1[:, 2:8, 8:264], p1[:, 2:8, 6:262], ALU.add, t)
        t = tt(p1[:, 4:8, 8:264], p2[:, 4:8, 8:264], p2[:, 4:8, 4:260], ALU.add, t)
        t = tt(p2[:, 6:8, 8:264], p1[:, 6:8, 8:264], p1[:, 6:8, 0:256], ALU.add, t)
        t_pd = []
        for g in range(4):
            src = (p1, p2)[g % 2]
            o = pd[:, 2 * g:2 * g + 2, :]
            ti = tt(o, src[:, 2 * g:2 * g + 2, 8:264], invcnt[:, g:g + 1, :].to_broadcast([P, 2, 256]), ALU.mult, t)
            t_pd.append(tt(o, o, p0[:, 2 * g:2 * g + 2, 8:264], ALU.subtract, ti))
        slot, landed, s = load(T["pool_w_2"][0].rearrange("g (t p) n -> p (g t) n", p=P), 8, 256)
        t_py = []
        for g in range(4):
            b, bank, free = take()
            for j in range(2):
                for k in range(2):
                    last = mm(bank[:, j * 256:j * 256 + 256], slot[:, 2 * g + k, j * P:j * P + P], pd[:, 2 * g + k, :],
                              k == 0, k == 1, free, landed, t_pd[g])
            for j in range(2):
                t = act(py[:, 2 * g + j, :], bank[:, j * 256:j * 256 + 256], ACT.Copy, last,
                        scale=col("pool_scale_2", 2 * g + j))
            bank_free[b] = t
            t_py.append(t)
        ring_free[s] = last
        branch_gate(1, end_a)
        project_cols(T["w_b_2"][0], 0, 1024, lambda k: py[:, k, :], next_branch, t_py)
        end_b = list(t_m.values())

        top[0] = base2
        zs = buf(2048, (8, 256))
        xb = buf(12 * 259, (12, 259))
        xc = buf(3072, (12, 256))
        xT2 = buf(2048, (2, 1024))
        xd = buf(1024)
        BT = buf(256)
        S0 = buf(1024)
        ys = buf(2048, (8, 256))
        Lb = buf(512)
        Cd = buf(512)
        cbm = buf(256, (2, 128))
        dtt = buf(192)
        t_z = {}

        def put_z(m, ps, t):
            t_z[m] = act(zs[:, m, :], ps, ACT.Silu, t, end_b)
            return t_z[m]
        project_cols(w_in, IN2["z"], 1024, rhs_u, put_z, t_u)
        t_xp = fill(xb[:, :, 0:3], 0.0, end_b)
        t_xb = {}

        def put_x(m, ps, t):
            t_xb[m] = act(xb[:, m, 3:259], ps, ACT.Copy, t, end_b)
            return t_xb[m]
        project_cols(w_in, IN2["xbc"], 1536, rhs_u, put_x, t_u)
        t_xc = []
        for m0 in range(0, 12, 4):
            tl = [ts(xc[:, m, :], xb[:, m, 0:256], col("ssd_conv_w_2", 4 * m), ALU.mult, col("ssd_conv_b_2", m), ALU.add,
                     t_xb[m], t_xp, end_b) for m in range(m0, m0 + 4)]
            for j in range(1, 4):
                tl = [stt(xc[:, m, :], xb[:, m, j:j + 256], col("ssd_conv_w_2", 4 * m + j), xc[:, m, :], ALU.mult, ALU.add,
                          tl[m - m0]) for m in range(m0, m0 + 4)]
            t_xc.append(act(xc[:, m0:m0 + 4, :], xc[:, m0:m0 + 4, :], ACT.Silu, tl))

        dx, dl, da, dcs, dd = (dtt[:, 32 * i:32 * i + 32] for i in range(5))
        an = dtt[:, 160:176]
        b, bank, free = take()
        for tc in range(2):
            for k in range(KT):
                last = mm(bank[:, 16 * tc:16 * tc + 16], u[:, k, tc * P:tc * P + P], wdt[:, k, :], k == 0, k == KT - 1,
                          free, t_wdt, t_u)
        t = tt(view(dx, 2, 16), view(bank[:, 0:32], 2, 16),
               col("dt_bias", 0, 16).rearrange("p (o n) -> p o n", o=1).to_broadcast([P, 2, 16]), ALU.add, last, end_b)
        bank_free[b] = t
        t1 = act(dl, dx, ACT.Abs, t)
        t1 = act(dl, dl, ACT.Exp, t1, scale=-1.0)
        t1 = act(dl, dl, ACT.Ln, t1, bias=1.0)
        t_dt = stt(dx, dx, 0.0, dl, ALU.max, ALU.add, t1)
        t_an = act(an, col("a_log", 0, 16), ACT.Exp, t_cols, end_b)
        t_da = stt(view(da, 2, 16), view(dx, 2, 16), -1.0,
                   an.rearrange("p (o n) -> p o n", o=1).to_broadcast([P, 2, 16]), ALU.mult, ALU.mult, t_dt, t_an)
        b, bank, free = take()
        last = mm(bank[:, 0:32], u128, da, True, True, free, t_da)
        last = mm(bank[:, 32:48], ones, da[:, 0:16], True, True)
        t_cs = copy(dcs, bank[:, 0:32], last)
        t = tt(dd[:, 0:16], bank[:, 32:48], dcs[:, 0:16], ALU.subtract, t_cs)
        bank_free[b] = t
        t_dd = act(dd[:, 0:16], dd[:, 0:16], ACT.Exp, t)

        t_xT = []
        for tc in range(2):
            for g in range(2):
                b, bank, free = take()
                for j in range(4):
                    m = 4 * g + j
                    last = tp(bank[:, j * P:j * P + P], xc[:, m, tc * P:tc * P + P], ident, free, t_xc[g])
                t = tt(view(xT2[:, tc, 512 * g:512 * g + 512], 8, 64), view(bank[:, :], 8, 64),
                       dx[:, 16 * tc + 8 * g:16 * tc + 8 * g + 8].rearrange("p (a o) -> p a o", o=1)
                       .to_broadcast([P, 8, 64]), ALU.mult, last, t_dt, end_b)
                bank_free[b] = t
                t_xT.append(t)
        t_xd = tt(view(xd, 16, 64), view(xT2[:, 0, :], 16, 64),
                  dd[:, 0:16].rearrange("p (a o) -> p a o", o=1).to_broadcast([P, 16, 64]), ALU.mult, t_xT, t_dd, end_b)
        b, bank, free = take()
        for g in range(2):
            last = tp(bank[:, g * P:g * P + P], xc[:, 8 + g, 0:P], ident, free, t_xc[2])
        t_BT = copy(BT, bank[:, 0:256], last, end_b)
        bank_free[b] = t_BT
        t_S0 = []
        for g in range(2):
            b, bank, free = take()
            last = mm(bank[:, :], BT[:, g * P:g * P + P], xd[:, 512 * g:512 * g + 512], True, True, free, t_BT, t_xd)
            t = act(S0[:, 512 * g:512 * g + 512], bank[:, :], ACT.Copy, last, end_b)
            bank_free[b] = t
            t_S0.append(t)

        t_ys = []
        t_y = None
        for tc in range(2):
            b, bank, free = take()
            for g in range(2):
                last = mm(bank[:, g * P:g * P + P], xc[:, 8 + g, tc * P:tc * P + P], xc[:, 10 + g, tc * P:tc * P + P],
                          True, True, free, t_xc[2])
            t_cb = tt(cbm, view(bank[:, 0:256], 2, P), u128.rearrange("p (o n) -> p o n", o=1).to_broadcast([P, 2, P]),
                      ALU.mult, last, t_y, end_b)
            bank_free[b] = t_cb
            for g in range(2):
                for hq in range(2):
                    h0 = 8 * g + 4 * hq
                    b, bank, free = take()
                    for j in range(4):
                        last = mm(bank[:, j * P:j * P + P],
                                  da[:, 16 * tc + h0 + j:16 * tc + h0 + j + 1].to_broadcast([P, P]), u128, True, True,
                                  free, t_da)
                    t = None
                    for j in range(4):
                        t = ts(Lb[:, j * P:j * P + P], bank[:, j * P:j * P + P],
                               dcs[:, 16 * tc + h0 + j:16 * tc + h0 + j + 1], ALU.subtract, 0.0, ALU.min,
                               last, t_cs, t_y)
                    t_L = act(Lb, Lb, ACT.Exp, t)
                    t_L = tt(view(Lb, 4, P), view(Lb, 4, P), cbm[:, g:g + 1, :].to_broadcast([P, 4, P]), ALU.mult, t_L, t_cb)
                    if tc:
                        t = act(Cd, bank[:, :], ACT.Exp, t, t_y)
                        bank_free[b] = t
                        t_C = tt(view(Cd, 4, P), view(Cd, 4, P),
                                 xc[:, 10 + g:11 + g, tc * P:tc * P + P].to_broadcast([P, 4, P]), ALU.mult, t, t_xc)
                    else:
                        bank_free[b] = t
                        t_C = None
                    b, bank, free = take()
                    for j in range(4):
                        o = bank[64 * (j % 2):64 * (j % 2) + 64, (j // 2) * P:(j // 2) * P + P]
                        hd = h0 + j
                        last = mm(o, xT2[:, tc, hd * 64:hd * 64 + 64], Lb[:, j * P:j * P + P], True, not tc,
                                  free, t_L, t_xT, skip=True)
                        if tc:
                            last = mm(o, S0[:, hd * 64:hd * 64 + 64], Cd[:, j * P:j * P + P], False, True, t_C, t_S0, skip=True)
                    t_y = last
                    for j in range(2):
                        m = h0 // 2 + j
                        t = stt(ys[:, m, tc * P:tc * P + P], xc[:, m, tc * P:tc * P + P], col("ssd_d_2", m),
                                bank[:, j * P:j * P + P], ALU.mult, ALU.add, last, t_xc, end_b)
                    bank_free[b] = t
                    t_ys.append(t)
        t_ys = tt(ys, ys, zs, ALU.mult, t_ys, list(t_z.values()))
        t_sq = act(sq, ys, ACT.Square, t_ys, t_u)
        t_yn = []
        for g in range(2):
            b, bank, free = take()
            for j in range(4):
                last = mm(bank[:, 0:256], ones, sq[:, 4 * g + j, :], j == 0, j == 3, free, t_sq)
            rr = Lb[:, 256 * g:256 * g + 256]
            t = act(rr, bank[:, 0:256], ACT.Sqrt, last, t_y, bias=eps, scale=1.0 / 512)
            bank_free[b] = t
            t = recip(rr, rr, t)
            for j in range(4):
                m = 4 * g + j
                t_yn.append(stt(ys[:, m, :], ys[:, m, :], col("ssd_norm_w_2", m), rr, ALU.mult, ALU.mult, t, t_sq))
        branch_gate(2, end_b)
        project_cols(T["w_c_2"][0], 0, 1024, lambda k: ys[:, k, :], next_branch, t_yn)
        end_c = list(t_m.values())

        t_h1 = {}

        def add_x(m, ps, t):
            t_h1[m] = tt(h[:, m, :], ps, h[:, m, :], ALU.add, t)
            return t_h1[m]
        project_cols(T["w_o_2"][0], 0, 1024, lambda k: merged[:, k, :], add_x, end_c)
        t_h = list(t_h1.values())

        t_u = norm(h, t_h, t_yn, sq, lambda k: col("ln2_g_2", k), None, u, None, t_cols)
        top[0] = base2
        hid = buf(22 * 256, (22, 256))
        NP_ = 4
        pads = [buf(2 * 258, (2, 258)) for _ in range(NP_)]
        cv = [buf(512, (2, 256)) for _ in range(NP_)]
        t_pad = [fill(x[:, :, 0:2], 0.0, end_c) for x in pads]
        pad_free = [None] * NP_
        cv_free = [None] * NP_
        t_hid = {}
        nn = 0
        up = T["ffn_w_up_2"][0]
        order = []
        for c in range(11):
            slot, landed, s = wcols(up, 512 * c, 512)
            for j0 in range(2):
                ms = [4 * c + 2 * j0, 4 * c + 2 * j0 + 1]
                b, bank, free = take()
                for j in range(2):
                    for k in range(KT):
                        last = mm(bank[:, j * 256:j * 256 + 256], slot[:, k, (2 * j0 + j) * P:(2 * j0 + j + 1) * P],
                                  u[:, k, :], k == 0, k == KT - 1, free, landed, t_u)
                i = nn % NP_
                nn += 1
                pd_, cv_ = pads[i], cv[i]
                t = act(pd_[:, :, 2:258], view(bank[:, :], 2, 256), ACT.Copy, last, t_pad[i], pad_free[i], end_c)
                bank_free[b] = t
                tl = [ts(cv_[:, j, :], pd_[:, j, 0:256], col("ffn_conv_w_2", 3 * ms[j]), ALU.mult,
                         col("ffn_conv_b_2", ms[j]), ALU.add, t, cv_free[i], end_c) for j in range(2)]
                for tap in range(1, 3):
                    tl = [stt(cv_[:, j, :], pd_[:, j, tap:tap + 256], col("ffn_conv_w_2", 3 * ms[j] + tap), cv_[:, j, :],
                              ALU.mult, ALU.add, tl[j]) for j in range(2)]
                pad_free[i] = tl
                if ms[0] < 22:
                    t = act(hid[:, ms[0]:ms[0] + 2, :], cv_, ACT.Silu, tl, end_c)
                else:
                    o = hid[:, ms[0] - 22:ms[0] - 20, :]
                    t = tt(o, o, cv_, ALU.mult, tl, t_hid[ms[0] - 22])
                cv_free[i] = t
                for m in ms:
                    t_hid[m % 22] = t
            ring_free[s] = last
        down = T["ffn_w_down_2"][0]
        abanks = [take() for _ in range(4)]
        for t0 in range(0, 22, 4):
            t1 = min(t0 + 4, 22)
            slot, landed, s = wrows(down, t0, t1)
            for m in range(8):
                o = abanks[m // 2][1][:, (m % 2) * 256:(m % 2) * 256 + 256]
                for k in range(t0, t1):
                    last = mm(o, slot[:, k - t0, m * P:m * P + P], hid[:, k, :], k == 0 and m % 2 == 0, k == 21,
                              landed, t_hid[k], abanks[m // 2][2], skip=True)
            ring_free[s] = last
        t_h = []
        for m in range(8):
            o = abanks[m // 2][1][:, (m % 2) * 256:(m % 2) * 256 + 256]
            t = tt(h[:, m, :], o, h[:, m, :], ALU.add, last)
            t_h.append(t)
            bank_free[abanks[m // 2][0]] = t

        t_u = norm(h, t_h, None, sq, lambda k: col("final_g_2", k), None, u, last, t_cols)
        outs = []
        for tc in range(2):
            for g in range(2):
                b, bank, free = take()
                for j in range(4):
                    last = tp(bank[:, j * P:j * P + P], u[:, 4 * g + j, tc * P:tc * P + P], ident, free, t_u)
                o = xT[:, tc, 512 * g:512 * g + 512]
                t = copy(o, bank[:, :], last)
                bank_free[b] = t
                outs.append(dma(out[0, tc * P:tc * P + P, 512 * g:512 * g + 512], o, t))
        op("sync", None, outs, t_rep_out)

        def needed(eng):
            seen = {}
            for fn, waits, tok, sem in queue[eng]:
                keep = []
                for w in waits:
                    key, val = (w.eng, w.at) if isinstance(w, Tok) else (w.sem, w.value)
                    if seen.get(key, -1) < val:
                        seen[key] = val
                        keep.append(w)
                best = {}
                for w in keep:
                    key, val = (w.eng, w.at) if isinstance(w, Tok) else (w.sem, w.value)
                    if key not in best or best[key][0] < val:
                        best[key] = (val, w)
                yield fn, [w for _, w in best.values()], tok, sem

        plan = {e: list(needed(e)) for e in engines}
        for e in engines:
            for _, waits, _, _ in plan[e]:
                for w in waits:
                    if isinstance(w, Tok):
                        w.used = True
        for e in engines:
            n = 0
            for _, _, tok, _ in plan[e]:
                n += tok.used
                tok.count = n

        block = ctx.enter_context(nc.Block())

        def emit(eng, e):
            for fn, waits, tok, sem in plan[eng]:
                for w in waits:
                    if isinstance(w, Tok):
                        e.wait_ge(done[w.eng], w.count)
                    else:
                        e.wait_ge(w.sem, w.value)
                if fn is None:
                    continue
                ins = fn(e)
                if sem is not None:
                    ins.then_inc(sem, 16)
                elif tok.used:
                    ins.then_inc(done[eng], 1)

        @block.sync
        def _(e):
            emit("sync", e)

        @block.gpsimd
        def _(e):
            emit("gpsimd", e)

        @block.scalar
        def _(e):
            emit("scalar", e)

        @block.vector
        def _(e):
            emit("vector", e)

        @block.tensor
        def _(e):
            emit("tensor", e)


DIRECT = ["x", "w_ada", "w_in", "w_conv_pw", "w_a2", "b_a2", "w_gla_o", "w_out", "w_router_g", "w_router_e",
          "w1", "w3", "w2", "w_ada_f", "rel_bias_2", "w_in_2", "w_a_2", "pool_w_2", "w_b_2", "w_c_2", "w_o_2",
          "ffn_w_up_2", "ffn_w_down_2"]


def lay_columns(inputs):
    def fcol(v):
        return v.reshape(-1, P).T

    def taps(v):
        return v.reshape(v.shape[0], -1, P).transpose(2, 1, 0).reshape(P, -1)

    def rows(v):
        return np.broadcast_to(v.reshape(1, -1), (P, v.size))

    a = {k: np.asarray(v) for k, v in inputs.items()}
    parts = {
        "w_dw": taps(a["w_dw"][0]), "ssd_conv_w_2": taps(a["ssd_conv_w_2"][0]),
        "ffn_conv_w_2": taps(a["ffn_conv_w_2"][0]),
        "ssd_d_2": fcol(np.repeat(a["ssd_d_2"][0], 64)),
        "router_b": rows(np.concatenate([a["b_router_g"][0], a["b_router_e"][0]])),
        "dt_bias": rows(a["ssd_dt_bias_2"][0]), "a_log": rows(a["ssd_a_log_2"][0]),
        "eps": np.full((P, 1), 1e-6, np.float32),
    }
    out = []
    for name, n in COLS:
        v = parts[name] if name in parts else fcol(a[name])
        assert v.shape == (P, n), (name, v.shape)
        out.append(v)
    return np.ascontiguousarray(np.concatenate(out, 1).astype(np.float32, copy=False))


def kernel(**inputs):
    import concourse.bacc as bacc
    from concourse.bass_utils import run_bass_kernel_spmd as run

    nc = bacc.Bacc("TRN2", target_bir_lowering=False, num_devices=1)
    arrays = {n: np.ascontiguousarray(np.asarray(inputs[n])) for n in DIRECT}
    arrays["cols"] = lay_columns(inputs)
    arrays["consts"] = constants()
    T, feed = {}, {}
    for n, a in arrays.items():
        feed["in_" + n] = a
        T[n] = nc.dram_tensor("in_" + n, a.shape, F32, kind="ExternalInput").ap()
    out = nc.dram_tensor("out_0", (1, S, D), F32, kind="ExternalOutput").ap()
    scratch = nc.dram_tensor("scratch", (P * 18 * 384,), F32, kind="Internal").ap()
    build(nc, T, out, scratch)
    res = run(nc, [feed], core_ids=[0])
    return res.results[0]["out_0"]
```

```python
from contextlib import ExitStack

import concourse.bass as bass
from concourse import mybir
import numpy as np

F32 = mybir.dt.float32
U32 = mybir.dt.uint32
ALU = mybir.AluOpType
ACT = mybir.ActivationFunctionType
AX = mybir.AxisListType.X

P = 128
S = 256
D = 1024
KT = D // P
NE = 32
NS = 4
SLOT = 4096
LEVELS = (32, 16, 8, 4, 2, 1)
WINDOWS = (2, 4, 8, 16)

IN1 = dict(a=0, gt=512, q=1024, k=1536, v=2048, r=3072, a1=4096, gates=4112)
IN2 = dict(q=0, k=1152, v=2304, pool=3456, z=4480, xbc=5504, dt=7040, gates=7056)

COLS = [("g_norm1", 8), ("g_norm2", 8), ("g_final", 8), ("c", 8), ("b_ada", 48), ("b_ada_f", 16),
        ("w_dw", 124), ("b_dw", 4), ("g_conv_ln", 4), ("b_conv_ln", 4), ("b_conv_pw", 8), ("g_gla_norm", 8),
        ("ln1_g_2", 8), ("b_gate_2", 24), ("pool_scale_2", 8), ("ssd_conv_w_2", 48), ("ssd_conv_b_2", 12),
        ("ssd_d_2", 8), ("ssd_norm_w_2", 8), ("ln2_g_2", 8), ("ffn_conv_w_2", 132), ("ffn_conv_b_2", 44),
        ("final_g_2", 8), ("router_b", 36), ("dt_bias", 16), ("a_log", 16), ("eps", 1), ("rtab", 18), ("w_a2", 512),
        ("w_a1", 128), ("w_dt", 128), ("w_r", 288)]
CONSTS = [("ident", 128), ("ones", 128), ("u128", 128), ("before", 128), ("invcnt", 4 * 256), ("iota", 64)]
CONSTS1 = [("u64", 128), ("masks", 7 * 128), ("oh", 3 * 384)]
CAP = 64


def spans(table):
    at, out = 0, {}
    for name, n in table:
        out[name] = (at, n)
        at += n
    return out, at


COL_AT, NCOLS = spans(COLS)
CONST_AT, NCONST = spans(CONSTS + CONSTS1)
NCONST0 = spans(CONSTS)[1]


def constants():
    c = np.zeros((P, NCONST), np.float32)

    def put(name, v):
        at, n = CONST_AT[name]
        c[:v.shape[0], at:at + n] = v

    i = np.arange(P)
    put("ident", np.eye(P))
    put("ones", np.ones((P, P)))
    le = i[:, None] <= i[None, :]
    same = i[:, None] // 64 == i[None, :] // 64
    put("u64", (le & same) / 16.0)
    put("u128", le * 1.0)
    ms = []
    for m in LEVELS:
        blk = i[:, None] // (2 * m) == i[None, :] // (2 * m)
        ms.append(blk & (i[:, None] % (2 * m) < m) & (i[None, :] % (2 * m) >= m))
    ms.append(i[:, None] == i[None, :])
    put("masks", np.concatenate(ms, 1) * 1.0)
    t = np.arange(S) + 1
    put("invcnt", np.broadcast_to(np.concatenate([1.0 / np.minimum(t, w) for w in WINDOWS]), (P, 4 * S)))
    dist = 255 - np.arange(384)
    nf = np.maximum(dist, 1).astype(np.float32)
    large = 16 + (np.log(nf / np.float32(16)) / np.float32(np.log(2048 / 16)) * np.float32(16)).astype(np.int32)
    bucket = np.where(dist < 16, np.maximum(dist, 0), np.minimum(large, 31))
    oh = np.zeros((33, 3, 384))
    for g, (w, dil) in enumerate(((128, 1), (512, 4), (2048, 16))):
        ok = (dist >= 0) & (dist <= w) & (dist % dil == 0)
        oh[bucket[ok], g, np.arange(384)[ok]] = 1.0
        oh[32, g, ~ok] = -1e30
    put("oh", oh.reshape(33, -1))
    put("before", (i[:, None] < i[None, :]) * 1.0)
    put("iota", np.broadcast_to(np.arange(64), (P, 64)))
    return c


class Tok:

    def __init__(self, eng, at, region):
        self.eng, self.at, self.region, self.used = eng, at, region, False
        self.key = (eng, region)


class Landed:
    def __init__(self, sem, value):
        self.sem, self.value = sem, value


def build(nc, T, out, scratch, dbg=None):
    ctx = ExitStack()
    engines = ("tensor", "vector", "scalar", "gpsimd", "sync")
    queue = {e: [] for e in engines}

    def flat(ws):
        for w in ws:
            if isinstance(w, (list, tuple)):
                yield from flat(w)
            elif w is not None:
                yield w

    def op(eng, fn, *waits, sem=None):
        tok = Tok(eng, len(queue[eng]), region[0])
        queue[eng].append((fn, list(flat(waits)), tok, sem))
        return tok

    region = [0]
    opened = []

    def begin(t_flag, flag):
        for e in ("tensor", "vector", "scalar", "sync"):
            opened.append(op(e, ("if", flag), t_flag))
        region[0] = 1

    def end():
        lasts = [queue[e][-1][2] for e in ("tensor", "vector", "scalar", "sync")]
        landed = {}
        for fn, _, tok, sem in queue["sync"]:
            if tok.region and sem is not None:
                landed[sem] = landed.get(sem, 0) + 16
        for e in ("tensor", "vector", "scalar", "sync"):
            op(e, None, [t for t in lasts if t.eng != "sync"], [Landed(s, n) for s, n in landed.items()])
        region[0] = 0
        for e in ("tensor", "vector", "scalar", "sync"):
            op(e, ("end",))

    with ctx:
        sem_n = [0]

        def new_sem(name):
            sem_n[0] += 1
            return ctx.enter_context(nc.semaphore(f"{name}{sem_n[0]}"))

        ARENA = 53000
        arena = ctx.enter_context(nc.sbuf_tensor("arena", [P, ARENA], F32))
        banks = [ctx.enter_context(nc.psum_tensor(f"bank{i}", [P, 512], F32)) for i in range(8)]
        idxb = ctx.enter_context(nc.sbuf_tensor("idxb", [P, 17], U32))
        done = {(e, g): new_sem("done_" + e) for e in engines for g in range(2)}

        top = [0]

        def buf(n, shape=None, at=None):
            if at is None:
                at = top[0]
                top[0] += n
            assert at + n <= ARENA, (at, n)
            v = arena[:, at:at + n]
            if shape is not None:
                names = "abcd"[:len(shape)]
                v = v.rearrange(f"p ({' '.join(names)}) -> p {' '.join(names)}", **dict(zip(names, shape)))
            return v

        def view(ap, *shape):
            names = "abcd"[:len(shape)]
            return ap.rearrange(f"p ({' '.join(names)}) -> p {' '.join(names)}", **dict(zip(names, shape)))

        def mm(o, l, r, start, stop, *w, skip=False):
            return op("tensor", lambda e: e.matmul(o, l, r, start=start, stop=stop, skip_group_check=skip), *w)

        def tp(o, i, idn, *w):
            return op("tensor", lambda e: e.transpose(o, i, idn), *w)

        def act(o, i, f, *w, bias=0.0, scale=1.0, accum=None):
            if accum is not None:
                return op("scalar", lambda e: e.activation(o, i, f, bias=bias, scale=scale, accum_out=accum), *w)
            return op("scalar", lambda e: e.activation(o, i, f, bias=bias, scale=scale), *w)

        def tt(o, a, b, f, *w, eng="vector"):
            return op(eng, lambda e: e.tensor_tensor(o, a, b, f), *w)

        def ts(o, a, s1, f1, s2, f2, *w, eng="vector"):
            if f2 is None:
                return op(eng, lambda e: e.tensor_scalar(o, a, s1, None, f1), *w)
            return op(eng, lambda e: e.tensor_scalar(o, a, s1, s2, f1, f2), *w)

        def stt(o, a, s, b, f1, f2, *w):
            return op("vector", lambda e: e.scalar_tensor_tensor(out=o, in0=a, scalar=s, in1=b, op0=f1, op1=f2), *w)

        def copy(o, i, *w, eng="vector"):
            return op(eng, lambda e: e.tensor_copy(o, i), *w)

        def recip(o, i, *w):
            return op("vector", lambda e: e.reciprocal(o, i), *w)

        def fill(o, v, *w, eng="gpsimd"):
            return op(eng, lambda e: e.memset(o, v), *w)

        def dma(o, i, *w):
            s = new_sem("d")
            op("sync", lambda e: e.dma_start(o, i), *w, sem=s)
            return Landed(s, 16)

        def finish(gen):
            for _ in gen:
                pass

        ring = [buf(SLOT) for _ in range(NS)]
        ring_sem = [new_sem("ring") for _ in range(NS)]
        ring_free = [None] * NS
        ring_n = [0]
        ring_use = [0] * NS

        def load(src, kt, n):
            s = ring_n[0] % NS
            ring_n[0] += 1
            dst = view(ring[s][:, 0:kt * n], kt, n)
            op("sync", lambda e: e.dma_start(dst, src), ring_free[s], sem=ring_sem[s])
            ring_use[s] += 1
            return dst, Landed(ring_sem[s], 16 * ring_use[s]), s

        def wcols(w, c0, n):
            return load(w[:, c0:c0 + n].rearrange("(t p) n -> p t n", p=P), w.shape[0] // P, n)

        def wrows(w, t0, t1):
            return load(w[t0 * P:t1 * P, :].rearrange("(t p) n -> p t n", p=P), t1 - t0, w.shape[1])

        bank_free = [None] * 8
        bank_set = [list(range(8))]
        bank_n = [0]

        def take():
            b = bank_set[0][bank_n[0] % len(bank_set[0])]
            bank_n[0] += 1
            return b, banks[b], bank_free[b]

        xbase = top[0]
        xT = buf(2048, (2, 1024))
        t_x = dma(xT, T["x"].rearrange("o (t p) d -> p (o t) d", p=P))
        consts = buf(NCONST0)
        t_consts = dma(consts, T["consts"][:, 0:NCONST0])
        cols = buf(NCOLS)
        t_cols = dma(cols, T["cols"])

        def col(name, i=0, n=1):
            at = COL_AT[name][0] + i
            return cols[:, at:at + n]

        consts1 = None

        def const(name):
            at, n = CONST_AT[name]
            return consts[:, at:at + n] if at < NCONST0 else consts1[:, at - NCONST0:at - NCONST0 + n]

        ident, ones, u128, before = (const(n) for n in ("ident", "ones", "u128", "before"))
        invcnt = view(const("invcnt"), 4, 256)
        iota = const("iota")
        eps = col("eps")

        rtab, wa2 = col("rtab", 0, 18), col("w_a2", 0, 512)
        wr = view(col("w_r", 0, 288), 8, 36)
        wa1 = view(col("w_a1", 0, 128), 8, 16)
        wdt = view(col("w_dt", 0, 128), 8, 16)
        t_rtab1 = t_rtab2 = t_wa2 = t_ba2 = t_wr1 = t_wr2 = t_wa1 = t_wdt = t_cols

        h = buf(2048, (8, 256))
        u = buf(2048, (8, 256))
        mod = buf(64)
        am = buf(24)
        cact = buf(8)
        rstd = buf(256)
        aacc = buf(1024, (2, 512))
        base = top[0]
        sq = view(xT.rearrange("p a b -> p (a b)"), 8, 256)

        def project(wget, kts, rhs, m_list, evac, *deps):
            last = None
            for j0 in range(0, len(m_list), 2):
                pair = m_list[j0:j0 + 2]
                b, bank, free = take()
                for j, m in enumerate(pair):
                    for k in range(kts):
                        w, wt = wget(m, k)
                        last = mm(bank[:, j * 256:j * 256 + 256], w, rhs(k), k == 0, k == kts - 1, free, wt, deps)
                bank_free[b] = [evac(m, bank[:, j * 256:j * 256 + 256], last) for j, m in enumerate(pair)]
                yield last

        def pieces(w, c0, n, rhs, evac, *deps, chunk=512):
            m0 = 0
            for c in range(0, n, chunk):
                k = min(chunk, n - c)
                slot, landed, s = wcols(w, c0 + c, k)
                for last in project(lambda m, kt, slot=slot, m0=m0: (slot[:, kt, (m - m0) * P:(m - m0) * P + P], landed),
                                    w.shape[0] // P, rhs, list(range(m0, m0 + k // P)), evac, *deps):
                    ring_free[s] = last
                    yield
                m0 += k // P

        def project_cols(*a, **k):
            finish(pieces(*a, **k))

        t_h = []
        for tc in range(2):
            for g in range(2):
                b, bank, free = take()
                for j in range(4):
                    last = tp(bank[:, j * P:j * P + P], xT[:, tc, (4 * g + j) * P:(4 * g + j + 1) * P], ident,
                              free, t_x, t_consts)
                t = copy(h[:, 4 * g:4 * g + 4, tc * P:tc * P + P], view(bank[:, :], 4, P), last)
                bank_free[b] = t
                t_h.append(t)
        t_xfree = last

        t_cact = act(cact, col("c", 0, 8), ACT.Silu, t_cols)
        mod_bank = 7
        bank_set[0] = list(range(7))
        aacc_free = [None, None]
        ada_n = [0]

        def ada(w, c0, n, m0):
            for c in range(0, n, 512):
                slot, landed, s = wcols(w, c0 + c, 512)
                i = ada_n[0] % 2
                ada_n[0] += 1
                o = aacc[:, i, :]
                t = ts(o, slot[:, 0, :], cact[:, 0:1], ALU.mult, None, None, landed, t_cact, aacc_free[i])
                for k in range(1, KT):
                    t = stt(o, slot[:, k, :], cact[:, k:k + 1], o, ALU.mult, ALU.add, t)
                ring_free[s] = t
                for m in range(4):
                    at = m0 + c // P + m
                    last = mm(banks[mod_bank][:, at:at + 1], aacc[:, i, m * P:m * P + P], ones[:, 0:1], True, True,
                              t, bank_free[mod_bank])
                aacc_free[i] = last
                yield last

        def ada_out(m0, n, bias, last):
            t = tt(mod[:, m0:m0 + n], banks[mod_bank][:, m0:m0 + n], bias, ALU.add, last, t_cols)
            bank_free[mod_bank] = t
            return t

        w_ada = T["w_ada"][0]
        *_, last = ada(w_ada, 0, 2048, 0)
        t_mod = ada_out(0, 16, col("b_ada", 0, 16), last)

        def gain(i, g, sc, t):
            return stt(am[:, 8 * i:8 * i + 8], mod[:, sc:sc + 8], 1.0, col(g, 0, 8), ALU.add, ALU.mult, t)

        t_am = gain(0, "g_norm1", 8, t_mod)

        def norm(x, t_x, t_sq_free, scale_col, shift_col, o, *t_ab):
            t_sq = [act(sq[:, 0:4, :], x[:, 0:4, :], ACT.Square, t_x, t_sq_free),
                    tt(sq[:, 4:8, :], x[:, 4:8, :], x[:, 4:8, :], ALU.mult, t_x, t_sq_free)]
            b, bank, free = take()
            for k in range(KT):
                last = mm(bank[:, 0:256], ones, sq[:, k, :], k == 0, k == KT - 1, free, t_sq[k // 4], t_consts)
            t = act(rstd, bank[:, 0:256], ACT.Sqrt, last, bias=eps, scale=1.0 / D)
            bank_free[b] = t
            t_r = recip(rstd, rstd, t)
            toks = []
            for g in range(2):
                t = tt(sq[:, 4 * g:4 * g + 4, :], x[:, 4 * g:4 * g + 4, :],
                       rstd.rearrange("p (o n) -> p o n", o=1).to_broadcast([P, 4, 256]), ALU.mult, t_r, last)
                for k in range(4 * g, 4 * g + 4):
                    if k % 2:
                        toks.append(act(o[:, k, :], sq[:, k, :], ACT.Identity, t, t_ab, scale=scale_col(k),
                                        bias=shift_col(k) if shift_col else 0.0))
                    elif shift_col:
                        toks.append(ts(o[:, k, :], sq[:, k, :], scale_col(k), ALU.mult, shift_col(k), ALU.add, t, t_ab))
                    else:
                        toks.append(ts(o[:, k, :], sq[:, k, :], scale_col(k), ALU.mult, None, None, t, t_ab))
            return toks

        rhs_u = lambda k: u[:, k, :]

        consts1 = buf(NCONST - NCONST0)
        t_consts1 = dma(consts1, T["consts"][:, NCONST0:NCONST])
        u64 = const("u64")
        masks = view(const("masks"), 7, 128)
        oh = view(const("oh"), 3, 384)
        scr = buf(5120)
        zp = buf(4 * 286, (4, 286))
        cacc = buf(1024, (4, 256))
        sig = buf(1024, (4, 256))
        q = buf(1024, (4, 256))
        kk = buf(1024, (4, 256))
        v = buf(2048, (2, 1024))
        rbase = top[0]
        r = buf(2048, (8, 256))
        gates = buf(4096, (16, 256))
        bcs = buf(1024, (4, 256))
        attn = buf(1024, (2, 4, 128), at=xbase)
        tmpm = buf(512)
        qb = scr[:, 3072:4096].rearrange("p (a b) -> p a b", a=4)
        kdT = buf(1024, (2, 4, 128), at=xbase + 1024)
        St = buf(3072, (3, 4, 256))
        a1 = aacc[:, 0, 0:256]
        small = buf(64)

        rep = buf(18 * 384, (18, 384), at=rbase)
        t_rep = []
        for i in range(18):
            b, bank, free = take()
            last = mm(bank[:, 0:384], rtab[0:33, i:i + 1].to_broadcast([33, P]), oh[0:33, i // 6, :], True, True,
                      free, t_cols, t_consts1)
            t = act(rep[:, i, :], bank[:, 0:384], ACT.Copy, last)
            bank_free[b] = t
            t_rep.append(t)
        t_rep_out = dma(scratch.rearrange("(p n) -> p n", n=18 * 384), rep.rearrange("p a b -> p (a b)"), t_rep)

        t_u = norm(h, t_h, t_xfree, lambda k: am[:, k:k + 1], lambda k: mod[:, k:k + 1], u, t_am, t_mod)

        w_in = T["w_in"][0]
        t_a1one = fill(a1[0:17, :], 1.0, aacc_free)
        t_zpad = fill(zp[:, :, 0:30], 0.0)

        b, bank, free = take()
        for k in range(KT):
            last = mm(bank[0:16, 0:256], wa1[:, k, :], u[:, k, :], k == 0, k == KT - 1, free, t_cols, t_u)
        t_a1 = copy(a1[0:16, :], bank[0:16, 0:256], last, t_a1one)
        bank_free[b] = t_a1
        lgT = view(scr[:, 2048:3072], 2, 512)
        lx = view(scr[:, 3072:4096], 2, 512)
        lps = []
        for tc in range(2):
            b, bank, free = take()
            last = mm(bank[:, :], a1[0:17, tc * P:tc * P + P], wa2[0:17, :], True, True, free, t_a1, t_cols)
            lps.append((b, bank, last))
        tl = [act(lx[:, tc, :], lps[tc][1][:, :], ACT.Abs, lps[tc][2]) for tc in range(2)]
        tl = act(lx, lx, ACT.Exp, tl, scale=-1.0)
        tl = act(lx, lx, ACT.Ln, tl, bias=1.0)
        t_lg = []
        for tc in range(2):
            b, bank, last = lps[tc]
            t = stt(lgT[:, tc, :], bank[:, :], 0.0, lx[:, tc, :], ALU.min, ALU.subtract, tl)
            bank_free[b] = t
            t_lg.append(t)
        t_b = []

        t_q, t_k = {}, {}

        def put_q(m, ps, t):
            t_q[m] = act(q[:, m, :], ps, ACT.Copy, t, scale=128.0 ** -0.5)
            return t_q[m]

        def put_k(m, ps, t):
            t_k[m] = act(kk[:, m, :], ps, ACT.Copy, t)
            return t_k[m]
        project_cols(w_in, IN1["q"], 512, rhs_u, put_q, t_u)
        for hh in range(4):
            b, bank, free = take()
            for tc in range(2):
                last = mm(bank[:, tc * P:tc * P + P], lgT[:, tc, hh * P:hh * P + P], u64, True, True,
                          free, t_lg[tc], t_consts1)
            t = copy(bcs[:, hh, :], bank[:, 0:256], last, t_rep_out)
            bank_free[b] = t
            t_b.append(t)
        project_cols(w_in, IN1["k"], 512, rhs_u, put_k, t_u)
        t_q, t_k = list(t_q.values()), list(t_k.values())

        t_sig = {}

        def put_sig(m, ps, t):
            t_sig[m] = act(sig[:, m, :], ps, ACT.Sigmoid, t)
            return t_sig[m]
        project_cols(w_in, IN1["gt"], 512, rhs_u, put_sig, t_u)
        t_z = {}

        def put_z1(m, ps, t):
            t_z[m] = tt(zp[:, m, 30:286], ps, sig[:, m, :], ALU.mult, t, t_sig[m])
            return t_z[m]
        project_cols(w_in, IN1["a"], 512, rhs_u, put_z1, t_u)

        t_conv = [None] * 4

        def conv_taps():
            for m in range(4):
                t_conv[m] = ts(cacc[:, m, :], zp[:, m, 0:256], col("w_dw", m * 31), ALU.mult, col("b_dw", m), ALU.add,
                               t_z[m], t_zpad, t_cols)
            yield
            for j in range(1, 31):
                for m in range(4):
                    t_conv[m] = stt(cacc[:, m, :], zp[:, m, j:j + 256], col("w_dw", m * 31 + j), cacc[:, m, :],
                                    ALU.mult, ALU.add, t_conv[m])
                yield

        t_v = []

        def values():
            for c in range(2):
                slot, landed, s = wcols(w_in, IN1["v"] + 512 * c, 512)
                for tc in range(2):
                    b, bank, free = take()
                    for k in range(KT):
                        last = mm(bank[:, :], u[:, k, tc * P:tc * P + P], slot[:, k, :], k == 0, k == KT - 1,
                                  free, landed, t_u)
                    t = act(v[:, tc, c * 512:c * 512 + 512], bank[:, :], ACT.Copy, last)
                    bank_free[b] = t
                    t_v.append(t)
                    ring_free[s] = last
                    yield

        t_r, t_g = {}, {}

        def put_r(m, ps, t):
            t_r[m] = act(r[:, m, :], ps, ACT.Copy, t, t_rep_out)
            return t_r[m]

        def put_g(m, ps, t):
            t_g[m] = act(gates[:, m, :], ps, ACT.Copy, t, t_rep_out)
            return t_g[m]

        def fillers():
            yield from values()
            yield from pieces(w_in, IN1["r"], 1024, rhs_u, put_r, t_u)
            yield from pieces(w_in, IN1["gates"], 2048, rhs_u, put_g, t_u)

        filler = fillers()
        taps = conv_taps()

        def run(gen, n):
            for _ in range(n):
                next(gen, None)

        dq, e1, e2, qe, ke = (scr[:, 1024 * i:1024 * i + 1024] for i in range(5))
        qf, kf, bf = (x.rearrange("p a b -> p (a b)") for x in (q, kk, bcs))
        t_attn = [None, None]
        t_free = [t_b]
        for li in range(7):
            if li < 6:
                m = LEVELS[li]
                n = 1024 // (2 * m)
                b3 = view(bf, n, 2 * m)
                t = tt(view(dq, n, 2 * m), b3, b3[:, :, m - 1:m].to_broadcast([P, n, 2 * m]), ALU.subtract, t_b, t_free)
                ta = ts(e1, dq, 0.0, ALU.min, None, None, t, t_free)
                tb = ts(e2, dq, 0.0, ALU.max, None, None, t, t_free)
                ta = act(e1, e1, ACT.Exp, ta)
                tb = act(e2, e2, ACT.Exp, tb, scale=-1.0)
                run(taps, 5)
                ta = tt(qe, qf, e1, ALU.mult, ta, t_q, t_free)
                tb = tt(ke, kf, e2, ALU.mult, tb, t_k, t_free)
                qs, ks = view(qe, 4, 256), view(ke, 4, 256)
                t_in = [ta, tb]
            else:
                qs, ks, t_in = q, kk, [t_q, t_k]
            run(filler, 2)
            t_free = []
            for tc in range(2):
                b, bank, free = take()
                for hh in range(4):
                    last = mm(bank[:, hh * P:hh * P + P], ks[:, hh, tc * P:tc * P + P], qs[:, hh, tc * P:tc * P + P],
                              True, True, free, t_in)
                t_free.append(last)
                mk = masks[:, li:li + 1, :].to_broadcast([P, 4, P])
                if li == 0:
                    t = tt(attn[:, tc, :, :], view(bank[:, :], 4, P), mk, ALU.mult, last, t_consts1)
                    bank_free[b] = t
                else:
                    t = tt(view(tmpm, 4, P), view(bank[:, :], 4, P), mk, ALU.mult, last, t_attn)
                    bank_free[b] = t
                    t = tt(attn[:, tc, :, :], attn[:, tc, :, :], view(tmpm, 4, P), ALU.add, t)
                t_attn[tc] = t
        t_lev = t_free
        finish(taps)

        t = act(e1, bf, ACT.Exp, t_b, t_lev)
        t_qb = tt(qb.rearrange("p a b -> p (a b)"), qf, e1, ALU.mult, t, t_q, t_lev)
        b3 = view(bf, 16, 64)
        t = tt(view(dq, 16, 64), b3, b3[:, :, 63:64].to_broadcast([P, 16, 64]), ALU.subtract, t_b, t_lev)
        t = act(e2, dq, ACT.Exp, t, t_lev, scale=-1.0)
        t_kd = tt(ke, kf, e2, ALU.mult, t, t_k, t_lev)
        dec = small[:, 0:16]
        t_dec = act(dec, b3[:, :, 63], ACT.Exp, t_b)
        dec3 = view(dec, 4, 4)
        ke3 = view(ke, 4, 256)
        run(filler, 2)
        t_kdT = []
        for tc in range(2):
            b, bank, free = take()
            for hh in range(4):
                last = tp(bank[:, hh * P:hh * P + P], ke3[:, hh, tc * P:tc * P + P], ident, free, t_kd)
            t = act(kdT[:, tc, :, :], view(bank[:, :], 4, P), ACT.Copy, last)
            bank_free[b] = t
            t_kdT.append(t)
        t_S = []
        for c in range(3):
            tc, s0 = c // 2, 64 * (c % 2)
            row = []
            for g in range(2):
                b, bank, free = take()
                for j in range(2):
                    hh = 2 * g + j
                    last = mm(bank[:, j * 256:j * 256 + 256], kdT[s0:s0 + 64, tc, hh, :],
                              v[s0:s0 + 64, tc, hh * 256:hh * 256 + 256], True, True, free, t_kdT[tc], t_v)
                for j in range(2):
                    hh = 2 * g + j
                    ps = bank[:, j * 256:j * 256 + 256]
                    if c == 0:
                        t = copy(St[:, c, hh, :], ps, last)
                    else:
                        t = stt(St[:, c, hh, :], St[:, c - 1, hh, :], dec3[:, hh, c:c + 1], ps, ALU.mult, ALU.add,
                                last, t_dec, t_S[c - 1][hh])
                    row.append(t)
                bank_free[b] = t
            t_S.append(row)

        b, bank, free = take()
        for m in range(4):
            last = mm(bank[:, 0:256], ones, cacc[:, m, :], m == 0, m == 3, free, t_conv[m])
        mu = tmpm[:, 0:256]
        t = ts(mu, bank[:, 0:256], 1.0 / 512, ALU.mult, None, None, last, t_attn)
        bank_free[b] = t
        t_c = tt(cacc, cacc, mu.rearrange("p (o n) -> p o n", o=1).to_broadcast([P, 4, 256]), ALU.subtract, t, last)
        t_s2 = act(sig, cacc, ACT.Square, t_c, list(t_z.values()))
        run(filler, 2)
        b, bank, free = take()
        for m in range(4):
            last = mm(bank[:, 0:256], ones, sig[:, m, :], m == 0, m == 3, free, t_s2)
        t_ln = last
        lnb = (b, bank)

        ss = small[:, 16:24]
        rs = small[:, 24:32]
        on = view(scr[:, 1024:3072], 2, 1024)
        junk = tmpm[:, 256:512]
        t_on = []
        obanks = []
        t_ss = None
        for tc in range(2):
            for g in range(2):
                b, bank, free = take()
                for j in range(2):
                    hh = 2 * g + j
                    last = mm(bank[:, j * 256:j * 256 + 256], attn[:, tc, hh, :], v[:, tc, hh * 256:hh * 256 + 256],
                              True, False, free, t_attn[tc], t_v, skip=True)
                    for s in range(2):
                        c = 2 * tc + s
                        if c:
                            last = mm(bank[64 * s:64 * s + 64, j * 256:j * 256 + 256], qb[:, hh, c * 64:c * 64 + 64],
                                      St[:, c - 1, hh, :], False, True, t_qb, t_S[c - 1][hh], skip=True)
                for j in range(2):
                    i = tc * 4 + 2 * g + j
                    t_ss = act(junk, bank[:, j * 256:j * 256 + 256], ACT.Square, last, t_ss, t_attn,
                               accum=ss[:, i:i + 1])
                obanks.append((b, bank, tc, g))
        t = act(rs, ss, ACT.Sqrt, t_ss, bias=eps, scale=1.0 / 256)
        t_mu = act(mu, lnb[1][:, 0:256], ACT.Sqrt, t_ln, t_c, bias=eps, scale=1.0 / 512)
        bank_free[lnb[0]] = t_mu
        t_rs = recip(rs, rs, t)
        for b, bank, tc, g in obanks:
            for j in range(2):
                hh = 2 * g + j
                t = ts(on[:, tc, hh * 256:hh * 256 + 256], bank[:, j * 256:j * 256 + 256],
                       rs[:, tc * 4 + hh:tc * 4 + hh + 1], ALU.mult, None, None, t_rs, t_lev, t_kd, t_qb)
            bank_free[b] = t
            t_on.append(t)
        t = recip(mu, mu, t_mu)
        t = tt(cacc, cacc, mu.rearrange("p (o n) -> p o n", o=1).to_broadcast([P, 4, 256]), ALU.mult, t, t_s2)
        finish(filler)
        t_cs = [act(sig[:, m, :], cacc[:, m, :], ACT.Silu, t, t_ln, scale=col("g_conv_ln", m), bias=col("b_conv_ln", m))
                for m in range(4)]
        t_rr = [act(r[:, 4 * g:4 * g + 4, :], r[:, 4 * g:4 * g + 4, :], ACT.Silu, [t_r[m] for m in range(4 * g, 4 * g + 4)])
                for g in range(2)]
        t_gg = [act(gates[:, 4 * g:4 * g + 4, :], gates[:, 4 * g:4 * g + 4, :], ACT.Sigmoid,
                    [t_g[m] for m in range(4 * g, 4 * g + 4)]) for g in range(4)]
        t_og = []
        for tc in range(2):
            for g in range(2):
                b, bank, free = take()
                for j in range(4):
                    m = 4 * g + j
                    last = tp(bank[:, j * P:j * P + P], on[:, tc, m * P:m * P + P], ident, free, t_on)
                for j in range(4):
                    m = 4 * g + j
                    t = stt(r[:, m, tc * P:tc * P + P], bank[:, j * P:j * P + P], col("g_gla_norm", m),
                            r[:, m, tc * P:tc * P + P], ALU.mult, ALU.mult, last, t_rr[g])
                bank_free[b] = t
                t_og.append(t)

        t_mg = {}

        def y_conv(m, ps, t):
            t_mg[m] = stt(gates[:, m, :], ps, col("b_conv_pw", m), gates[:, m, :], ALU.add, ALU.mult, t, t_gg[m // 4])
            return t_mg[m]
        project_cols(T["w_conv_pw"][0], 0, 1024, lambda k: sig[:, k, :], y_conv, t_cs)

        mods = ada(w_ada, 2048, 4096, 16)
        t_modp = [None]

        def mod_step(n):
            for _ in range(n):
                t = next(mods, None)
                if t is not None:
                    t_modp[0] = t

        def y_gla(m, ps, t):
            t1 = tt(gates[:, 8 + m, :], ps, gates[:, 8 + m, :], ALU.mult, t, t_gg[2 + m // 4])
            t_mg[m] = tt(gates[:, m, :], gates[:, m, :], gates[:, 8 + m, :], ALU.add, t1, t_mg[m])
            return t1
        for _ in pieces(T["w_gla_o"][0], 0, 1024, lambda k: r[:, k, :], y_gla, t_og):
            mod_step(1)
        mod_step(8)
        t_mod = ada_out(16, 32, col("b_ada", 16, 32), t_modp[0])

        t_h1 = {}

        def add_h(m, ps, t):
            t_h1[m] = stt(h[:, m, :], ps, mod[:, 16 + m:17 + m], h[:, m, :], ALU.mult, ALU.add, t, t_mod)
            return t_h1[m]
        t_mgl = list(t_mg.values())
        project_cols(T["w_out"][0], 0, 1024, lambda k: gates[:, k, :], add_h, t_mgl)
        t_h = list(t_h1.values())

        t_am = gain(1, "g_norm2", 32, t_mod)
        t_u = norm(h, t_h, t_xfree, lambda k: am[:, 8 + k:9 + k], lambda k: mod[:, 24 + k:25 + k], u, t_am, t_mod)
        end1 = t_u

        top[0] = base
        uT = buf(2048, (2, 1024))
        hot = buf(2 * 32 * CAP, (2, 32, CAP))
        wide = top[0]
        whot = buf(32 * CAP, (32, CAP))
        sendT = buf(16 * 256, (16, 256))
        xg = buf(2048, (2, 8, 128))
        s1 = buf(512)
        hid = buf(512)
        hidT = buf(1024, (2, 4, 128))
        ye = buf(2048, (2, 1024))
        lg = buf(72, (2, 36))
        rt = buf(256)
        comb = buf(64, (2, 32))
        mask = buf(64, (2, 32))
        rank = buf(64, (2, 32))
        slotn = buf(64, (2, 32))
        combO = buf(64, (2, 32))
        cnt = buf(2)

        b, bank, free = take()
        lgps = bank[:, 0:72].rearrange("p (a b) -> p a b", a=2)
        for tc in range(2):
            for k in range(KT):
                last = mm(lgps[:, tc, :], u[:, k, tc * P:tc * P + P], wr[:, k, :], k == 0, k == KT - 1,
                          free, t_u, t_cols)
        t_l = tt(lg, lgps, col("router_b", 0, 36).rearrange("p (o n) -> p o n", o=1).to_broadcast([P, 2, 36]),
                 ALU.add, last, t_cols, end1)
        bank_free[b] = t_l
        t_uT = []
        for tc in range(2):
            for g in range(2):
                b, bank, free = take()
                for j in range(4):
                    last = tp(bank[:, j * P:j * P + P], u[:, 4 * g + j, tc * P:tc * P + P], ident, free, t_u)
                t = act(uT[:, tc, 512 * g:512 * g + 512], bank[:, :], ACT.Copy, last, end1)
                bank_free[b] = t
                t_uT.append(t)
        t_comb, t_mask = [], []
        steps = [[], []]
        for tc in range(2):
            w = rt[:, 128 * tc:128 * tc + 128]
            l4 = lg[:, tc, 0:4]
            le = lg[:, tc, 4:36]
            gm, wg, oh4, prev = w[:, 0:1], w[:, 1:2], w[:, 4:8], w[:, 8:9]
            ex, sel, tmp = w[:, 12:16], w[:, 16:24], w[:, 24:56]
            m8, oi, o1, o2, ws = w[:, 56:64], w[:, 64:66], w[:, 72:80], w[:, 80:88], w[:, 96:104]
            om = w[:, 104:112]
            ix = idxb[:, 8 * tc:8 * tc + 8]
            oh4b = oh4.rearrange("p (g o) -> p g o", o=1).to_broadcast([P, 4, 8])
            t_gm = op("vector", lambda e, gm=gm, l4=l4: e.reduce_max(gm, l4, AX), t_l)
            t = ts(ex, l4, gm, ALU.subtract, None, None, t_gm)
            t_ex = act(ex, ex, ACT.Exp, t, accum=wg)
            t_o = ts(oh4, l4, gm, ALU.is_equal, None, None, t_gm)
            t = copy(prev, oh4[:, 0:1], t_o)
            for i in range(1, 4):
                t_o = tt(tmp[:, 0:1], oh4[:, i:i + 1], prev, ALU.is_gt, t, t_o)
                t = tt(prev, prev, oh4[:, i:i + 1], ALU.max, t_o)
                t_o = copy(oh4[:, i:i + 1], tmp[:, 0:1], t)
            t = tt(view(tmp, 4, 8), view(le, 4, 8), oh4b, ALU.mult, t_o)
            t = op("vector", lambda e, sel=sel, tmp=tmp: e.reduce_sum(sel, tmp.rearrange("p (g e) -> p e g", g=4), AX), t)
            t = op("vector", lambda e, m8=m8, sel=sel: e.max(m8, sel), t)
            t_d = tt(ws[:, 0:1], m8[:, 1:2], m8[:, 0:1], ALU.subtract, t)
            t_e = act(ws[:, 1:2], ws[:, 0:1], ACT.Exp, t_d)
            t = op("vector", lambda e, ix=ix, m8=m8, sel=sel: e.max_index(ix, m8, sel), t)
            t = copy(oi, ix[:, 0:2], t)
            t1 = ts(o1, iota[:, 0:8], oi[:, 0:1], ALU.is_equal, None, None, t, t_consts)
            t2 = ts(o2, iota[:, 0:8], oi[:, 1:2], ALU.is_equal, None, None, t)
            t = tt(om, o1, o2, ALU.add, t1, t2)
            t_mask.append(tt(view(mask[:, tc, :], 4, 8), oh4b, om.rearrange("p (o e) -> p o e", o=1).to_broadcast([P, 4, 8]),
                             ALU.mult, t, t_o))
            t_wg = recip(wg, wg, t_ex)
            t = ts(ws[:, 2:3], ws[:, 1:2], 1.0, ALU.add, None, None, t_e)
            t = recip(ws[:, 3:4], ws[:, 2:3], t)
            t = tt(ws[:, 4:5], ws[:, 3:4], wg, ALU.mult, t, t_wg)
            t = tt(ws[:, 5:6], ws[:, 4:5], ws[:, 1:2], ALU.mult, t)
            t = ts(o1, o1, ws[:, 4:5], ALU.mult, None, None, t, t_mask)
            t = stt(o1, o2, ws[:, 5:6], o1, ALU.mult, ALU.add, t)
            t_comb.append(tt(view(comb[:, tc, :], 4, 8), oh4b,
                             o1.rearrange("p (o e) -> p o e", o=1).to_broadcast([P, 4, 8]), ALU.mult, t))

        b, bank, free = take()
        mm(bank[:, 0:32], before, mask[:, 0, :], True, True, free, t_mask, t_consts)
        mm(bank[:, 32:64], ones, mask[:, 0, :], True, False)
        mm(bank[:, 32:64], before, mask[:, 1, :], False, True)
        mm(bank[:, 64:96], ones, mask[:, 0, :], True, False)
        last = mm(bank[:, 64:96], ones, mask[:, 1, :], False, True)
        t = copy(rank, view(bank[:, 0:64], 2, 32), last)
        t_cnt = op("vector", lambda e, i=bank[:, 64:96]: e.reduce_max(cnt[:, 0:1], i, AX), last)
        bank_free[b] = t_cnt
        t_flag = ts(idxb[:, 16:17], cnt[:, 0:1], CAP + 0.5, ALU.is_gt, None, None, t_cnt)
        t_r1 = stt(slotn, rank, 1.0, mask, ALU.add, ALU.mult, t)
        t_r2 = ts(slotn, slotn, -1.0, ALU.add, None, None, t_r1)
        t_hot = []
        for tc in range(2):
            t_hot.append(tt(hot[:, tc, :, :], slotn[:, tc, :].rearrange("p (e o) -> p e o", o=1).to_broadcast([P, 32, CAP]),
                            iota[:, 0:CAP].rearrange("p (o c) -> p o c", o=1).to_broadcast([P, 32, CAP]), ALU.is_equal,
                            t_r2))
        t_send = [[], []]
        t_w = None
        for tc in range(2):
            t_w = tt(whot, hot[:, tc, :, :], comb[:, tc, :].rearrange("p (e o) -> p e o", o=1).to_broadcast([P, 32, CAP]),
                     ALU.mult, t_hot[tc], t_comb[tc], t_w)
            wh = whot.rearrange("p e c -> p (e c)")
            for g in range(4):
                b, bank, free = take()
                for j in range(4):
                    i = 4 * g + j
                    t_w1 = tp(bank[:, j * P:j * P + P], wh[:, i * P:i * P + P], ident, free, t_w)
                t = act(sendT[:, 4 * g:4 * g + 4, tc * P:tc * P + P], view(bank[:, :], 4, P), ACT.Copy, t_w1)
                bank_free[b] = t
                t_send[tc].append(t)
            t_w = t_w1
        t = ts(combO, rank, CAP - 0.5, ALU.is_gt, None, None, t_r1)
        t_combO = tt(combO, combO, comb, ALU.mult, t, t_comb)

        acc_free = [bank_free[i] for i in range(4, 8)]
        bank_set[0] = [0, 1, 2, 3]
        w1v, w3v, w2v = (T[n][0].rearrange("(j e) (t p) n -> j p e t n", e=2, p=P) for n in ("w1", "w3", "w2"))
        hot2 = hot.rearrange("p t e c -> p t (e c)")
        t_xg = [None, None]
        t_hT = [None, None]
        t_sc = [None, None]
        t_s1 = None

        def load_pair(src, kts, n):
            s = ring_n[0] % NS
            ring_n[0] += 1
            dst = ring[s].rearrange("p (e t n) -> p e t n", e=2, t=kts)
            for i in range(2):
                op("sync", lambda e, i=i: e.dma_start(dst[:, i, :, :], src[:, i, :, :]), ring_free[s], sem=ring_sem[s])
            ring_use[s] += 2
            return dst, Landed(ring_sem[s], 16 * ring_use[s]), s

        def gather(pair):
            i = pair % 2
            toks = []
            for g in range(2):
                b, bank, free = take()
                for j in range(4):
                    k = 4 * g + j
                    for tc in range(2):
                        last = mm(bank[:, j * P:j * P + P], uT[:, tc, k * P:k * P + P], hot2[:, tc, pair * P:pair * P + P],
                                  tc == 0, tc == 1, free, t_uT, t_hot)
                t = copy(xg[:, i, 4 * g:4 * g + 4, :], view(bank[:, :], 4, P), last, t_xg[i])
                bank_free[b] = t
                toks.append(t)
            return toks

        t_in = gather(0)
        for pair in range(16):
            i = pair % 2
            up = []
            for wv in (w1v, w3v):
                b, bank, free = take()
                for th in range(2):
                    slot, landed, s = load_pair(wv[pair, :, :, 4 * th:4 * th + 4, :], 4, 512)
                    for k in range(4):
                        for e in range(2):
                            last = mm(bank[64 * e:64 * e + 64, :], xg[:, i, 4 * th + k, 64 * e:64 * e + 64], slot[:, e, k, :],
                                      th == 0 and k == 0, th == 1 and k == 3, free, landed, t_in[th], skip=True)
                    ring_free[s] = last
                up.append((b, bank, last))
            t_xg[i] = last
            ta = act(s1, up[0][1][:, :], ACT.Silu, up[0][2], t_s1)
            bank_free[up[0][0]] = ta
            t_s1 = tt(hid, s1, up[1][1][:, :], ALU.mult, ta, up[1][2], t_hT)
            bank_free[up[1][0]] = t_s1
            if pair < 15:
                t_in = gather(pair + 1)
            b, bank, free = take()
            for j in range(4):
                last = tp(bank[:, j * P:j * P + P], hid[:, j * P:j * P + P], ident, free, t_s1)
            t_hT[0] = last
            t = act(hidT[:, i, :, :], view(bank[:, :], 4, P), ACT.Copy, last, t_sc)
            bank_free[b] = t
            ob = [take() for _ in range(2)]
            for th in range(2):
                slot, landed, s = load_pair(w2v[pair, :, :, 2 * th:2 * th + 2, :], 2, 1024)
                for k in range(2):
                    for n in range(2):
                        for e in range(2):
                            last = mm(ob[n][1][64 * e:64 * e + 64, :], hidT[:, i, 2 * th + k, 64 * e:64 * e + 64],
                                      slot[:, e, k, 512 * n:512 * n + 512], th == 0 and k == 0, th == 1 and k == 1,
                                      t, landed, ob[n][2], skip=True)
                ring_free[s] = last
            t0 = act(ye[:, i, 0:512], ob[0][1][:, :], ACT.Copy, last, t_sc[i])
            t1 = copy(ye[:, i, 512:1024], ob[1][1][:, :], last, t_sc[i])
            bank_free[ob[0][0]], bank_free[ob[1][0]] = t0, t1
            for m in range(8):
                o = banks[4 + m // 2][:, (m % 2) * 256:(m % 2) * 256 + 256]
                last = mm(o, ye[:, i, m * P:m * P + P], sendT[:, pair, :], pair == 0 and m % 2 == 0, pair == 15,
                          t0 if m < 4 else t1, t_send, acc_free if pair == 0 else None, skip=True)
            t_sc[i] = last
        t_acc = last

        kept = (list(ring_free), list(bank_free))
        begin(t_flag, idxb[0:1, 16:17])
        combT = buf(256, at=wide)
        combB = buf(8192, (32, 256), at=wide + 256)
        hidG = buf(2048, (2, 4, 256), at=base)
        sG = buf(1024, (2, 512), at=base + 2048)
        gsem = [new_sem("general") for _ in range(NS)]
        guse = [0] * NS

        def load_general(src, kt, n):
            s = ring_n[0] % NS
            ring_n[0] += 1
            dst = view(ring[s][:, 0:kt * n], kt, n)
            op("sync", lambda e: e.dma_start(dst, src), ring_free[s], sem=gsem[s])
            guse[s] += 1
            return dst, Landed(gsem[s], 16 * guse[s]), s

        b, bank, free = take()
        for tc in range(2):
            last = tp(bank[0:32, tc * P:tc * P + P], combO[:, tc, :], ident, free, t_combO)
        t_cT = copy(combT[0:32, :], bank[0:32, 0:256], last, t_acc)
        bank_free[b] = t_cT
        t_cB = []
        for e0 in range(0, NE, 2):
            b, bank, free = take()
            for j in range(2):
                last = mm(bank[:, j * 256:j * 256 + 256], ident[0:32, e0 + j:e0 + j + 1].to_broadcast([32, P]),
                          combT[0:32, :], True, True, free, t_cT)
            t = copy(combB[:, e0:e0 + 2, :], view(bank[:, :], 2, 256), last, t_acc)
            bank_free[b] = t
            t_cB.append(t)
        t_down = [None, None]
        t_sG = [None, None]
        for e in range(NE):
            hb = e % 2
            wsrc = [T[n][0, e].rearrange("(t p) n -> p t n", p=P) for n in ("w1", "w3", "w2")]
            w1, l1, n1 = load_general(wsrc[0], 8, 512)
            w3, l3, n3 = load_general(wsrc[1], 8, 512)
            w2, l2, n2 = load_general(wsrc[2], 4, 1024)
            t_hid = []
            for g in range(2):
                b1, bank1, free1 = take()
                for j in range(2):
                    m = 2 * g + j
                    for k in range(KT):
                        last1 = mm(bank1[:, j * 256:j * 256 + 256], w1[:, k, m * P:m * P + P], u[:, k, :],
                                   k == 0, k == KT - 1, free1, l1, t_u)
                b3, bank3, free3 = take()
                for j in range(2):
                    m = 2 * g + j
                    for k in range(KT):
                        last3 = mm(bank3[:, j * 256:j * 256 + 256], w3[:, k, m * P:m * P + P], u[:, k, :],
                                   k == 0, k == KT - 1, free3, l3)
                ta = act(sG[:, g, :], bank1[:, :], ACT.Silu, last1, t_sG[g], t_acc)
                bank_free[b1] = ta
                hv = hidG[:, hb, 2 * g:2 * g + 2, :]
                tb = tt(hv, view(sG[:, g, :], 2, 256), view(bank3[:, :], 2, 256), ALU.mult, ta, last3, t_down[hb], t_acc)
                bank_free[b3] = tb
                t_sG[g] = tb
                t_hid.append(tt(hv, hv, combB[:, e:e + 1, :].to_broadcast([P, 2, 256]), ALU.mult, tb, t_cB[e // 2]))
            ring_free[n1], ring_free[n3] = last1, last3
            for m in range(8):
                o = banks[4 + m // 2][:, (m % 2) * 256:(m % 2) * 256 + 256]
                for k in range(4):
                    last = mm(o, w2[:, k, m * P:m * P + P], hidG[:, hb, k, :], False, e == NE - 1 and k == 3,
                              l2, t_hid[k // 2], t_acc, skip=True)
            t_down[hb] = last
            ring_free[n2] = last
        end()
        ring_free[:], bank_free[:] = kept

        t_h = []
        for m in range(8):
            o = banks[4 + m // 2][:, (m % 2) * 256:(m % 2) * 256 + 256]
            t = stt(h[:, m, :], o, mod[:, 40 + m:41 + m], h[:, m, :], ALU.mult, ALU.add, t_acc, t_mod)
            t_h.append(t)
            bank_free[4 + m // 2] = t
        bank_set[0] = list(range(7))

        *_, last = ada(T["w_ada_f"], 0, 2048, 48)
        t_mod = ada_out(48, 16, col("b_ada_f", 0, 16), last)
        t_am = gain(2, "g_final", 56, t_mod)
        t_h = norm(h, t_h, t_uT, lambda k: am[:, 16 + k:17 + k], lambda k: mod[:, 48 + k:49 + k], h, t_am, t_mod)
        bank_set[0] = list(range(8))

        t_u = norm(h, t_h, t_h, lambda k: col("ln1_g_2", k), None, u, t_cols)
        end2 = t_u
        w_in = T["w_in_2"][0]
        top[0] = base
        merged = buf(2048, (8, 256))
        gate_b = [buf(2048, (8, 256)) for _ in range(2)]
        zs = buf(2048, (8, 256))
        p0 = buf(8 * 264, (8, 264))
        base2 = top[0]

        t_gb = [{}, {}, {}]

        def branch_gate(i, *w):
            def evac(m, ps, t):
                t_gb[i][m] = act(gate_b[i % 2][:, m, :], ps, ACT.Identity, t, w, bias=col("b_gate_2", 8 * i + m))
                return t_gb[i][m]
            return pieces(w_in, IN2["gates"] + 1024 * i, 1024, rhs_u, evac, t_u)

        def gate_on(i):
            g = gate_b[i % 2]
            for n in range(2):
                t = act(g[:, 4 * n:4 * n + 4, :], g[:, 4 * n:4 * n + 4, :], ACT.Sigmoid,
                        [t_gb[i][m] for m in range(4 * n, 4 * n + 4)])
                for m in range(4 * n, 4 * n + 4):
                    t_gb[i][m] = t

        q = buf(2304, (9, 256))
        kk = buf(2304, (9, 256))
        vT = buf(2304, (2, 1152))
        toep = buf(18 * 256, (18, 256))
        scs = [buf(768) for _ in range(2)]
        pTs = [buf(768) for _ in range(2)]
        ya = buf(768, (2, 384))
        yaF = q[:, 0:3, :]
        sm = buf(64)
        toep4 = toep.rearrange("p (g h) n -> p g h n", g=3)

        skew = 18 * 384 - 1
        t_toep = dma(toep, bass.AP(scratch.tensor, 127, [[skew, P], [384, 18], [1, 256]]), t_rep_out, end2)

        t_q, t_k = {}, {}

        def put_q(m, ps, t):
            t_q[m] = act(q[:, m, :], ps, ACT.Copy, t, end2, scale=0.125)
            return t_q[m]

        def put_k(m, ps, t):
            t_k[m] = copy(kk[:, m, :], ps, t, end2)
            return t_k[m]
        project_cols(w_in, IN2["q"], 1152, rhs_u, put_q, t_u, chunk=384)
        project_cols(w_in, IN2["k"], 1152, rhs_u, put_k, t_u, chunk=384)

        t_v = []
        t_pad = [fill(p0[:, :, 0:8], 0.0, end2)]
        t_p0, t_z = {}, {}

        def put_p(m, ps, t):
            t_p0[m] = act(p0[:, m, 8:264], ps, ACT.Copy, t, end2)
            return t_p0[m]

        def put_z(m, ps, t):
            t_z[m] = act(zs[:, m, :], ps, ACT.Copy, t, end2)
            return t_z[m]

        def values2():
            for c in range(3):
                slot, landed, s = wcols(w_in, IN2["v"] + 384 * c, 384)
                for tc in range(2):
                    b, bank, free = take()
                    for k in range(KT):
                        last = mm(bank[:, 0:384], u[:, k, tc * P:tc * P + P], slot[:, k, :], k == 0, k == KT - 1,
                                  free, landed, t_u)
                    t = act(vT[:, tc, c * 384:c * 384 + 384], bank[:, 0:384], ACT.Copy, last, end2)
                    bank_free[b] = t
                    t_v.append(t)
                    ring_free[s] = last
                    yield

        def fillers2():
            yield from pieces(w_in, IN2["pool"], 1024, rhs_u, put_p, t_u)
            yield from pieces(w_in, IN2["z"], 1024, rhs_u, put_z, t_u)
            yield from branch_gate(0, end2)

        filler = fillers2()
        finish(values2())

        t_sc, t_pv = [None, None], [None, None]
        t_es = []
        lsum = sm[:, 16:28]
        jobs = [(ic, hh) for ic in range(2) for hh in range(6)]
        bank_set[0] = list(range(6))

        def scores(n):
            ic, hh = jobs[n]
            sc, i = scs[n % 2], n % 2
            nk = P * (ic + 1)
            t_s = []
            for gs in ((0, 1), (2,)):
                b, bank, free = take()
                for g in gs:
                    hd = 6 * g + hh
                    r0 = 64 * (hd % 2)
                    last = mm(bank[:, (g % 2) * nk:(g % 2) * nk + nk], q[r0:r0 + 64, hd // 2, ic * P:ic * P + P],
                              kk[r0:r0 + 64, hd // 2, 0:nk], True, True, free, t_q[hd // 2], t_k[hd // 2])
                m = len(gs)
                t = tt(view(sc[:, gs[0] * nk:(gs[0] + m) * nk], m, nk), view(bank[:, 0:m * nk], m, nk),
                       toep4[:, gs[0]:gs[0] + m, hh, 256 - nk:256], ALU.add, last, t_toep, t_sc[i])
                bank_free[b] = t
                t_s.append(t)
            mx, lv = sm[:, n:n + 1], sm[:, 16 + n:17 + n]
            t = op("vector", lambda e: e.reduce_max(mx, sc[:, 0:3 * nk], AX), t_s)
            t = ts(mx, mx, -1.0, ALU.mult, None, None, t)
            return act(sc[:, 0:3 * nk], sc[:, 0:3 * nk], ACT.Exp, t, bias=mx, accum=lv)

        def values_of(n, t_e):
            ic, hh = jobs[n]
            sc, pT, i = scs[n % 2], pTs[n % 2], n % 2
            ob = 6 + ic
            nb = 3 * (ic + 1)
            t_p = []
            for j0 in range(0, nb, 4):
                m = min(4, nb - j0)
                b, bank, free = take()
                for j in range(m):
                    last = tp(bank[:, j * P:j * P + P], sc[:, (j0 + j) * P:(j0 + j + 1) * P], ident, free, t_e)
                t = copy(pT[:, j0 * P:(j0 + m) * P], bank[:, 0:m * P], last, t_pv[i])
                bank_free[b] = t
                t_p.append(t)
            t_sc[i] = last
            return t_p

        def weigh(n, t_p):
            ic, hh = jobs[n]
            pT, i = pTs[n % 2], n % 2
            ob = 6 + ic
            nb = 3 * (ic + 1)
            o = banks[ob][:, hh * 64:hh * 64 + 64]
            for j in range(nb):
                g, jc = j // (ic + 1), j % (ic + 1)
                hd = 6 * g + hh
                last = mm(o, pT[:, j * P:j * P + P], vT[:, jc, hd * 64:hd * 64 + 64], j == 0, j == nb - 1,
                          t_p, t_v, bank_free[ob])
            t_pv[i] = last

        t_e = scores(0)
        t_ya = []
        held = None
        for n in range(12):
            nxt = scores(n + 1) if n < 11 else None
            run(filler, 1)
            t_p = values_of(n, t_e)
            t_es.append(t_e)
            if held is not None:
                weigh(n - 1, held)
                if n == 6:
                    ends = [t_pv[1]]
            held = t_p
            t_e = nxt
        weigh(11, held)
        for ic in range(2):
            ob = 6 + ic
            t = recip(lsum[:, 6 * ic:6 * ic + 6], lsum[:, 6 * ic:6 * ic + 6], t_es[6 * ic:6 * ic + 6])
            t = tt(view(ya[:, ic, :], 6, 64), view(banks[ob][:, 0:384], 6, 64),
                   lsum[:, 6 * ic:6 * ic + 6].rearrange("p (a o) -> p a o", o=1).to_broadcast([P, 6, 64]),
                   ALU.mult, t, t_pv)
            bank_free[ob] = t
            t_ya.append(t)
        finish(filler)
        bank_set[0] = list(range(8))
        t_yaF = []
        for tc in range(2):
            b, bank, free = take()
            for j in range(3):
                last = tp(bank[:, j * P:j * P + P], ya[:, tc, j * P:j * P + P], ident, free, t_ya[tc])
            t = copy(yaF[:, :, tc * P:tc * P + P], view(bank[:, 0:384], 3, P), last)
            bank_free[b] = t
            t_yaF.append(t)
        gate_on(0)
        t_m = {}

        def first_branch(m, ps, t):
            t_m[m] = tt(merged[:, m, :], ps, gate_b[0][:, m, :], ALU.mult, t, t_gb[0][m], end2)
            return t_m[m]
        end_a = t_yaF + [last]

        def next_branch(i):
            def evac(m, ps, t):
                g = gate_b[i % 2]
                t1 = tt(g[:, m, :], ps, g[:, m, :], ALU.mult, t, t_gb[i][m])
                t_m[m] = tt(merged[:, m, :], merged[:, m, :], g[:, m, :], ALU.add, t1, t_m[m])
                return t1
            return evac

        top[0] = base2
        over = top[0]
        top[0] = over + 768
        p1, p2 = (buf(8 * 264, (8, 264)) for _ in range(2))
        pd = buf(2048, (8, 256))
        py = p0.rearrange("p a b -> p (a b)")[:, 0:2048].rearrange("p (a b) -> p a b", a=8)
        xb = buf(12 * 259, (12, 259))
        xc = buf(3072, (12, 256))
        t_pad += [fill(x[:, :, 0:8], 0.0, end_a) for x in (p1, p2)]
        t = tt(p1[:, :, 8:264], p0[:, :, 8:264], p0[:, :, 7:263], ALU.add, list(t_p0.values()), t_pad, end_a)
        t = tt(p2[:, 2:8, 8:264], p1[:, 2:8, 8:264], p1[:, 2:8, 6:262], ALU.add, t)
        t = tt(p1[:, 4:8, 8:264], p2[:, 4:8, 8:264], p2[:, 4:8, 4:260], ALU.add, t)
        t = tt(p2[:, 6:8, 8:264], p1[:, 6:8, 8:264], p1[:, 6:8, 0:256], ALU.add, t)
        t_pd = []
        for g in range(4):
            src = (p1, p2)[g % 2]
            o = pd[:, 2 * g:2 * g + 2, :]
            ti = tt(o, src[:, 2 * g:2 * g + 2, 8:264], invcnt[:, g:g + 1, :].to_broadcast([P, 2, 256]), ALU.mult, t)
            t_pd.append(tt(o, o, p0[:, 2 * g:2 * g + 2, 8:264], ALU.subtract, ti))
        t_xp = fill(xb[:, :, 0:3], 0.0, end_a)
        t_xb = {}

        def put_x(m, ps, t):
            t_xb[m] = act(xb[:, m, 3:259], ps, ACT.Copy, t, end_a)
            return t_xb[m]
        project_cols(w_in, IN2["xbc"], 1536, rhs_u, put_x, t_u)
        slot, landed, s = wrows(T["w_a_2"][0], 0, 3)
        for last in project(lambda m, k: (slot[:, k, m * P:m * P + P], landed), 3, lambda k: yaF[:, k, :],
                            list(range(8)), first_branch, t_yaF):
            ring_free[s] = last
        t_wa = last
        slot, landed, s = load(T["pool_w_2"][0].rearrange("g (t p) n -> p (g t) n", p=P), 8, 256)
        t_py = []
        for g in range(4):
            b, bank, free = take()
            for j in range(2):
                for k in range(2):
                    last = mm(bank[:, j * 256:j * 256 + 256], slot[:, 2 * g + k, j * P:j * P + P], pd[:, 2 * g + k, :],
                              k == 0, k == 1, free, landed, t_pd[g])
            for j in range(2):
                t = act(py[:, 2 * g + j, :], bank[:, j * 256:j * 256 + 256], ACT.Copy, last, t_pd,
                        scale=col("pool_scale_2", 2 * g + j))
            bank_free[b] = t
            t_py.append(t)
        ring_free[s] = last
        end_p = [last, t_wa] + t_py

        t_xc = []
        for m0 in range(0, 12, 4):
            tl = [ts(xc[:, m, :], xb[:, m, 0:256], col("ssd_conv_w_2", 4 * m), ALU.mult, col("ssd_conv_b_2", m), ALU.add,
                     t_xb[m], t_xp, end_a) for m in range(m0, m0 + 4)]
            for j in range(1, 4):
                tl = [stt(xc[:, m, :], xb[:, m, j:j + 256], col("ssd_conv_w_2", 4 * m + j), xc[:, m, :], ALU.mult, ALU.add,
                          tl[m - m0]) for m in range(m0, m0 + 4)]
            t_xc.append(act(xc[:, m0:m0 + 4, :], xc[:, m0:m0 + 4, :], ACT.Silu, tl))
        t_zs = [act(zs[:, 4 * g:4 * g + 4, :], zs[:, 4 * g:4 * g + 4, :], ACT.Silu, [t_z[m] for m in range(4 * g, 4 * g + 4)])
                for g in range(2)]
        t_pc = list(t_m.values())

        top[0] = over
        xT2 = buf(2048, (2, 1024))
        xd = buf(1024)
        BT = buf(256)
        S0 = buf(1024)
        ys = xb.rearrange("p a b -> p (a b)")[:, 0:2048].rearrange("p (a b) -> p a b", a=8)
        cbm = buf(256, (2, 128))
        dtt = buf(192)
        Lbs = [buf(512) for _ in range(2)]
        Cds = [buf(512) for _ in range(2)]
        assert top[0] <= over + 768 + 2 * 2112 + 2048
        dx, dl, da, dcs, dd = (dtt[:, 32 * i:32 * i + 32] for i in range(5))
        an = dtt[:, 160:176]
        b, bank, free = take()
        for tc in range(2):
            for k in range(KT):
                last = mm(bank[:, 16 * tc:16 * tc + 16], u[:, k, tc * P:tc * P + P], wdt[:, k, :], k == 0, k == KT - 1,
                          free, t_cols, t_u)
        t = tt(view(dx, 2, 16), view(bank[:, 0:32], 2, 16),
               col("dt_bias", 0, 16).rearrange("p (o n) -> p o n", o=1).to_broadcast([P, 2, 16]), ALU.add, last, end_p)
        bank_free[b] = t
        t1 = act(dl, dx, ACT.Abs, t)
        t1 = act(dl, dl, ACT.Exp, t1, scale=-1.0)
        t1 = act(dl, dl, ACT.Ln, t1, bias=1.0)
        t_dt = stt(dx, dx, 0.0, dl, ALU.max, ALU.add, t1)
        t_an = act(an, col("a_log", 0, 16), ACT.Exp, t_cols, end_p)
        t_da = stt(view(da, 2, 16), view(dx, 2, 16), -1.0,
                   an.rearrange("p (o n) -> p o n", o=1).to_broadcast([P, 2, 16]), ALU.mult, ALU.mult, t_dt, t_an)
        finish(branch_gate(1))
        gate_on(1)
        b, bank, free = take()
        last = mm(bank[:, 0:32], u128, da, True, True, free, t_da)
        last = mm(bank[:, 32:48], ones, da[:, 0:16], True, True)
        t_cs = copy(dcs, bank[:, 0:32], last)
        t = tt(dd[:, 0:16], bank[:, 32:48], dcs[:, 0:16], ALU.subtract, t_cs)
        bank_free[b] = t
        t_dd = act(dd[:, 0:16], dd[:, 0:16], ACT.Exp, t)

        t_xT = []
        for tc in range(2):
            for g in range(2):
                b, bank, free = take()
                for j in range(4):
                    m = 4 * g + j
                    last = tp(bank[:, j * P:j * P + P], xc[:, m, tc * P:tc * P + P], ident, free, t_xc[g])
                t = tt(view(xT2[:, tc, 512 * g:512 * g + 512], 8, 64), view(bank[:, :], 8, 64),
                       dx[:, 16 * tc + 8 * g:16 * tc + 8 * g + 8].rearrange("p (a o) -> p a o", o=1)
                       .to_broadcast([P, 8, 64]), ALU.mult, last, t_dt, end_p)
                bank_free[b] = t
                t_xT.append(t)
        t_xd = tt(view(xd, 16, 64), view(xT2[:, 0, :], 16, 64),
                  dd[:, 0:16].rearrange("p (a o) -> p a o", o=1).to_broadcast([P, 16, 64]), ALU.mult, t_xT, t_dd, end_p)
        b, bank, free = take()
        for g in range(2):
            last = tp(bank[:, g * P:g * P + P], xc[:, 8 + g, 0:P], ident, free, t_xc[2])
        t_BT = copy(BT, bank[:, 0:256], last, end_p)
        bank_free[b] = t_BT

        def fillers3():
            yield from pieces(T["w_b_2"][0], 0, 1024, lambda k: py[:, k, :], next_branch(1), t_py)
            yield from branch_gate(2, t_pc)

        filler = fillers3()
        run(filler, 1)
        t_S0 = []
        for g in range(2):
            b, bank, free = take()
            last = mm(bank[:, :], BT[:, g * P:g * P + P], xd[:, 512 * g:512 * g + 512], True, True, free, t_BT, t_xd)
            t = act(S0[:, 512 * g:512 * g + 512], bank[:, :], ACT.Copy, last, end_p)
            bank_free[b] = t
            t_S0.append(t)

        t_ys = []
        t_yy = [None, None]
        t_cbu = []
        nn = 0
        for tc in range(2):
            b, bank, free = take()
            for g in range(2):
                last = mm(bank[:, g * P:g * P + P], xc[:, 8 + g, tc * P:tc * P + P], xc[:, 10 + g, tc * P:tc * P + P],
                          True, True, free, t_xc[2])
            t_cb = tt(cbm, view(bank[:, 0:256], 2, P), u128.rearrange("p (o n) -> p o n", o=1).to_broadcast([P, 2, P]),
                      ALU.mult, last, t_cbu, end_p)
            bank_free[b] = t_cb
            for g in range(2):
                for hq in range(2):
                    h0 = 8 * g + 4 * hq
                    i = nn % 2
                    nn += 1
                    Lb, Cd = Lbs[i], Cds[i]
                    b, bank, free = take()
                    for j in range(4):
                        last = mm(bank[:, j * P:j * P + P],
                                  da[:, 16 * tc + h0 + j:16 * tc + h0 + j + 1].to_broadcast([P, P]), u128, True, True,
                                  free, t_da)
                    run(filler, 1)
                    for j in range(4):
                        t = ts(Lb[:, j * P:j * P + P], bank[:, j * P:j * P + P],
                               dcs[:, 16 * tc + h0 + j:16 * tc + h0 + j + 1], ALU.subtract, 0.0, ALU.min,
                               last, t_cs, t_yy[i], end_p)
                    t_L = act(Lb, Lb, ACT.Exp, t)
                    if tc:
                        t = act(Cd, bank[:, :], ACT.Exp, t, t_yy[i], end_p)
                    bank_free[b] = t
                    t_L = tt(view(Lb, 4, P), view(Lb, 4, P), cbm[:, g:g + 1, :].to_broadcast([P, 4, P]), ALU.mult, t_L, t_cb)
                    t_cbu = [t_L]
                    t_C = tt(view(Cd, 4, P), view(Cd, 4, P),
                             xc[:, 10 + g:11 + g, tc * P:tc * P + P].to_broadcast([P, 4, P]), ALU.mult, t, t_xc) if tc else None
                    b, bank, free = take()
                    for j in range(4):
                        o = bank[64 * (j % 2):64 * (j % 2) + 64, (j // 2) * P:(j // 2) * P + P]
                        hd = h0 + j
                        last = mm(o, xT2[:, tc, hd * 64:hd * 64 + 64], Lb[:, j * P:j * P + P], True, not tc,
                                  free, t_L, t_xT, skip=True)
                        if tc:
                            last = mm(o, S0[:, hd * 64:hd * 64 + 64], Cd[:, j * P:j * P + P], False, True, t_C, t_S0, skip=True)
                    t_yy[i] = last
                    for j in range(2):
                        m = h0 // 2 + j
                        t = stt(ys[:, m, tc * P:tc * P + P], xc[:, m, tc * P:tc * P + P], col("ssd_d_2", m),
                                bank[:, j * P:j * P + P], ALU.mult, ALU.add, last, t_xc, end_p)
                    bank_free[b] = t
                    t_ys.append(t)
        t_yq = []
        t_yz = []
        for g in range(2):
            t = tt(ys[:, 4 * g:4 * g + 4, :], ys[:, 4 * g:4 * g + 4, :], zs[:, 4 * g:4 * g + 4, :], ALU.mult, t_ys, t_zs)
            t_yz.append(t)
            t_yq.append(act(sq[:, 4 * g:4 * g + 4, :], ys[:, 4 * g:4 * g + 4, :], ACT.Square, t, t_u))
        t_yn = []
        finish(filler)
        for g in range(2):
            b, bank, free = take()
            for j in range(4):
                last = mm(bank[:, 0:256], ones, sq[:, 4 * g + j, :], j == 0, j == 3, free, t_yq[g])
            rr = Lbs[g][:, 0:256]
            t = act(rr, bank[:, 0:256], ACT.Sqrt, last, t_yy, bias=eps, scale=1.0 / 512)
            bank_free[b] = t
            t = recip(rr, rr, t)
            for j in range(4):
                m = 4 * g + j
                t_yn.append(stt(ys[:, m, :], ys[:, m, :], col("ssd_norm_w_2", m), rr, ALU.mult, ALU.mult, t, t_yq[g]))
        gate_on(2)
        project_cols(T["w_c_2"][0], 0, 1024, lambda k: ys[:, k, :], next_branch(2), t_yn)
        end_c = list(t_m.values())

        t_h1 = {}

        def add_x(m, ps, t):
            t_h1[m] = tt(h[:, m, :], ps, h[:, m, :], ALU.add, t)
            return t_h1[m]
        project_cols(T["w_o_2"][0], 0, 1024, lambda k: merged[:, k, :], add_x, end_c)
        t_h = list(t_h1.values())

        t_u = norm(h, t_h, t_yn, lambda k: col("ln2_g_2", k), None, u, t_cols)
        top[0] = base2
        hid = buf(22 * 256, (22, 256))
        NP_ = 4
        pads = [buf(2 * 258, (2, 258)) for _ in range(NP_)]
        cv = [buf(512, (2, 256)) for _ in range(NP_)]
        t_pad = [fill(x[:, :, 0:2], 0.0, end_c) for x in pads]
        pad_free = [None] * NP_
        cv_free = [None] * NP_
        t_hid = {}
        nn = 0
        up = T["ffn_w_up_2"][0]
        order = []
        for c in range(11):
            slot, landed, s = wcols(up, 512 * c, 512)
            for j0 in range(2):
                ms = [4 * c + 2 * j0, 4 * c + 2 * j0 + 1]
                b, bank, free = take()
                for j in range(2):
                    for k in range(KT):
                        last = mm(bank[:, j * 256:j * 256 + 256], slot[:, k, (2 * j0 + j) * P:(2 * j0 + j + 1) * P],
                                  u[:, k, :], k == 0, k == KT - 1, free, landed, t_u)
                i = nn % NP_
                nn += 1
                pd_, cv_ = pads[i], cv[i]
                t = act(pd_[:, :, 2:258], view(bank[:, :], 2, 256), ACT.Copy, last, t_pad[i], pad_free[i], end_c)
                bank_free[b] = t
                tl = [ts(cv_[:, j, :], pd_[:, j, 0:256], col("ffn_conv_w_2", 3 * ms[j]), ALU.mult,
                         col("ffn_conv_b_2", ms[j]), ALU.add, t, cv_free[i], end_c) for j in range(2)]
                for tap in range(1, 3):
                    tl = [stt(cv_[:, j, :], pd_[:, j, tap:tap + 256], col("ffn_conv_w_2", 3 * ms[j] + tap), cv_[:, j, :],
                              ALU.mult, ALU.add, tl[j]) for j in range(2)]
                pad_free[i] = tl
                if ms[0] < 22:
                    t = act(hid[:, ms[0]:ms[0] + 2, :], cv_, ACT.Silu, tl, end_c)
                else:
                    o = hid[:, ms[0] - 22:ms[0] - 20, :]
                    t = tt(o, o, cv_, ALU.mult, tl, t_hid[ms[0] - 22])
                cv_free[i] = t
                for m in ms:
                    t_hid[m % 22] = t
            ring_free[s] = last
        down = T["ffn_w_down_2"][0]
        abanks = [take() for _ in range(4)]
        for t0 in range(0, 22, 4):
            t1 = min(t0 + 4, 22)
            slot, landed, s = wrows(down, t0, t1)
            for m in range(8):
                o = abanks[m // 2][1][:, (m % 2) * 256:(m % 2) * 256 + 256]
                for k in range(t0, t1):
                    last = mm(o, slot[:, k - t0, m * P:m * P + P], hid[:, k, :], k == 0 and m % 2 == 0, k == 21,
                              landed, t_hid[k], abanks[m // 2][2], skip=True)
            ring_free[s] = last
        t_h = []
        for m in range(8):
            o = abanks[m // 2][1][:, (m % 2) * 256:(m % 2) * 256 + 256]
            t = tt(h[:, m, :], o, h[:, m, :], ALU.add, last)
            t_h.append(t)
            bank_free[abanks[m // 2][0]] = t

        t_u = norm(h, t_h, None, lambda k: col("final_g_2", k), None, u, last, t_cols)
        outs = []
        for tc in range(2):
            for g in range(2):
                b, bank, free = take()
                for j in range(4):
                    last = tp(bank[:, j * P:j * P + P], u[:, 4 * g + j, tc * P:tc * P + P], ident, free, t_u)
                o = xT[:, tc, 512 * g:512 * g + 512]
                t = copy(o, bank[:, :], last)
                bank_free[b] = t
                outs.append(dma(out[0, tc * P:tc * P + P, 512 * g:512 * g + 512], o, t))
        op("sync", None, outs, t_rep_out)

        def key_of(w):
            return (w.key, w.at) if isinstance(w, Tok) else (w.sem, w.value)

        def needed(eng):
            seen, outer = {}, None
            for fn, waits, tok, sem in queue[eng]:
                best = {}
                for w in waits:
                    key, val = key_of(w)
                    if seen.get(key, -1) < val:
                        seen[key] = val
                        best[key] = w
                yield fn, list(best.values()), tok, sem
                if isinstance(fn, tuple):
                    if fn[0] == "if":
                        outer = dict(seen)
                    else:
                        seen = outer

        plan = {e: list(needed(e)) for e in engines}
        for e in engines:
            for _, waits, _, _ in plan[e]:
                for w in waits:
                    if isinstance(w, Tok):
                        w.used = True
        for e in engines:
            n = [0, 0]
            for _, _, tok, _ in plan[e]:
                n[tok.region] += tok.used
                tok.count = n[tok.region]

        block = ctx.enter_context(nc.Block())

        def emit(eng, e):
            guard = None
            for fn, waits, tok, sem in plan[eng]:
                for w in waits:
                    if isinstance(w, Tok):
                        e.wait_ge(done[w.key], w.count)
                    else:
                        e.wait_ge(w.sem, w.value)
                if fn is None:
                    continue
                if isinstance(fn, tuple):
                    if fn[0] == "if":
                        reg = e.alloc_register()
                        e.reg_load(reg, fn[1])
                        guard = e.If_ne(reg, 0)
                        guard.__enter__()
                    else:
                        guard.__exit__(None, None, None)
                    continue
                ins = fn(e)
                if sem is not None:
                    ins.then_inc(sem, 16)
                elif tok.used:
                    ins.then_inc(done[tok.key], 1)

        @block.sync
        def _(e):
            emit("sync", e)

        @block.gpsimd
        def _(e):
            emit("gpsimd", e)

        @block.scalar
        def _(e):
            emit("scalar", e)

        @block.vector
        def _(e):
            emit("vector", e)

        @block.tensor
        def _(e):
            emit("tensor", e)


DIRECT = ["x", "w_ada", "w_in", "w_conv_pw", "w_gla_o", "w_out", "w1", "w3", "w2", "w_ada_f", "w_in_2", "w_a_2", "pool_w_2", "w_b_2", "w_c_2", "w_o_2",
          "ffn_w_up_2", "ffn_w_down_2"]


def lay_columns(inputs):
    def fcol(v):
        return v.reshape(-1, P).T

    def taps(v):
        return v.reshape(v.shape[0], -1, P).transpose(2, 1, 0).reshape(P, -1)

    def pad(v):
        return np.concatenate([v, np.zeros((P - v.shape[0], v.shape[1]), np.float32)])

    def tiles(v):
        return v.reshape(-1, P, v.shape[1]).transpose(1, 0, 2).reshape(P, -1)

    def rows(v):
        return np.broadcast_to(v.reshape(1, -1), (P, v.size))

    a = {k: np.asarray(v) for k, v in inputs.items()}
    parts = {
        "w_dw": taps(a["w_dw"][0]), "ssd_conv_w_2": taps(a["ssd_conv_w_2"][0]),
        "ffn_conv_w_2": taps(a["ffn_conv_w_2"][0]),
        "ssd_d_2": fcol(np.repeat(a["ssd_d_2"][0], 64)),
        "router_b": rows(np.concatenate([a["b_router_g"][0], a["b_router_e"][0]])),
        "dt_bias": rows(a["ssd_dt_bias_2"][0]), "a_log": rows(a["ssd_a_log_2"][0]),
        "eps": np.full((P, 1), 1e-6, np.float32),
        "rtab": pad(np.concatenate([a["rel_bias_2"], np.ones((1, 18), np.float32)])),
        "w_a2": pad(np.concatenate([a["w_a2"][0], a["b_a2"]])),
        "w_a1": tiles(a["w_in"][0][:, IN1["a1"]:IN1["a1"] + 16]),
        "w_dt": tiles(a["w_in_2"][0][:, IN2["dt"]:IN2["dt"] + 16]),
        "w_r": tiles(np.concatenate([a["w_router_g"][0], a["w_router_e"][0]], 1)),
    }
    out = []
    for name, n in COLS:
        v = parts[name] if name in parts else fcol(a[name])
        assert v.shape == (P, n), (name, v.shape)
        out.append(v)
    return np.ascontiguousarray(np.concatenate(out, 1).astype(np.float32, copy=False))


def kernel(**inputs):
    import concourse.bacc as bacc
    from concourse.bass_utils import run_bass_kernel_spmd as run

    nc = bacc.Bacc("TRN2", target_bir_lowering=False, num_devices=1)
    arrays = {n: np.ascontiguousarray(np.asarray(inputs[n])) for n in DIRECT}
    arrays["cols"] = lay_columns(inputs)
    arrays["consts"] = constants()
    T, feed = {}, {}
    for n, a in arrays.items():
        feed["in_" + n] = a
        T[n] = nc.dram_tensor("in_" + n, a.shape, F32, kind="ExternalInput").ap()
    out = nc.dram_tensor("out_0", (1, S, D), F32, kind="ExternalOutput").ap()
    scratch = nc.dram_tensor("scratch", (P * 18 * 384,), F32, kind="Internal").ap()
    build(nc, T, out, scratch)
    res = run(nc, [feed], core_ids=[0])
    return res.results[0]["out_0"]
```

```python
from contextlib import ExitStack

import concourse.bass as bass
from concourse import mybir
import numpy as np

F32 = mybir.dt.float32
F32R = mybir.dt.float32r
U32 = mybir.dt.uint32
ALU = mybir.AluOpType
ACT = mybir.ActivationFunctionType
AX = mybir.AxisListType.X

P = 128
S = 256
D = 1024
KT = D // P
NE = 32
NS = 3
SLOT = 2048
NU = 4
UNIT = 1024
WIDE = 4096
LEVELS = (32, 16, 8, 4, 2, 1)
WINDOWS = (2, 4, 8, 16)

IN1 = dict(a=0, gt=512, q=1024, k=1536, v=2048, r=3072, a1=4096, gates=4112)
IN2 = dict(q=0, k=1152, v=2304, pool=3456, z=4480, xbc=5504, dt=7040, gates=7056)

COLS = [("g_norm1", 8), ("g_norm2", 8), ("g_final", 8), ("c", 8), ("b_ada", 48), ("b_ada_f", 16),
        ("w_dw", 124), ("b_dw", 4), ("g_conv_ln", 4), ("b_conv_ln", 4), ("b_conv_pw", 8), ("g_gla_norm", 8),
        ("ln1_g_2", 8), ("b_gate_2", 24), ("pool_scale_2", 8), ("ssd_conv_w_2", 48), ("ssd_conv_b_2", 12),
        ("ssd_d_2", 8), ("ssd_norm_w_2", 8), ("ln2_g_2", 8), ("ffn_conv_w_2", 132), ("ffn_conv_b_2", 44),
        ("final_g_2", 8), ("router_b", 36), ("dt_bias", 16), ("a_log", 16), ("eps", 1), ("rtab", 18), ("w_a2", 512),
        ("w_a1", 128), ("w_dt", 128), ("w_r", 288)]
CONSTS = [("ident", 128), ("ones", 128), ("u128", 128), ("before", 128), ("invcnt", 4 * 256), ("iota", 64)]
CONSTS1 = [("u64", 128), ("masks", 7 * 128), ("oh", 3 * 384)]
CAP = 64


def spans(table):
    at, out = 0, {}
    for name, n in table:
        out[name] = (at, n)
        at += n
    return out, at


COL_AT, NCOLS = spans(COLS)
CONST_AT, NCONST = spans(CONSTS + CONSTS1)
NCONST0 = spans(CONSTS)[1]
NCONST1 = spans(CONSTS1[:2])[1]


def constants():
    c = np.zeros((P, NCONST), np.float32)

    def put(name, v):
        at, n = CONST_AT[name]
        c[:v.shape[0], at:at + n] = v

    i = np.arange(P)
    put("ident", np.eye(P))
    put("ones", np.ones((P, P)))
    le = i[:, None] <= i[None, :]
    same = i[:, None] // 64 == i[None, :] // 64
    put("u64", (le & same) / 16.0)
    put("u128", le * 1.0)
    ms = []
    for m in LEVELS:
        blk = i[:, None] // (2 * m) == i[None, :] // (2 * m)
        ms.append(blk & (i[:, None] % (2 * m) < m) & (i[None, :] % (2 * m) >= m))
    ms.append(i[:, None] == i[None, :])
    put("masks", np.concatenate(ms, 1) * 1.0)
    t = np.arange(S) + 1
    put("invcnt", np.broadcast_to(np.concatenate([1.0 / np.minimum(t, w) for w in WINDOWS]), (P, 4 * S)))
    dist = 255 - np.arange(384)
    nf = np.maximum(dist, 1).astype(np.float32)
    large = 16 + (np.log(nf / np.float32(16)) / np.float32(np.log(2048 / 16)) * np.float32(16)).astype(np.int32)
    bucket = np.where(dist < 16, np.maximum(dist, 0), np.minimum(large, 31))
    oh = np.zeros((33, 3, 384))
    for g, (w, dil) in enumerate(((128, 1), (512, 4), (2048, 16))):
        ok = (dist >= 0) & (dist <= w) & (dist % dil == 0)
        oh[bucket[ok], g, np.arange(384)[ok]] = 1.0
        oh[32, g, ~ok] = -1e30
    put("oh", oh.reshape(33, -1))
    put("before", (i[:, None] < i[None, :]) * 1.0)
    put("iota", np.broadcast_to(np.arange(64), (P, 64)))
    return c


class Tok:

    def __init__(self, eng, at, region):
        self.eng, self.at, self.region, self.used = eng, at, region, False
        self.key = (eng, region)


class Landed:
    def __init__(self, sem, value):
        self.sem, self.value = sem, value


def build(nc, T, out, scratch, dbg=None):
    ctx = ExitStack()
    engines = ("tensor", "vector", "scalar", "gpsimd", "sync")
    queue = {e: [] for e in engines}

    def flat(ws):
        for w in ws:
            if isinstance(w, (list, tuple)):
                yield from flat(w)
            elif w is not None:
                yield w

    def op(eng, fn, *waits, sem=None):
        tok = Tok(eng, len(queue[eng]), region[0])
        queue[eng].append((fn, list(flat(waits)), tok, sem))
        return tok

    region = [0]
    opened = []

    def begin(t_flag, flag):
        for e in ("tensor", "vector", "scalar", "sync"):
            opened.append(op(e, ("if", flag), t_flag))
        region[0] = 1

    def end():
        lasts = [queue[e][-1][2] for e in ("tensor", "vector", "scalar", "sync")]
        landed = {}
        for fn, _, tok, sem in queue["sync"]:
            if tok.region and sem is not None:
                landed[sem] = landed.get(sem, 0) + 16
        for e in ("tensor", "vector", "scalar", "sync"):
            op(e, None, [t for t in lasts if t.eng != "sync"], [Landed(s, n) for s, n in landed.items()])
        region[0] = 0
        for e in ("tensor", "vector", "scalar", "sync"):
            op(e, ("end",))

    with ctx:
        sem_n = [0]

        def new_sem(name):
            sem_n[0] += 1
            return ctx.enter_context(nc.semaphore(f"{name}{sem_n[0]}"))

        ARENA = 40870
        FINE = 12288
        arena = ctx.enter_context(nc.sbuf_tensor("arena", [P, ARENA], F32))
        phase = [ExitStack()]

        def upper(name, dtype):
            phase[0].close()
            phase[0] = ExitStack()
            return phase[0].enter_context(nc.sbuf_tensor(name, [P, FINE], dtype))
        banks = [ctx.enter_context(nc.psum_tensor(f"bank{i}", [P, 512], F32)) for i in range(8)]
        idxb = ctx.enter_context(nc.sbuf_tensor("idxb", [P, 17], U32))
        ctx.callback(lambda: phase[0].close())
        done = {(e, g): new_sem("done_" + e) for e in engines for g in range(2)}

        top = [0]

        def buf(n, shape=None, at=None):
            if at is None:
                at = top[0]
                top[0] += n
            assert at + n <= ARENA, (at, n)
            v = arena[:, at:at + n]
            if shape is not None:
                names = "abcd"[:len(shape)]
                v = v.rearrange(f"p ({' '.join(names)}) -> p {' '.join(names)}", **dict(zip(names, shape)))
            return v

        def view(ap, *shape):
            names = "abcd"[:len(shape)]
            return ap.rearrange(f"p ({' '.join(names)}) -> p {' '.join(names)}", **dict(zip(names, shape)))

        def mm(o, l, r, start, stop, *w, skip=False):
            return op("tensor", lambda e: e.matmul(o, l, r, start=start, stop=stop, skip_group_check=skip), *w)

        def tp(o, i, idn, *w):
            return op("tensor", lambda e: e.transpose(o, i, idn), *w)

        def act(o, i, f, *w, bias=0.0, scale=1.0, accum=None):
            if accum is not None:
                return op("scalar", lambda e: e.activation(o, i, f, bias=bias, scale=scale, accum_out=accum), *w)
            return op("scalar", lambda e: e.activation(o, i, f, bias=bias, scale=scale), *w)

        def tt(o, a, b, f, *w, eng="vector"):
            return op(eng, lambda e: e.tensor_tensor(o, a, b, f), *w)

        def ts(o, a, s1, f1, s2, f2, *w, eng="vector"):
            if f2 is None:
                return op(eng, lambda e: e.tensor_scalar(o, a, s1, None, f1), *w)
            return op(eng, lambda e: e.tensor_scalar(o, a, s1, s2, f1, f2), *w)

        def stt(o, a, s, b, f1, f2, *w):
            return op("vector", lambda e: e.scalar_tensor_tensor(out=o, in0=a, scalar=s, in1=b, op0=f1, op1=f2), *w)

        def copy(o, i, *w, eng="vector"):
            return op(eng, lambda e: e.tensor_copy(o, i), *w)

        def recip(o, i, *w):
            return op("vector", lambda e: e.reciprocal(o, i), *w)

        def fill(o, v, *w, eng="gpsimd"):
            return op(eng, lambda e: e.memset(o, v), *w)

        def dma(o, i, *w, eng="sync"):
            s = new_sem("d")
            op(eng, lambda e: e.dma_start(o, i), *w, sem=s)
            return Landed(s, 16)

        def run(gen, n):
            for _ in range(n):
                next(gen, None)

        def finish(gen):
            for _ in gen:
                pass

        ring = [buf(SLOT) for _ in range(NS)]
        ring_sem = [new_sem("ring") for _ in range(NS)]
        ring_free = [None] * NS
        ring_n = [0]
        ring_use = [0] * NS

        def load(src, kt, n):
            s = ring_n[0] % NS
            ring_n[0] += 1
            dst = view(ring[s][:, 0:kt * n], kt, n)
            op("sync", lambda e: e.dma_start(dst, src), ring_free[s], sem=ring_sem[s])
            ring_use[s] += 1
            return dst, Landed(ring_sem[s], 16 * ring_use[s]), s

        def wcols(w, c0, n):
            return load(w[:, c0:c0 + n].rearrange("(t p) n -> p t n", p=P), w.shape[0] // P, n)

        def wrows(w, t0, t1):
            return load(w[t0 * P:t1 * P, :].rearrange("(t p) n -> p t n", p=P), t1 - t0, w.shape[1])

        bank_free = [None] * 8
        bank_set = [list(range(8))]
        bank_n = [0]
        bank_held = set()

        def take():
            while True:
                b = bank_set[0][bank_n[0] % len(bank_set[0])]
                bank_n[0] += 1
                if b not in bank_held:
                    break
            return b, banks[b], bank_free[b]

        xbase = top[0]
        xT = buf(2048, (2, 1024))
        t_x = dma(xT, T["x"].rearrange("o (t p) d -> p (o t) d", p=P))
        consts = buf(NCONST0)
        t_consts = dma(consts, T["consts"][:, 0:NCONST0])
        cols = buf(NCOLS)
        t_cols = dma(cols, T["cols"])

        def col(name, i=0, n=1):
            at = COL_AT[name][0] + i
            return cols[:, at:at + n]

        consts1 = None

        def const(name):
            at, n = CONST_AT[name]
            return consts[:, at:at + n] if at < NCONST0 else consts1[:, at - NCONST0:at - NCONST0 + n]

        ident, ones, u128, before = (const(n) for n in ("ident", "ones", "u128", "before"))
        invcnt = view(const("invcnt"), 4, 256)
        iota = const("iota")
        eps = col("eps")

        rtab, wa2 = col("rtab", 0, 18), col("w_a2", 0, 512)
        wr = view(col("w_r", 0, 288), 8, 36)
        wa1 = view(col("w_a1", 0, 128), 8, 16)
        wdt = view(col("w_dt", 0, 128), 8, 16)
        t_rtab1 = t_rtab2 = t_wa2 = t_ba2 = t_wr1 = t_wr2 = t_wa1 = t_wdt = t_cols

        h = buf(2048, (8, 256))
        u = buf(2048, (8, 256))
        mod = buf(64)
        am = buf(24)
        cact = buf(8)
        rstd = buf(256)
        aacc_at = top[0]
        aacc = buf(1024, (2, 512))
        base = top[0]
        sq = view(xT.rearrange("p a b -> p (a b)"), 8, 256)

        def project(wget, kts, rhs, m_list, evac, *deps):
            last = None
            for j0 in range(0, len(m_list), 2):
                pair = m_list[j0:j0 + 2]
                b, bank, free = take()
                for j, m in enumerate(pair):
                    for k in range(kts):
                        w, wt = wget(m, k)
                        last = mm(bank[:, j * 256:j * 256 + 256], w, rhs(k), k == 0, k == kts - 1, free, wt, deps)
                bank_free[b] = [evac(m, bank[:, j * 256:j * 256 + 256], last) for j, m in enumerate(pair)]
                yield last

        def pieces(w, c0, n, rhs, evac, *deps, chunk=256):
            m0 = 0
            for c in range(0, n, chunk):
                k = min(chunk, n - c)
                slot, landed, s = wcols(w, c0 + c, k)
                for last in project(lambda m, kt, slot=slot, m0=m0: (slot[:, kt, (m - m0) * P:(m - m0) * P + P], landed),
                                    w.shape[0] // P, rhs, list(range(m0, m0 + k // P)), evac, *deps):
                    ring_free[s] = last
                    yield
                m0 += k // P

        def project_cols(*a, **k):
            finish(pieces(*a, **k))

        xs_tok, xs_free = [None] * KT, [None, None]
        w_free, w_n = [None] * NU, [0]
        pending = []
        fine = {}

        def fine_memory(name):
            f = upper(name, F32R)
            fine["xh"], fine["xl"] = (view(f[:, 2048 * i:2048 * i + 2048], 8, 256) for i in range(2))
            fine["w"] = [[f[:, 4096 + UNIT * (2 * i + j):4096 + UNIT * (2 * i + j) + UNIT] for j in range(2)] for i in range(NU)]

        def split(hi, lo, src, low, *w):
            t = act(hi, src, ACT.Copy, *w)
            return [t, tt(lo, src, hi.bitcast(F32), ALU.subtract, t, eng=low)]

        def split_x(src, toks, groups=(0, 1), low="vector"):
            for g in groups:
                at = slice(4 * g, 4 * g + 4)
                t = split(fine["xh"][:, at, :], fine["xl"][:, at, :], src[:, at, :], low, toks[at], xs_free[g])
                xs_tok[at] = [t] * 4

        def split_w(slot, k0, kn, n, landed, low):
            i = w_n[0] % NU
            w_n[0] += 1
            hi, lo = (x[:, 0:kn * n] for x in fine["w"][i])
            t = split(hi, lo, slot[:, k0:k0 + kn, :].rearrange("p a b -> p (a b)"), low, landed, w_free[i])
            return view(hi, kn, n), view(lo, kn, n), t, i

        def flush(left=0):
            while len(pending) > left:
                pending.pop(0)()

        def defer(f):
            pending.append(f)
            flush(NU - 1)

        def mm3(o, wh, wl, at, k, tok, first, final, free, rows=None):
            xh, xl = fine["xh"], fine["xl"]
            last = None
            for i, (w, x) in enumerate(((wh, xh), (wh, xl), (wl, xh))):
                l, r = (w[at], x[:, k, :]) if rows is None else (x[:, k, rows], w[at])
                last = mm(o, l, r, first and i == 0, final and i == 2, free, tok, xs_tok[k], skip=True)
            return last

        def pieces3(w, c0, n, evac, low=("vector",), pair=None):
            for ci, c in enumerate(range(0, n, 256)):
                width = min(256, n - c)
                slot, landed, s = wcols(w, c0 + c, width)
                bank_of = {}
                ts_ = []
                for k0 in range(0, KT, 4):
                    wh, wl, tok, wi = split_w(slot, k0, 4, width, landed, low[ci % len(low)])
                    ts_.append(tok)

                    def products(k0=k0, m0=c // P, nm=width // P, wh=wh, wl=wl, tok=tok, wi=wi, bank_of=bank_of):
                        if k0 == 0:
                            bank_of[0] = take()
                            bank_held.add(bank_of[0][0])
                        b, bank, free = bank_of[0]
                        for j in range(nm):
                            for k in range(4):
                                last = mm3(bank[:, j * 256:j * 256 + 256], wh, wl,
                                           (slice(None), k, slice(j * P, j * P + P)), k0 + k,
                                           tok, k0 + k + j == 0, k0 + k == KT - 1, free)
                        w_free[wi] = xs_free[k0 // 4] = last
                        if k0:
                            bank_held.discard(b)
                        if k0 and pair is not None:
                            bank_free[b] = pair(m0, view(bank[:, :], 2, 256), last)
                        elif k0:
                            bank_free[b] = [evac(m0 + j, bank[:, j * 256:j * 256 + 256], last) for j in range(nm)]
                    defer(products)
                ring_free[s] = ts_
                yield

        def rows3(w, c0, n, evac, low=("vector",)):
            for ci, c in enumerate(range(0, n, 256)):
                slot, landed, s = wcols(w, c0 + c, 256)
                bank_of = {}
                ts_ = []
                for k0 in range(0, KT, 4):
                    wh, wl, tok, wi = split_w(slot, k0, 4, 256, landed, low[ci % len(low)])
                    ts_.append(tok)

                    def products(k0=k0, c=c, wh=wh, wl=wl, tok=tok, wi=wi, bank_of=bank_of):
                        if k0 == 0:
                            bank_of[0] = take()
                            bank_held.add(bank_of[0][0])
                        b, bank, free = bank_of[0]
                        for tc in range(2):
                            for k in range(4):
                                last = mm3(bank[:, tc * 256:tc * 256 + 256], wh, wl, (slice(None), k, slice(0, 256)),
                                           k0 + k, tok, k0 + k + tc == 0, k0 + k == KT - 1, free,
                                           rows=slice(tc * P, tc * P + P))
                        w_free[wi] = xs_free[k0 // 4] = last
                        if k0:
                            bank_held.discard(b)
                            bank_free[b] = evac(c, view(bank[:, :], 2, 256), last)
                    defer(products)
                ring_free[s] = ts_
                yield

        fine_memory("fine1")

        t_h = []
        for tc in range(2):
            for g in range(2):
                b, bank, free = take()
                for j in range(4):
                    last = tp(bank[:, j * P:j * P + P], xT[:, tc, (4 * g + j) * P:(4 * g + j + 1) * P], ident,
                              free, t_x, t_consts)
                t = copy(h[:, 4 * g:4 * g + 4, tc * P:tc * P + P], view(bank[:, :], 4, P), last)
                bank_free[b] = t
                t_h.append(t)
        t_xfree = last

        t_cact = act(cact, col("c", 0, 8), ACT.Silu, t_cols)
        mod_bank = 7
        bank_set[0] = list(range(7))
        aacc_free = [None, None]
        ada_n = [0]
        ada_last = [None]
        ada_sem = [new_sem("ada") for _ in range(4)]
        ada_use = [0] * 4
        ada_slots = []

        def ada(w, c0, n, m0, on_vector=True):
            landed = {}

            def fetch(c):
                for half in range(2):
                    a, flat_slot, free = ada_slots.pop(0)
                    slot = view(flat_slot, 4, 512)
                    src = w[512 * half:512 * half + 512, c0 + c:c0 + c + 512].rearrange("(t p) n -> p t n", p=P)
                    op("sync", lambda e, slot=slot, src=src: e.dma_start(slot, src), free, sem=ada_sem[a])
                    ada_use[a] += 1
                    landed[c, half] = (a, flat_slot, slot, Landed(ada_sem[a], 16 * ada_use[a]))
            ahead = len(ada_slots) // 2
            for c in range(0, min(n, 512 * ahead), 512):
                fetch(c)
            for c in range(0, n, 512):
                i = ada_n[0] % 2
                ada_n[0] += 1
                o = aacc[:, i, :]
                t = None
                for half in range(2):
                    a, flat_slot, slot, there = landed[c, half]
                    if not on_vector:
                        tm = [act(slot[:, k, :], slot[:, k, :], ACT.Copy, there, t_cact,
                                  scale=cact[:, 4 * half + k:4 * half + k + 1]) for k in range(4)]
                        t1 = tt(slot[:, 0:2, :], slot[:, 0:2, :], slot[:, 2:4, :], ALU.add, tm, eng="gpsimd")
                        if half:
                            t1 = tt(slot[:, 0, :], slot[:, 0, :], slot[:, 1, :], ALU.add, t1, eng="gpsimd")
                            t = tt(o, o, slot[:, 0, :], ALU.add, t, t1, eng="gpsimd")
                        else:
                            t = tt(o, slot[:, 0, :], slot[:, 1, :], ALU.add, t1, aacc_free[i], eng="gpsimd")
                    for k in range(4) if on_vector else ():
                        cc = cact[:, 4 * half + k:4 * half + k + 1]
                        if t is None:
                            t = ts(o, slot[:, k, :], cc, ALU.mult, None, None, there, t_cact, aacc_free[i])
                        else:
                            t = stt(o, slot[:, k, :], cc, o, ALU.mult, ALU.add, t, there)
                    ada_slots.append((a, flat_slot, t))
                yield
                if c + 512 * ahead < n:
                    fetch(c + 512 * ahead)
                for m in range(4):
                    at = m0 + c // P + m
                    last = mm(banks[mod_bank][:, at:at + 1], aacc[:, i, m * P:m * P + P], ones[:, 0:1], True, True,
                              t, bank_free[mod_bank])
                aacc_free[i] = last
            ada_last[0] = last

        def ada_out(m0, n, bias):
            t = tt(mod[:, m0:m0 + n], banks[mod_bank][:, m0:m0 + n], bias, ALU.add, ada_last[0], t_cols)
            bank_free[mod_bank] = t
            return t

        def gain(i, g, sc, t):
            return stt(am[:, 8 * i:8 * i + 8], mod[:, sc:sc + 8], 1.0, col(g, 0, 8), ALU.add, ALU.mult, t)

        def norm_rows(x, t_x, t_sq_free):
            first, second = (t_x[0:4], t_x[4:8]) if len(t_x) == 8 else (t_x, t_x)
            t_sq = [act(sq[:, 0:4, :], x[:, 0:4, :], ACT.Square, first, t_sq_free),
                    tt(sq[:, 4:8, :], x[:, 4:8, :], x[:, 4:8, :], ALU.mult, second, t_sq_free)]
            b, bank, free = take()
            for k in range(KT):
                last = mm(bank[:, 0:256], ones, sq[:, k, :], k == 0, k == KT - 1, free, t_sq[k // 4], t_consts)
            t = act(rstd, bank[:, 0:256], ACT.Sqrt, last, bias=eps, scale=1.0 / D)
            bank_free[b] = t
            return t, last

        def norm_apply(x, t_x, t_rows):
            t, last = t_rows
            t_r = recip(rstd, rstd, t)
            return [tt(sq[:, 4 * g:4 * g + 4, :], x[:, 4 * g:4 * g + 4, :],
                       rstd.rearrange("p (o n) -> p o n", o=1).to_broadcast([P, 4, 256]), ALU.mult, t_x, t_r, last)
                    for g in range(2)]

        def norm_scale(t_n, scale_col, shift_col, o, *t_ab, then_split=False):
            toks = []
            for k in range(KT):
                if k % 2:
                    toks.append(act(o[:, k, :], sq[:, k, :], ACT.Identity, t_n[k // 4], t_ab, scale=scale_col(k),
                                    bias=shift_col(k) if shift_col else 0.0))
                elif shift_col:
                    toks.append(ts(o[:, k, :], sq[:, k, :], scale_col(k), ALU.mult, shift_col(k), ALU.add, t_n[k // 4], t_ab))
                else:
                    toks.append(ts(o[:, k, :], sq[:, k, :], scale_col(k), ALU.mult, None, None, t_n[k // 4], t_ab))
                if then_split and k % 4 == 3:
                    split_x(o, toks + [None] * 4, (k // 4,))
            return toks

        def norm(x, t_x, t_sq_free, scale_col, shift_col, o, *t_ab, then_split=False):
            return norm_scale(norm_apply(x, t_x, norm_rows(x, t_x, t_sq_free)), scale_col, shift_col, o, *t_ab, then_split=then_split)

        rhs_u = lambda k: u[:, k, :]

        consts1 = buf(NCONST1)
        scr = buf(5120)
        zp = buf(4 * 286, (4, 286))
        cacc = buf(1024, (4, 256))
        sig = buf(1024, (4, 256))
        q_at = top[0]
        q = buf(1024, (4, 256))
        kk = buf(1024, (4, 256))
        v = buf(2048, (2, 1024))
        r = u
        gates = buf(4096, (16, 256))
        bcs = buf(1024, (4, 256))
        tmpm = buf(512)
        St = buf(3072, (3, 4, 256))
        attn = buf(1024, (2, 4, 128), at=xbase)
        qb = buf(1024, (4, 256))
        kdT = buf(1024, (2, 4, 128), at=xbase + 1024)
        a1 = tmpm[:, 0:256]
        tmp2 = [tmpm, buf(512)]
        small = buf(64)
        gates_flat = gates.rearrange("p a b -> p (a b)")
        St_flat = St.rearrange("p a b c -> p (a b c)")
        ada_slots += [(0, gates_flat[:, 0:SLOT], None), (1, gates_flat[:, SLOT:2 * SLOT], None), (2, St_flat[:, 0:SLOT], None),
                      (3, arena[:, q_at:q_at + SLOT], None)]
        w_ada = T["w_ada"][0]
        mods = ada(w_ada, 0, 2048, 0)
        run(mods, 1)
        t_n = norm_rows(h, t_h, t_xfree)
        run(mods, 1)
        t_n = norm_apply(h, t_h, t_n)
        oh_flat = v.rearrange("p a b -> p (a b)")[:, 0:1152]
        t_consts1 = [dma(consts1, T["consts"][:, NCONST0:NCONST0 + NCONST1]),
                     dma(oh_flat, T["consts"][:, NCONST0 + NCONST1:NCONST])]
        u64 = const("u64")
        masks = view(const("masks"), 7, 128)
        oh = view(oh_flat, 3, 384)

        rep = view(scr[:, 0:1152], 3, 384)
        t_rep = []
        for g in range(3):
            b, bank, free = take()
            last = mm(bank[0:6, 0:384], rtab[0:33, 6 * g:6 * g + 6], oh[0:33, g, :], True, True, free, t_cols, t_consts1)
            t = act(rep[0:6, g, :], bank[0:6, 0:384], ACT.Copy, last)
            bank_free[b] = t
            t_rep.append(t)
        rows = 18 * 384
        t_row = dma(bass.AP(scratch.tensor, P * rows, [[384, 6], [6 * 384, 3], [1, 384]]), rep[0:6, :, :], t_rep, eng="scalar")
        t_rep_out = dma(bass.AP(scratch.tensor, 0, [[rows, P], [1, rows]]),
                        bass.AP(scratch.tensor, P * rows, [[0, P], [1, rows]]), t_row, eng="gpsimd")
        run(mods, 2)
        finish(mods)
        w_in = T["w_in"][0]
        t_b = []

        t_q, t_k = {}, {}

        def put_q(m, ps, t):
            t_q[m] = act(q[:, m, :], ps, ACT.Copy, t, t_qk_free, scale=128.0 ** -0.5)
            return t_q[m]

        def put_k(m, ps, t):
            t_k[m] = act(kk[:, m, :], ps, ACT.Copy, t, t_qk_free)
            return t_k[m]
        q_in = pieces3(w_in, IN1["q"], 512, put_q, ("vector", "gpsimd"))
        run(q_in, 1)
        t_mod = ada_out(0, 16, col("b_ada", 0, 16))
        t_am = gain(0, "g_norm1", 8, t_mod)
        t_u = norm_scale(t_n, lambda k: am[:, k:k + 1], lambda k: mod[:, k:k + 1], u, t_am, t_mod, then_split=True)

        t_qk_free = [x[2] for x in ada_slots if x[0] == 3]
        ada_slots[:] = [x for x in ada_slots if x[0] != 3]
        mods = ada(w_ada, 2048, 3072, 16)

        t_a1one = fill(a1[0:17, :], 1.0)

        finish(q_in)
        k_in = pieces3(w_in, IN1["k"], 512, put_k, ("gpsimd",))
        run(k_in, 1)
        b, bank, free = take()
        for k in range(KT):
            last = mm(bank[0:16, 0:256], wa1[:, k, :], u[:, k, :], k == 0, k == KT - 1, free, t_cols, t_u)
        t_a1 = copy(a1[0:16, :], bank[0:16, 0:256], last, t_a1one)
        bank_free[b] = t_a1
        lgT = view(scr[:, 2048:3072], 2, 512)
        lx = view(scr[:, 3072:4096], 2, 512)
        lps = []
        for tc in range(2):
            b, bank, free = take()
            last = mm(bank[:, :], a1[0:17, tc * P:tc * P + P], wa2[0:17, :], True, True, free, t_a1, t_cols)
            lps.append((b, bank, last))
        tl = [copy(lgT[:, tc, :], lps[tc][1][:, :], lps[tc][2], t_rep_out) for tc in range(2)]
        tl = stt(lx, lgT, -1.0, lgT, ALU.mult, ALU.max, tl)
        tl = act(lx, lx, ACT.Exp, tl, scale=-1.0)
        tl = act(lx, lx, ACT.Ln, tl, bias=1.0)
        t_lg = []
        for tc in range(2):
            b, bank, last = lps[tc]
            t = stt(lgT[:, tc, :], bank[:, :], 0.0, lx[:, tc, :], ALU.min, ALU.subtract, tl)
            bank_free[b] = t
            t_lg.append(t)
        for _ in k_in:
            run(mods, 1)

        t_zpad = fill(zp[:, :, 0:30], 0.0, t_rep_out)
        t_sig = {}

        def put_sig(m, ps, t):
            t_sig[m] = act(sig[:, m, :], ps, ACT.Sigmoid, t)
            return t_sig[m]
        for _ in pieces3(w_in, IN1["gt"], 512, put_sig, ("gpsimd",)):
            run(mods, 1)
        for hh in range(4):
            b, bank, free = take()
            for tc in range(2):
                last = mm(bank[:, tc * P:tc * P + P], lgT[:, tc, hh * P:hh * P + P], u64, True, True,
                          free, t_lg[tc], t_consts1)
            t = copy(bcs[:, hh, :], bank[:, 0:256], last)
            bank_free[b] = t
            t_b.append(t)
        t_v = []

        def put_v(c, ps, t):
            t = act(v[:, :, c:c + 256], ps, ACT.Copy, t, t_rep, [x[2] for x in ada_slots])
            t_v.append(t)
            return t

        t_z = {}

        def put_z1(m, ps, t):
            t_z[m] = tt(zp[:, m, 30:286], ps, sig[:, m, :], ALU.mult, t, t_sig[m])
            return t_z[m]
        t_r, t_g = {}, {}

        def put_r(m, ps, t):
            t_r[m] = act(r[:, m, :], ps, ACT.Copy, t)
            return t_r[m]

        def put_g(m, ps, t):
            t_g[m] = act(gates[:, m, :], ps, ACT.Copy, t, [x[2] for x in ada_slots])
            return t_g[m]

        def fillers():
            yield from pieces3(w_in, IN1["a"], 512, put_z1, ("gpsimd",))
            yield from pieces3(w_in, IN1["r"], 1024, put_r, ("gpsimd",))
            yield from rows3(w_in, IN1["v"], 1024, put_v, ("gpsimd",))
            yield from pieces3(w_in, IN1["gates"], 2048, put_g, ("gpsimd",))
            flush()

        filler = fillers()

        dq, e1, e2, qe, ke = (scr[:, 1024 * i:1024 * i + 1024] for i in range(5))
        qf, kf, bf = (x.rearrange("p a b -> p (a b)") for x in (q, kk, bcs))
        t_mul = []

        def decays(li):
            m = LEVELS[li]
            n = 1024 // (2 * m)
            b3 = view(bf, n, 2 * m)
            t = tt(view(dq, n, 2 * m), b3, b3[:, :, m - 1:m].to_broadcast([P, n, 2 * m]), ALU.subtract, t_b, t_e)
            ta = act(e1, dq, ACT.Relu, t, t_mul, scale=-1.0)
            tb = act(e2, dq, ACT.Relu, t, t_mul)
            t_e[:] = [act(e1, e1, ACT.Exp, ta, scale=-1.0), act(e2, e2, ACT.Exp, tb, scale=-1.0)]
        t_e = []
        run(filler, 2)
        decays(0)
        t_q, t_k = list(t_q.values()), list(t_k.values())

        t_conv = [None] * 4

        def conv_taps():
            for m in range(4):
                t_conv[m] = ts(cacc[:, m, :], zp[:, m, 0:256], col("w_dw", m * 31), ALU.mult, col("b_dw", m), ALU.add,
                               t_z[m], t_zpad, t_cols)
            yield
            for j in range(1, 31):
                for m in range(4):
                    t_conv[m] = stt(cacc[:, m, :], zp[:, m, j:j + 256], col("w_dw", m * 31 + j), cacc[:, m, :],
                                    ALU.mult, ALU.add, t_conv[m])
                yield

        taps = conv_taps()
        t_attn = [None, None]
        t_free = []
        FILL = (3, 3, 2, 2, 2, 2, 2)
        TAPS = (4, 5, 5, 5, 5, 4, 3)
        STATES_AT = 5
        for li in range(7):
            if li < 6:
                ta = tt(qe, qf, e1, ALU.mult, t_e[0], t_q, t_free)
                tb = tt(ke, kf, e2, ALU.mult, t_e[1], t_k, t_free)
                qs, ks = view(qe, 4, 256), view(ke, 4, 256)
                t_in = [ta, tb]
                t_mul[:] = t_in
            else:
                qs, ks, t_in = q, kk, [t_q, t_k]
            t_free = []
            scored = []
            for tc in range(2):
                b, bank, free = take()
                for hh in range(4):
                    last = mm(bank[:, hh * P:hh * P + P], ks[:, hh, tc * P:tc * P + P], qs[:, hh, tc * P:tc * P + P],
                              True, True, free, t_in)
                t_free.append(last)
                scored.append((b, bank, last))
            if li < 5:
                decays(li + 1)
            for tc, (b, bank, last) in enumerate(scored):
                mk = masks[:, li:li + 1, :].to_broadcast([P, 4, P])
                if li == 0:
                    t = tt(attn[:, tc, :, :], view(bank[:, :], 4, P), mk, ALU.mult, last, t_consts1)
                    bank_free[b] = t
                else:
                    t = tt(view(tmp2[tc], 4, P), view(bank[:, :], 4, P), mk, ALU.mult, last, t_attn[tc])
                    bank_free[b] = t
                    t = tt(attn[:, tc, :, :], attn[:, tc, :, :], view(tmp2[tc], 4, P), ALU.add, t, eng="gpsimd")
                t_attn[tc] = t
            if li < 3:
                run(mods, 1)
            elif li == 3:
                finish(mods)
                t_ada_free = [x[2] for x in ada_slots]
            run(filler, FILL[li])
            if li == STATES_AT:
                t = act(e1, bf, ACT.Exp, t_b, t_mul)
                t_qb = tt(qb.rearrange("p a b -> p (a b)"), qf, e1, ALU.mult, t, t_q)
                b3 = view(bf, 16, 64)
                t = tt(view(dq, 16, 64), b3, b3[:, :, 63:64].to_broadcast([P, 16, 64]), ALU.subtract, t_b, t_e)
                t = act(e2, dq, ACT.Exp, t, t_mul, scale=-1.0)
                t_kd = tt(ke, kf, e2, ALU.mult, t, t_k, t_free)
                dec = small[:, 0:16]
                t_dec = act(dec, b3[:, :, 63], ACT.Exp, t_b)
                dec3 = view(dec, 4, 4)
                ke3 = view(ke, 4, 256)
                t_mul[:] = [t_qb, t_kd]
                t_e[:] = [t]
                t_kdT = []
                for tc in range(2):
                    b, bank, free = take()
                    for hh in range(4):
                        last = tp(bank[:, hh * P:hh * P + P], ke3[:, hh, tc * P:tc * P + P], ident, free, t_kd)
                    t_kdT_last = last
                    t = act(kdT[:, tc, :, :], view(bank[:, :], 4, P), ACT.Copy, last)
                    bank_free[b] = t
                    t_kdT.append(t)
                t_S = []
                for c in range(3):
                    tc, s0 = c // 2, 64 * (c % 2)
                    row = []
                    for g in range(2):
                        b, bank, free = take()
                        for j in range(2):
                            hh = 2 * g + j
                            last = mm(bank[:, j * 256:j * 256 + 256], kdT[s0:s0 + 64, tc, hh, :],
                                      v[s0:s0 + 64, tc, hh * 256:hh * 256 + 256], True, True, free, t_kdT[tc], t_v)
                        for j in range(2):
                            hh = 2 * g + j
                            ps = bank[:, j * 256:j * 256 + 256]
                            if c == 0:
                                t = copy(St[:, c, hh, :], ps, last, t_ada_free)
                            else:
                                t = stt(St[:, c, hh, :], St[:, c - 1, hh, :], dec3[:, hh, c:c + 1], ps, ALU.mult, ALU.add,
                                        last, t_dec, t_S[c - 1][hh])
                            row.append(t)
                        bank_free[b] = t
                    t_S.append(row)
                t_free += [t_kdT_last]
            run(taps, TAPS[li])
        t_lev = t_free
        finish(taps)

        b, bank, free = take()
        for m in range(4):
            last = mm(bank[:, 0:256], ones, cacc[:, m, :], m == 0, m == 3, free, t_conv[m])
        mu = tmpm[:, 0:256]
        t = ts(mu, bank[:, 0:256], 1.0 / 512, ALU.mult, None, None, last, t_attn)
        bank_free[b] = t
        t_c = tt(cacc, cacc, mu.rearrange("p (o n) -> p o n", o=1).to_broadcast([P, 4, 256]), ALU.subtract, t, last)
        t_s2 = act(sig, cacc, ACT.Square, t_c, list(t_z.values()))
        run(filler, 2)
        b, bank, free = take()
        for m in range(4):
            last = mm(bank[:, 0:256], ones, sig[:, m, :], m == 0, m == 3, free, t_s2)
        t_ln = last
        lnb = (b, bank)

        ss = small[:, 16:24]
        rs = small[:, 24:32]
        on = view(scr[:, 1024:3072], 2, 1024)
        junk = tmpm[:, 256:512]
        t_on = []
        obanks = []
        t_ss = None
        for tc in range(2):
            for g in range(2):
                b, bank, free = take()
                for j in range(2):
                    hh = 2 * g + j
                    last = mm(bank[:, j * 256:j * 256 + 256], attn[:, tc, hh, :], v[:, tc, hh * 256:hh * 256 + 256],
                              True, False, free, t_attn[tc], t_v, skip=True)
                    for s in range(2):
                        c = 2 * tc + s
                        if c:
                            last = mm(bank[64 * s:64 * s + 64, j * 256:j * 256 + 256], qb[:, hh, c * 64:c * 64 + 64],
                                      St[:, c - 1, hh, :], False, True, t_qb, t_S[c - 1][hh], skip=True)
                for j in range(2):
                    i = tc * 4 + 2 * g + j
                    t_ss = act(junk, bank[:, j * 256:j * 256 + 256], ACT.Square, last, t_ss, t_attn,
                               accum=ss[:, i:i + 1])
                obanks.append((b, bank, tc, g))
        t = act(rs, ss, ACT.Sqrt, t_ss, bias=eps, scale=1.0 / 256)
        t_mu = act(mu, lnb[1][:, 0:256], ACT.Sqrt, t_ln, t_c, bias=eps, scale=1.0 / 512)
        bank_free[lnb[0]] = t_mu
        t_rs = recip(rs, rs, t)
        for b, bank, tc, g in obanks:
            for j in range(2):
                hh = 2 * g + j
                t = ts(on[:, tc, hh * 256:hh * 256 + 256], bank[:, j * 256:j * 256 + 256],
                       rs[:, tc * 4 + hh:tc * 4 + hh + 1], ALU.mult, None, None, t_rs, t_lev, t_kd, t_qb)
            bank_free[b] = t
            t_on.append(t)
        t_mod = ada_out(16, 24, col("b_ada", 16, 24))
        t_am = gain(1, "g_norm2", 32, t_mod)

        def rest_of_ada():
            yield from ada(w_ada, 5120, 1024, 40, False)
            yield from ada(T["w_ada_f"], 0, 2048, 48, False)
        mods = rest_of_ada()
        ada_slots[:] = [(0, arena[:, q_at:q_at + SLOT], [t_qb, t_kd, t_ss]), (1, v.rearrange("p a b -> p (a b)"), t_ss),
                        (2, St_flat[:, 0:SLOT], t_ss)]
        run(mods, 1)
        t = recip(mu, mu, t_mu)
        t = tt(cacc, cacc, mu.rearrange("p (o n) -> p o n", o=1).to_broadcast([P, 4, 256]), ALU.mult, t, t_s2)
        finish(filler)
        t_cs = [act(sig[:, m, :], cacc[:, m, :], ACT.Silu, t, t_ln, scale=col("g_conv_ln", m), bias=col("b_conv_ln", m))
                for m in range(4)]
        t_rr = [act(r[:, 4 * g:4 * g + 4, :], r[:, 4 * g:4 * g + 4, :], ACT.Silu, [t_r[m] for m in range(4 * g, 4 * g + 4)])
                for g in range(2)]
        t_gg = [act(gates[:, 4 * g:4 * g + 4, :], gates[:, 4 * g:4 * g + 4, :], ACT.Sigmoid,
                    [t_g[m] for m in range(4 * g, 4 * g + 4)]) for g in range(4)]
        t_og = []
        for tc in range(2):
            for g in range(2):
                b, bank, free = take()
                for j in range(4):
                    m = 4 * g + j
                    last = tp(bank[:, j * P:j * P + P], on[:, tc, m * P:m * P + P], ident, free, t_on)
                for j in range(4):
                    m = 4 * g + j
                    t = stt(r[:, m, tc * P:tc * P + P], bank[:, j * P:j * P + P], col("g_gla_norm", m),
                            r[:, m, tc * P:tc * P + P], ALU.mult, ALU.mult, last, t_rr[g])
                bank_free[b] = t
                t_og.append(t)

        t_mg = {}

        def y_conv(m, ps, t):
            t_mg[m] = stt(gates[:, m, :], ps, col("b_conv_pw", m), gates[:, m, :], ALU.add, ALU.mult, t, t_gg[m // 4])
            return t_mg[m]
        project_cols(T["w_conv_pw"][0], 0, 1024, lambda k: sig[:, k, :], y_conv, t_cs, chunk=512)
        run(mods, 1)

        def y_gla(m, ps, t):
            t1 = tt(gates[:, 8 + m, :], ps, gates[:, 8 + m, :], ALU.mult, t, t_gg[2 + m // 4])
            t_mg[m] = tt(gates[:, m, :], gates[:, m, :], gates[:, 8 + m, :], ALU.add, t1, t_mg[m])
            return t1
        gla_out = pieces3(T["w_gla_o"][0], 0, 1024, y_gla)
        run(gla_out, 1)
        split_x(r, [[t_og[m // 4], t_og[2 + m // 4]] for m in range(8)])
        for i, _ in enumerate(gla_out):
            if i == 1:
                run(mods, 1)
        flush()

        t_h1 = {}

        def add_h(m, ps, t):
            t_h1[m] = stt(h[:, m, :], ps, mod[:, 16 + m:17 + m], h[:, m, :], ALU.mult, ALU.add, t, t_mod)
            return t_h1[m]
        t_mgl = [t_mg[m] for m in range(8)]
        mixer_out = pieces3(T["w_out"][0], 0, 1024, add_h)
        run(mixer_out, 1)
        split_x(gates, t_mgl)
        finish(mixer_out)
        flush()
        run(mods, 2)
        t_h = [t_h1[m] for m in range(8)]

        t_u = norm(h, t_h, t_xfree, lambda k: am[:, 8 + k:9 + k], lambda k: mod[:, 24 + k:25 + k], u, t_am, t_mod)
        end1 = t_u

        top[0] = base
        lg = buf(72, (2, 36))
        rt = buf(256)
        comb = buf(64, (2, 32))
        mask = buf(64, (2, 32))
        rank = buf(64, (2, 32))
        slotn = buf(64, (2, 32))
        combO = buf(64, (2, 32))
        cnt = buf(2)
        uT_at = top[0]
        uT = buf(2048, (2, 1024))
        hot = buf(2 * 32 * CAP, (2, 32, CAP))
        sendw = buf(512, (2, 2, 128))
        sendT = buf(512, (2, 256))
        xg = buf(2048, (2, 8, 128), at=xbase)
        s1 = buf(512)
        hid = buf(512)
        hidT = buf(1024, (2, 4, 128), at=aacc_at)
        ye = buf(2048, (2, 1024))
        moe_end = top[0]

        b, bank, free = take()
        lgps = bank[:, 0:72].rearrange("p (a b) -> p a b", a=2)
        for tc in range(2):
            for k in range(KT):
                last = mm(lgps[:, tc, :], u[:, k, tc * P:tc * P + P], wr[:, k, :], k == 0, k == KT - 1,
                          free, t_u, t_cols)
        t_l = tt(lg, lgps, col("router_b", 0, 36).rearrange("p (o n) -> p o n", o=1).to_broadcast([P, 2, 36]),
                 ALU.add, last, t_cols, end1)
        bank_free[b] = t_l
        run(mods, 1)
        t_uT = []
        for tc in range(2):
            for g in range(2):
                b, bank, free = take()
                for j in range(4):
                    last = tp(bank[:, j * P:j * P + P], u[:, 4 * g + j, tc * P:tc * P + P], ident, free, t_u)
                t = act(uT[:, tc, 512 * g:512 * g + 512], bank[:, :], ACT.Copy, last, end1)
                bank_free[b] = t
                t_uT.append(t)
        t_comb, t_mask = [], []
        steps = [[], []]
        for tc in range(2):
            w = rt[:, 128 * tc:128 * tc + 128]
            l4 = lg[:, tc, 0:4]
            le = lg[:, tc, 4:36]
            gm, wg, oh4, prev = w[:, 0:1], w[:, 1:2], w[:, 4:8], w[:, 8:9]
            ex, sel, tmp = w[:, 12:16], w[:, 16:24], w[:, 24:56]
            m8, oi, o1, o2, ws = w[:, 56:64], w[:, 64:66], w[:, 72:80], w[:, 80:88], w[:, 96:104]
            om = w[:, 104:112]
            ix = idxb[:, 8 * tc:8 * tc + 8]
            oh4b = oh4.rearrange("p (g o) -> p g o", o=1).to_broadcast([P, 4, 8])
            t_gm = op("vector", lambda e, gm=gm, l4=l4: e.reduce_max(gm, l4, AX), t_l)
            t = ts(ex, l4, gm, ALU.subtract, None, None, t_gm)
            t_ex = act(ex, ex, ACT.Exp, t, accum=wg)
            t_o = ts(oh4, l4, gm, ALU.is_equal, None, None, t_gm)
            t = copy(prev, oh4[:, 0:1], t_o)
            for i in range(1, 4):
                t_o = tt(tmp[:, 0:1], oh4[:, i:i + 1], prev, ALU.is_gt, t, t_o)
                t = tt(prev, prev, oh4[:, i:i + 1], ALU.max, t_o)
                t_o = copy(oh4[:, i:i + 1], tmp[:, 0:1], t)
            t = tt(view(tmp, 4, 8), view(le, 4, 8), oh4b, ALU.mult, t_o)
            t = op("vector", lambda e, sel=sel, tmp=tmp: e.reduce_sum(sel, tmp.rearrange("p (g e) -> p e g", g=4), AX), t)
            t = op("vector", lambda e, m8=m8, sel=sel: e.max(m8, sel), t)
            t_d = tt(ws[:, 0:1], m8[:, 1:2], m8[:, 0:1], ALU.subtract, t)
            t_e = act(ws[:, 1:2], ws[:, 0:1], ACT.Exp, t_d)
            t = op("vector", lambda e, ix=ix, m8=m8, sel=sel: e.max_index(ix, m8, sel), t)
            t = copy(oi, ix[:, 0:2], t)
            t1 = ts(o1, iota[:, 0:8], oi[:, 0:1], ALU.is_equal, None, None, t, t_consts)
            t2 = ts(o2, iota[:, 0:8], oi[:, 1:2], ALU.is_equal, None, None, t)
            t = tt(om, o1, o2, ALU.add, t1, t2)
            t_mask.append(tt(view(mask[:, tc, :], 4, 8), oh4b, om.rearrange("p (o e) -> p o e", o=1).to_broadcast([P, 4, 8]),
                             ALU.mult, t, t_o))
            t_wg = recip(wg, wg, t_ex)
            t = ts(ws[:, 2:3], ws[:, 1:2], 1.0, ALU.add, None, None, t_e)
            t = recip(ws[:, 3:4], ws[:, 2:3], t)
            t = tt(ws[:, 4:5], ws[:, 3:4], wg, ALU.mult, t, t_wg)
            t = tt(ws[:, 5:6], ws[:, 4:5], ws[:, 1:2], ALU.mult, t)
            t = ts(o1, o1, ws[:, 4:5], ALU.mult, None, None, t, t_mask)
            t = stt(o1, o2, ws[:, 5:6], o1, ALU.mult, ALU.add, t)
            t_comb.append(tt(view(comb[:, tc, :], 4, 8), oh4b,
                             o1.rearrange("p (o e) -> p o e", o=1).to_broadcast([P, 4, 8]), ALU.mult, t))

        b, bank, free = take()
        mm(bank[:, 0:32], before, mask[:, 0, :], True, True, free, t_mask, t_consts)
        mm(bank[:, 32:64], ones, mask[:, 0, :], True, False)
        mm(bank[:, 32:64], before, mask[:, 1, :], False, True)
        mm(bank[:, 64:96], ones, mask[:, 0, :], True, False)
        last = mm(bank[:, 64:96], ones, mask[:, 1, :], False, True)
        t = copy(rank, view(bank[:, 0:64], 2, 32), last)
        t_cnt = op("vector", lambda e, i=bank[:, 64:96]: e.reduce_max(cnt[:, 0:1], i, AX), last)
        bank_free[b] = t_cnt
        t_flag = ts(idxb[:, 16:17], cnt[:, 0:1], CAP + 0.5, ALU.is_gt, None, None, t_cnt)
        t_r1 = stt(slotn, rank, 1.0, mask, ALU.add, ALU.mult, t)
        t_r2 = ts(slotn, slotn, -1.0, ALU.add, None, None, t_r1)
        t_hot = []
        for tc in range(2):
            t_hot.append(tt(hot[:, tc, :, :], slotn[:, tc, :].rearrange("p (e o) -> p e o", o=1).to_broadcast([P, 32, CAP]),
                            iota[:, 0:CAP].rearrange("p (o c) -> p o c", o=1).to_broadcast([P, 32, CAP]), ALU.is_equal,
                            t_r2))
        w1v, w3v, w2v = (T[n][0].rearrange("(j e) (t p) n -> j p e t n", e=2, p=P) for n in ("w1", "w3", "w2"))
        hot2 = hot.rearrange("p t e c -> p t (e c)")
        t_xg = [t_u, t_u]
        t_hT = [None, None]
        t_sc = [None, None]
        t_sw = [None, None]
        t_s1 = None

        above = upper("above", F32)
        wides = [above[:, WIDE * i:WIDE * i + WIDE] for i in range(FINE // WIDE)]
        wide_free = [t_h] * len(wides)
        wides.append(arena[:, 0:WIDE])
        wide_free.append(t_h)
        while top[0] + WIDE <= ARENA:
            wides.append(buf(WIDE))
            wide_free.append(end1 + [x[2] for x in ada_slots])
        NW = len(wides)
        wide_sem = [new_sem("wide") for _ in range(NW)]
        wide_use = [0] * NW
        wide_n = [0]

        def load_pair(src, kts, n):
            s = wide_n[0] % NW
            wide_n[0] += 1
            dst = wides[s].rearrange("p (e t n) -> p e t n", e=2, t=kts)
            for i in range(2):
                op("sync", lambda e, i=i: e.dma_start(dst[:, i, :, :], src[:, i, :, :]), wide_free[s], sem=wide_sem[s])
            wide_use[s] += 2
            return dst, Landed(wide_sem[s], 16 * wide_use[s]), s

        def gather(pair):
            i = pair % 2
            toks = []
            for g in range(2):
                b, bank, free = take()
                for j in range(4):
                    k = 4 * g + j
                    for tc in range(2):
                        last = mm(bank[:, j * P:j * P + P], uT[:, tc, k * P:k * P + P], hot2[:, tc, pair * P:pair * P + P],
                                  tc == 0, tc == 1, free, t_uT, t_hot)
                t = copy(xg[:, i, 4 * g:4 * g + 4, :], view(bank[:, :], 4, P), last, t_xg[i])
                bank_free[b] = t
                toks.append(t)
            return toks

        t_in = gather(0)
        bank_set[0] = [0, 1, 2, 3]
        for pair in range(16):
            i = pair % 2
            up = []
            for wv in (w1v, w3v):
                b, bank, free = take()
                for th in range(2):
                    slot, landed, s = load_pair(wv[pair, :, :, 4 * th:4 * th + 4, :], 4, 512)
                    for k in range(4):
                        for e in range(2):
                            last = mm(bank[64 * e:64 * e + 64, :], xg[:, i, 4 * th + k, 64 * e:64 * e + 64], slot[:, e, k, :],
                                      th == 0 and k == 0, th == 1 and k == 3, free, landed, t_in[th], skip=True)
                    wide_free[s] = last
                up.append((b, bank, last))
            t_xg[i] = last
            if pair == 0:
                finish(mods)
                t_mod2 = ada_out(40, 24, col("b_ada", 40, 24))
                t_am = gain(2, "g_final", 56, t_mod2)
                t = ts(combO, rank, CAP - 0.5, ALU.is_gt, None, None, t_r1)
                t_combO = tt(combO, combO, comb, ALU.mult, t, t_comb)

                acc_free = [bank_free[n] for n in range(4, 8)]
            ta = act(s1, up[0][1][:, :], ACT.Silu, up[0][2], t_s1)
            bank_free[up[0][0]] = ta
            t_s1 = tt(hid, s1, up[1][1][:, :], ALU.mult, ta, up[1][2], t_hT)
            bank_free[up[1][0]] = t_s1
            if pair < 15:
                t_in = gather(pair + 1)
            t = tt(sendw[:, i, :, :].rearrange("p t (e c) -> p t e c", e=2), hot[:, :, 2 * pair:2 * pair + 2, :],
                   comb[:, :, 2 * pair:2 * pair + 2].rearrange("p t (e o) -> p t e o", o=1).to_broadcast([P, 2, 2, CAP]),
                   ALU.mult, t_hot, t_comb, t_sw[i])
            b, bank, free = take()
            for tc in range(2):
                t_sw[i] = tp(bank[:, tc * P:tc * P + P], sendw[:, i, tc, :], ident, free, t)
            t_send = act(sendT[:, i, :], bank[:, 0:256], ACT.Copy, t_sw[i], t_sc[i])
            bank_free[b] = t_send
            b, bank, free = take()
            for j in range(4):
                last = tp(bank[:, j * P:j * P + P], hid[:, j * P:j * P + P], ident, free, t_s1)
            t_hT[0] = last
            t = act(hidT[:, i, :, :], view(bank[:, :], 4, P), ACT.Copy, last, t_sc)
            bank_free[b] = t
            ob = [take() for _ in range(2)]
            for th in range(2):
                slot, landed, s = load_pair(w2v[pair, :, :, 2 * th:2 * th + 2, :], 2, 1024)
                for k in range(2):
                    for n in range(2):
                        for e in range(2):
                            last = mm(ob[n][1][64 * e:64 * e + 64, :], hidT[:, i, 2 * th + k, 64 * e:64 * e + 64],
                                      slot[:, e, k, 512 * n:512 * n + 512], th == 0 and k == 0, th == 1 and k == 1,
                                      t, landed, ob[n][2], skip=True)
                wide_free[s] = last
            t0 = act(ye[:, i, 0:512], ob[0][1][:, :], ACT.Copy, last, t_sc[i])
            t1 = copy(ye[:, i, 512:1024], ob[1][1][:, :], last, t_sc[i])
            bank_free[ob[0][0]], bank_free[ob[1][0]] = t0, t1
            for m in range(8):
                o = banks[4 + m // 2][:, (m % 2) * 256:(m % 2) * 256 + 256]
                last = mm(o, ye[:, i, m * P:m * P + P], sendT[:, i, :], pair == 0 and m % 2 == 0, pair == 15,
                          t0 if m < 4 else t1, t_send, acc_free if pair == 0 else None, skip=True)
            t_sc[i] = last
        t_acc = t_acc_free = last

        kept = (list(wide_free), list(bank_free))
        begin(t_flag, idxb[0:1, 16:17])
        combT = buf(256, at=xbase + 1024)
        combB = buf(8192, (32, 256), at=uT_at + 2048)
        assert uT_at + 2048 + 8192 <= moe_end
        hidG = buf(2048, (2, 4, 256), at=uT_at)
        sG = buf(1024, (2, 512), at=xbase)
        gsem = [new_sem("general") for _ in range(NW)]
        guse = [0] * NW

        def load_general(src, kt, n):
            s = wide_n[0] % NW
            wide_n[0] += 1
            dst = view(wides[s][:, 0:kt * n], kt, n)
            op("sync", lambda e: e.dma_start(dst, src), wide_free[s], sem=gsem[s])
            guse[s] += 1
            return dst, Landed(gsem[s], 16 * guse[s]), s

        b, bank, free = take()
        for tc in range(2):
            last = tp(bank[0:32, tc * P:tc * P + P], combO[:, tc, :], ident, free, t_combO)
        t_cT = copy(combT[0:32, :], bank[0:32, 0:256], last, t_acc)
        bank_free[b] = t_cT
        t_cB = []
        for e0 in range(0, NE, 2):
            b, bank, free = take()
            for j in range(2):
                last = mm(bank[:, j * 256:j * 256 + 256], ident[0:32, e0 + j:e0 + j + 1].to_broadcast([32, P]),
                          combT[0:32, :], True, True, free, t_cT)
            t = copy(combB[:, e0:e0 + 2, :], view(bank[:, :], 2, 256), last, t_acc)
            bank_free[b] = t
            t_cB.append(t)
        t_down = [None, None]
        t_sG = [None, None]
        for e in range(NE):
            hb = e % 2
            wsrc = [T[n][0, e].rearrange("(t p) n -> p t n", p=P) for n in ("w1", "w3", "w2")]
            w1, l1, n1 = load_general(wsrc[0], 8, 512)
            w3, l3, n3 = load_general(wsrc[1], 8, 512)
            w2, l2, n2 = load_general(wsrc[2], 4, 1024)
            t_hid = []
            for g in range(2):
                b1, bank1, free1 = take()
                for j in range(2):
                    m = 2 * g + j
                    for k in range(KT):
                        last1 = mm(bank1[:, j * 256:j * 256 + 256], w1[:, k, m * P:m * P + P], u[:, k, :],
                                   k == 0, k == KT - 1, free1, l1, t_u)
                b3, bank3, free3 = take()
                for j in range(2):
                    m = 2 * g + j
                    for k in range(KT):
                        last3 = mm(bank3[:, j * 256:j * 256 + 256], w3[:, k, m * P:m * P + P], u[:, k, :],
                                   k == 0, k == KT - 1, free3, l3)
                ta = act(sG[:, g, :], bank1[:, :], ACT.Silu, last1, t_sG[g], t_acc)
                bank_free[b1] = ta
                hv = hidG[:, hb, 2 * g:2 * g + 2, :]
                tb = tt(hv, view(sG[:, g, :], 2, 256), view(bank3[:, :], 2, 256), ALU.mult, ta, last3, t_down[hb], t_acc)
                bank_free[b3] = tb
                t_sG[g] = tb
                t_hid.append(tt(hv, hv, combB[:, e:e + 1, :].to_broadcast([P, 2, 256]), ALU.mult, tb, t_cB[e // 2]))
            wide_free[n1], wide_free[n3] = last1, last3
            for m in range(8):
                o = banks[4 + m // 2][:, (m % 2) * 256:(m % 2) * 256 + 256]
                for k in range(4):
                    last = mm(o, w2[:, k, m * P:m * P + P], hidG[:, hb, k, :], False, e == NE - 1 and k == 3,
                              l2, t_hid[k // 2], t_acc, skip=True)
            t_down[hb] = last
            wide_free[n2] = last
        end()
        wide_free[:], bank_free[:] = kept

        t_h = []
        for m in range(8):
            o = banks[4 + m // 2][:, (m % 2) * 256:(m % 2) * 256 + 256]
            t = stt(h[:, m, :], o, mod[:, 40 + m:41 + m], h[:, m, :], ALU.mult, ALU.add, t_acc, t_mod2)
            t_h.append(t)
            bank_free[4 + m // 2] = t

        ring_free[0:2] = [wide_free[3]] * 2
        fine_memory("fine2")
        xs_free[:] = [t_acc_free] * 2
        w_free[:] = [t_acc_free] * NU
        w_in = T["w_in_2"][0]
        t_q, t_k = {}, {}
        q_in = pieces3(w_in, IN2["q"], 1152, lambda m, ps, t: put_q(m, ps, t))
        run(q_in, 1)
        t_h = norm(h, t_h, t_uT, lambda k: am[:, 16 + k:17 + k], lambda k: mod[:, 48 + k:49 + k], h, t_am, t_mod2)
        bank_set[0] = list(range(8))

        t_u = norm(h, t_h, t_h, lambda k: col("ln1_g_2", k), None, u, t_cols, then_split=True)
        end2 = t_u + [t_acc_free]
        top[0] = base
        merged = u
        dtx = buf(32)
        dtt = buf(192)
        dx, dl, da, dcs, dd = (dtt[:, 32 * i:32 * i + 32] for i in range(5))
        an = dtt[:, 160:176]
        gate_b = [buf(2048, (8, 256)) for _ in range(2)]
        zs = buf(2048, (8, 256))
        p0 = buf(8 * 264, (8, 264))
        base2 = top[0]

        t_gb = [{}, {}, {}]

        def branch_gate(i, *w):
            def evac(m, ps, t):
                t_gb[i][m] = act(gate_b[i % 2][:, m, :], ps, ACT.Identity, t, w, bias=col("b_gate_2", 8 * i + m))
                return t_gb[i][m]
            return pieces3(w_in, IN2["gates"] + 1024 * i, 1024, evac, ("gpsimd",))

        def gate_on(i):
            g = gate_b[i % 2]
            for n in range(2):
                t = act(g[:, 4 * n:4 * n + 4, :], g[:, 4 * n:4 * n + 4, :], ACT.Sigmoid,
                        [t_gb[i][m] for m in range(4 * n, 4 * n + 4)])
                for m in range(4 * n, 4 * n + 4):
                    t_gb[i][m] = t

        q = buf(2304, (9, 256))
        kk = buf(2304, (9, 256))
        vT = buf(2304, (2, 1152))
        toep = buf(18 * 256, (18, 256))
        scs = [buf(768) for _ in range(2)]
        pTs = [buf(768) for _ in range(2)]
        ya = buf(768, (2, 384))
        yaF = q[:, 0:3, :]
        sm = buf(64)
        toep4 = toep.rearrange("p (g h) n -> p g h n", g=3)


        def put_q(m, ps, t):
            t_q[m] = act(q[:, m, :], ps, ACT.Copy, t, end2, scale=0.125)
            return t_q[m]

        def put_k(m, ps, t):
            t_k[m] = copy(kk[:, m, :], ps, t, end2)
            return t_k[m]
        finish(q_in)
        t_toep = dma(toep, bass.AP(scratch.tensor, 127, [[rows - 1, P], [384, 18], [1, 256]]), t_rep_out, end2)
        finish(pieces3(w_in, IN2["k"], 1152, put_k))

        t_v = []
        t_pad = [fill(p0[:, :, 0:8], 0.0, end2)]
        t_p0, t_z = {}, {}

        def put_p(m, ps, t):
            t_p0[m] = act(p0[:, m, 8:264], ps, ACT.Copy, t, end2)
            return t_p0[m]

        def put_z(m, ps, t):
            t_z[m] = act(zs[:, m, :], ps, ACT.Copy, t, end2)
            return t_z[m]

        def put_v(c, ps, t):
            t = act(vT[:, :, c:c + 256], ps, ACT.Copy, t, end2)
            t_v.append(t)
            return t

        def fillers2():
            yield from pieces3(w_in, IN2["pool"], 1024, put_p)
            yield from pieces3(w_in, IN2["z"], 1024, put_z)
            yield from branch_gate(0, end2)
            flush()

        filler = fillers2()
        finish(rows3(w_in, IN2["v"], 1024, put_v))
        flush()
        slot, landed, s = wcols(w_in, IN2["v"] + 1024, 128)
        b, bank, free = take()
        for tc in range(2):
            for k in range(KT):
                last = mm(bank[:, tc * P:tc * P + P], u[:, k, tc * P:tc * P + P], slot[:, k, :], k == 0, k == KT - 1,
                          free, landed, t_u)
        t = act(vT[:, :, 1024:1152], view(bank[:, 0:256], 2, P), ACT.Copy, last, end2)
        ring_free[s] = last
        bank_free[b] = t
        t_v.append(t)
        b, bank, free = take()
        for tc in range(2):
            for k in range(KT):
                last = mm(bank[:, 16 * tc:16 * tc + 16], u[:, k, tc * P:tc * P + P], wdt[:, k, :], k == 0, k == KT - 1,
                          free, t_cols, t_u)
        t_dtx = tt(view(dtx, 2, 16), view(bank[:, 0:32], 2, 16),
                   col("dt_bias", 0, 16).rearrange("p (o n) -> p o n", o=1).to_broadcast([P, 2, 16]), ALU.add, last, end2)
        bank_free[b] = t_dtx

        t_sc, t_pv = [None, None], [None, None]
        t_es = []
        lsum = sm[:, 16:28]
        jobs = [(ic, hh) for ic in range(2) for hh in range(6)]
        bank_set[0] = list(range(6))

        def scores(n):
            ic, hh = jobs[n]
            sc, i = scs[n % 2], n % 2
            nk = P * (ic + 1)
            t_s = []
            for gs in ((0, 1), (2,)):
                b, bank, free = take()
                for g in gs:
                    hd = 6 * g + hh
                    r0 = 64 * (hd % 2)
                    last = mm(bank[:, (g % 2) * nk:(g % 2) * nk + nk], q[r0:r0 + 64, hd // 2, ic * P:ic * P + P],
                              kk[r0:r0 + 64, hd // 2, 0:nk], True, True, free, t_q[hd // 2], t_k[hd // 2])
                m = len(gs)
                t = tt(view(sc[:, gs[0] * nk:(gs[0] + m) * nk], m, nk), view(bank[:, 0:m * nk], m, nk),
                       toep4[:, gs[0]:gs[0] + m, hh, 256 - nk:256], ALU.add, last, t_toep, t_sc[i])
                bank_free[b] = t
                t_s.append(t)
            mx, lv = sm[:, n:n + 1], sm[:, 16 + n:17 + n]
            t = op("vector", lambda e: e.reduce_max(mx, sc[:, 0:3 * nk], AX), t_s)
            t = ts(mx, mx, -1.0, ALU.mult, None, None, t)
            return act(sc[:, 0:3 * nk], sc[:, 0:3 * nk], ACT.Exp, t, bias=mx, accum=lv)

        def values_of(n, t_e):
            ic, hh = jobs[n]
            sc, pT, i = scs[n % 2], pTs[n % 2], n % 2
            ob = 6 + ic
            nb = 3 * (ic + 1)
            t_p = []
            for j0 in range(0, nb, 4):
                m = min(4, nb - j0)
                b, bank, free = take()
                for j in range(m):
                    last = tp(bank[:, j * P:j * P + P], sc[:, (j0 + j) * P:(j0 + j + 1) * P], ident, free, t_e)
                t = copy(pT[:, j0 * P:(j0 + m) * P], bank[:, 0:m * P], last, t_pv[i])
                bank_free[b] = t
                t_p.append(t)
            t_sc[i] = last
            return t_p

        def weigh(n, t_p):
            ic, hh = jobs[n]
            pT, i = pTs[n % 2], n % 2
            ob = 6 + ic
            nb = 3 * (ic + 1)
            o = banks[ob][:, hh * 64:hh * 64 + 64]
            for j in range(nb):
                g, jc = j // (ic + 1), j % (ic + 1)
                hd = 6 * g + hh
                last = mm(o, pT[:, j * P:j * P + P], vT[:, jc, hd * 64:hd * 64 + 64], j == 0, j == nb - 1,
                          t_p, t_v, bank_free[ob])
            t_pv[i] = last

        t_e = scores(0)
        t_ya = []
        held = None
        for n in range(12):
            nxt = scores(n + 1) if n < 11 else None
            run(filler, 1)
            t_p = values_of(n, t_e)
            t_es.append(t_e)
            if held is not None:
                weigh(n - 1, held)
                if n == 6:
                    ends = [t_pv[1]]
            held = t_p
            t_e = nxt
        weigh(11, held)
        for ic in range(2):
            ob = 6 + ic
            t = recip(lsum[:, 6 * ic:6 * ic + 6], lsum[:, 6 * ic:6 * ic + 6], t_es[6 * ic:6 * ic + 6])
            t = tt(view(ya[:, ic, :], 6, 64), view(banks[ob][:, 0:384], 6, 64),
                   lsum[:, 6 * ic:6 * ic + 6].rearrange("p (a o) -> p a o", o=1).to_broadcast([P, 6, 64]),
                   ALU.mult, t, t_pv)
            bank_free[ob] = t
            t_ya.append(t)
        t1 = act(dl, dtx, ACT.Abs, t_dtx)
        t1 = act(dl, dl, ACT.Exp, t1, scale=-1.0)
        t1 = act(dl, dl, ACT.Ln, t1, bias=1.0)
        t_dt = stt(dx, dtx, 0.0, dl, ALU.max, ALU.add, t1)
        t_an = act(an, col("a_log", 0, 16), ACT.Exp, t_cols)
        t_da = stt(view(da, 2, 16), view(dx, 2, 16), -1.0,
                   an.rearrange("p (o n) -> p o n", o=1).to_broadcast([P, 2, 16]), ALU.mult, ALU.mult, t_dt, t_an)
        finish(filler)
        bank_set[0] = list(range(8))
        xb_in = pieces3(w_in, IN2["xbc"], 1536, lambda m, ps, t: put_x(m, ps, t), ("gpsimd",))
        run(xb_in, 1)
        t_yaF = []
        for tc in range(2):
            b, bank, free = take()
            for j in range(3):
                last = tp(bank[:, j * P:j * P + P], ya[:, tc, j * P:j * P + P], ident, free, t_ya[tc])
            t = copy(yaF[:, :, tc * P:tc * P + P], view(bank[:, 0:384], 3, P), last)
            bank_free[b] = t
            t_yaF.append(t)
        t_m = {}

        def first_branch(m, ps, t):
            t_m[m] = tt(merged[:, m, :], ps, gate_b[0][:, m, :], ALU.mult, t, t_gb[0][m], end2)
            return t_m[m]
        end_a = t_yaF + [last]

        def next_branch(i):
            def evac(m, ps, t):
                g = gate_b[i % 2]
                t1 = tt(g[:, m, :], ps, g[:, m, :], ALU.mult, t, t_gb[i][m])
                t_m[m] = tt(merged[:, m, :], merged[:, m, :], g[:, m, :], ALU.add, t1, t_m[m])
                return t1
            return evac

        top[0] = base2
        over = top[0]
        top[0] = over + 768
        p1, p2 = (buf(8 * 264, (8, 264)) for _ in range(2))
        pd = buf(2048, (8, 256))
        py = p0.rearrange("p a b -> p (a b)")[:, 0:2048].rearrange("p (a b) -> p a b", a=8)
        xb = buf(12 * 259, (12, 259))
        xc = buf(3072, (12, 256))
        t_pad += [fill(x[:, :, 0:8], 0.0, end_a) for x in (p1, p2)]
        t = tt(p1[:, :, 8:264], p0[:, :, 8:264], p0[:, :, 7:263], ALU.add, list(t_p0.values()), t_pad, end_a)
        t = tt(p2[:, 2:8, 8:264], p1[:, 2:8, 8:264], p1[:, 2:8, 6:262], ALU.add, t)
        t = tt(p1[:, 4:8, 8:264], p2[:, 4:8, 8:264], p2[:, 4:8, 4:260], ALU.add, t)
        t = tt(p2[:, 6:8, 8:264], p1[:, 6:8, 8:264], p1[:, 6:8, 0:256], ALU.add, t)
        t_pd = []
        for g in range(4):
            src = (p1, p2)[g % 2]
            o = pd[:, 2 * g:2 * g + 2, :]
            ti = tt(o, src[:, 2 * g:2 * g + 2, 8:264], invcnt[:, g:g + 1, :].to_broadcast([P, 2, 256]), ALU.mult, t)
            t_pd.append(tt(o, o, p0[:, 2 * g:2 * g + 2, 8:264], ALU.subtract, ti))
        t_xp = fill(xb[:, :, 0:3], 0.0, end_a)
        t_xb = {}

        def put_x(m, ps, t):
            t_xb[m] = act(xb[:, m, 3:259], ps, ACT.Copy, t, end_a)
            return t_xb[m]
        finish(xb_in)
        flush()
        b, bank, free = take()
        last = mm(bank[:, 0:32], u128, da, True, True, free, t_da)
        last = mm(bank[:, 32:48], ones, da[:, 0:16], True, True)
        t_cs = copy(dcs, bank[:, 0:32], last)
        t = tt(dd[:, 0:16], bank[:, 32:48], dcs[:, 0:16], ALU.subtract, t_cs)
        bank_free[b] = t
        t_dd = act(dd[:, 0:16], dd[:, 0:16], ACT.Exp, t)
        gate1 = branch_gate(1)
        run(gate1, 1)
        gate_on(0)
        attn_out = pieces(T["w_a_2"][0], 0, 1024, lambda k: yaF[:, k, :], first_branch, t_yaF, chunk=512)
        finish(attn_out)
        t_wa = queue["tensor"][-1][2]
        slot, landed, s = load(T["pool_w_2"][0].rearrange("g (t p) n -> p (g t) n", p=P), 8, 256)
        t_py = []
        for g in range(4):
            b, bank, free = take()
            for j in range(2):
                for k in range(2):
                    last = mm(bank[:, j * 256:j * 256 + 256], slot[:, 2 * g + k, j * P:j * P + P], pd[:, 2 * g + k, :],
                              k == 0, k == 1, free, landed, t_pd[g])
            for j in range(2):
                t = act(py[:, 2 * g + j, :], bank[:, j * 256:j * 256 + 256], ACT.Copy, last, t_pd,
                        scale=col("pool_scale_2", 2 * g + j))
            bank_free[b] = t
            t_py.append(t)
        ring_free[s] = last
        end_p = [last, t_wa] + t_py

        t_xc = []
        for m0 in range(0, 12, 4):
            tl = [ts(xc[:, m, :], xb[:, m, 0:256], col("ssd_conv_w_2", 4 * m), ALU.mult, col("ssd_conv_b_2", m), ALU.add,
                     t_xb[m], t_xp, end_a) for m in range(m0, m0 + 4)]
            for j in range(1, 4):
                tl = [stt(xc[:, m, :], xb[:, m, j:j + 256], col("ssd_conv_w_2", 4 * m + j), xc[:, m, :], ALU.mult, ALU.add,
                          tl[m - m0]) for m in range(m0, m0 + 4)]
            run(gate1, 1)
            t_xc.append(act(xc[:, m0:m0 + 4, :], xc[:, m0:m0 + 4, :], ACT.Silu, tl))
        t_zs = [act(zs[:, 4 * g:4 * g + 4, :], zs[:, 4 * g:4 * g + 4, :], ACT.Silu, [t_z[m] for m in range(4 * g, 4 * g + 4)])
                for g in range(2)]
        t_pc = list(t_m.values())

        top[0] = over
        xT2 = buf(2048, (2, 1024))
        xd = buf(1024)
        BT = buf(256)
        S0 = buf(1024)
        ys = xb.rearrange("p a b -> p (a b)")[:, 0:2048].rearrange("p (a b) -> p a b", a=8)
        cbm = buf(256, (2, 128))
        Lbs = [buf(512) for _ in range(2)]
        Cds = [buf(512) for _ in range(2)]
        assert top[0] <= over + 768 + 2 * 2112 + 2048
        finish(gate1)
        flush()

        t_xT = []
        for tc in range(2):
            for g in range(2):
                b, bank, free = take()
                for j in range(4):
                    m = 4 * g + j
                    last = tp(bank[:, j * P:j * P + P], xc[:, m, tc * P:tc * P + P], ident, free, t_xc[g])
                t = tt(view(xT2[:, tc, 512 * g:512 * g + 512], 8, 64), view(bank[:, :], 8, 64),
                       dx[:, 16 * tc + 8 * g:16 * tc + 8 * g + 8].rearrange("p (a o) -> p a o", o=1)
                       .to_broadcast([P, 8, 64]), ALU.mult, last, t_dt, end_p)
                bank_free[b] = t
                t_xT.append(t)
        t_xd = tt(view(xd, 16, 64), view(xT2[:, 0, :], 16, 64),
                  dd[:, 0:16].rearrange("p (a o) -> p a o", o=1).to_broadcast([P, 16, 64]), ALU.mult, t_xT, t_dd, end_p)
        b, bank, free = take()
        for g in range(2):
            last = tp(bank[:, g * P:g * P + P], xc[:, 8 + g, 0:P], ident, free, t_xc[2])
        t_BT = copy(BT, bank[:, 0:256], last, end_p)
        bank_free[b] = t_BT
        gate_on(1)

        def fillers3():
            yield from branch_gate(2, t_pc)
            flush()
            pool_out = pieces3(T["w_b_2"][0], 0, 1024, next_branch(1), ("gpsimd",))
            run(pool_out, 1)
            split_x(py, [t_py[m // 2] for m in range(8)])
            yield
            yield from pool_out
            flush()

        filler = fillers3()
        run(filler, 1)
        SSD_FILL = (1, 1, 1, 1, 1, 0, 0, 0)
        t_S0 = []
        for g in range(2):
            b, bank, free = take()
            last = mm(bank[:, :], BT[:, g * P:g * P + P], xd[:, 512 * g:512 * g + 512], True, True, free, t_BT, t_xd)
            t = act(S0[:, 512 * g:512 * g + 512], bank[:, :], ACT.Copy, last, end_p)
            bank_free[b] = t
            t_S0.append(t)

        t_ys = []
        t_yy = [None, None]
        t_cbs = [None]
        t_cbu = []
        ssd_jobs = [(tc, g, hq) for tc in range(2) for g in range(2) for hq in range(2)]
        ready = {}

        def decayed(n):
            tc, g, hq = ssd_jobs[n]
            h0 = 8 * g + 4 * hq
            i = n % 2
            Lb, Cd = Lbs[i], Cds[i]
            if n % 4 == 0:
                b, bank, free = take()
                for gg in range(2):
                    last = mm(bank[:, gg * P:gg * P + P], xc[:, 8 + gg, tc * P:tc * P + P], xc[:, 10 + gg, tc * P:tc * P + P],
                              True, True, free, t_xc[2])
                t_cbs[0] = tt(cbm, view(bank[:, 0:256], 2, P), u128.rearrange("p (o n) -> p o n", o=1).to_broadcast([P, 2, P]),
                              ALU.mult, last, end_p, t_cbu)
                bank_free[b] = t_cbs[0]
            b, bank, free = take()
            for j in range(4):
                last = mm(bank[:, j * P:j * P + P],
                          da[:, 16 * tc + h0 + j:16 * tc + h0 + j + 1].to_broadcast([P, P]), u128, True, True,
                          free, t_da)
            for j in range(4):
                t = ts(Lb[:, j * P:j * P + P], bank[:, j * P:j * P + P],
                       dcs[:, 16 * tc + h0 + j:16 * tc + h0 + j + 1], ALU.subtract, 0.0, ALU.min,
                       last, t_cs, t_yy[i], end_p)
            t_L = act(Lb, Lb, ACT.Exp, t)
            if tc:
                t = act(Cd, bank[:, :], ACT.Exp, t, t_yy[i], end_p)
            bank_free[b] = t
            t_L = tt(view(Lb, 4, P), view(Lb, 4, P), cbm[:, g:g + 1, :].to_broadcast([P, 4, P]), ALU.mult, t_L, t_cbs[0])
            t_cbu[:] = [t_L]
            t_C = tt(view(Cd, 4, P), view(Cd, 4, P),
                     xc[:, 10 + g:11 + g, tc * P:tc * P + P].to_broadcast([P, 4, P]), ALU.mult, t, t_xc) if tc else None
            ready[n] = (t_L, t_C)

        def outputs(n):
            tc, g, hq = ssd_jobs[n]
            h0 = 8 * g + 4 * hq
            i = n % 2
            Lb, Cd = Lbs[i], Cds[i]
            t_L, t_C = ready[n]
            b, bank, free = take()
            for j in range(4):
                o = bank[64 * (j % 2):64 * (j % 2) + 64, (j // 2) * P:(j // 2) * P + P]
                hd = h0 + j
                last = mm(o, xT2[:, tc, hd * 64:hd * 64 + 64], Lb[:, j * P:j * P + P], True, not tc,
                          free, t_L, t_xT, skip=True)
                if tc:
                    last = mm(o, S0[:, hd * 64:hd * 64 + 64], Cd[:, j * P:j * P + P], False, True, t_C, t_S0, skip=True)
            t_yy[i] = last
            for j in range(2):
                m = h0 // 2 + j
                t = stt(ys[:, m, tc * P:tc * P + P], xc[:, m, tc * P:tc * P + P], col("ssd_d_2", m),
                        bank[:, j * P:j * P + P], ALU.mult, ALU.add, last, t_xc, end_p)
            bank_free[b] = t
            t_ys.append(t)

        decayed(0)
        for n in range(8):
            if n < 7:
                decayed(n + 1)
            run(filler, SSD_FILL[n])
            outputs(n)
        t_yq = []
        t_yz = []
        for g in range(2):
            t = tt(ys[:, 4 * g:4 * g + 4, :], ys[:, 4 * g:4 * g + 4, :], zs[:, 4 * g:4 * g + 4, :], ALU.mult, t_ys, t_zs)
            t_yz.append(t)
            t_yq.append(act(sq[:, 4 * g:4 * g + 4, :], ys[:, 4 * g:4 * g + 4, :], ACT.Square, t, t_u))
        t_yn = []
        run(filler, 2)
        for g in range(2):
            b, bank, free = take()
            for j in range(4):
                last = mm(bank[:, 0:256], ones, sq[:, 4 * g + j, :], j == 0, j == 3, free, t_yq[g])
            rr = Lbs[g][:, 0:256]
            t = act(rr, bank[:, 0:256], ACT.Sqrt, last, t_yy, bias=eps, scale=1.0 / 512)
            bank_free[b] = t
            t = recip(rr, rr, t)
            for j in range(4):
                m = 4 * g + j
                t_yn.append(stt(ys[:, m, :], ys[:, m, :], col("ssd_norm_w_2", m), rr, ALU.mult, ALU.mult, t, t_yq[g]))
        finish(filler)
        gate_on(2)
        ssd_out = pieces3(T["w_c_2"][0], 0, 1024, next_branch(2))
        run(ssd_out, 1)
        split_x(ys, t_yn)
        finish(ssd_out)
        flush()
        end_c = [t_m[m] for m in range(8)]

        t_h1 = {}

        def add_x(m, ps, t):
            t_h1[m] = tt(h[:, m, :], ps, h[:, m, :], ALU.add, t)
            return t_h1[m]
        mixer_out = pieces3(T["w_o_2"][0], 0, 1024, add_x)
        run(mixer_out, 1)
        split_x(merged, end_c)
        finish(mixer_out)
        flush()
        t_h = [t_h1[m] for m in range(8)]

        up = T["ffn_w_up_2"][0]
        up_in = pieces3(up, 0, 5632, None, ("vector", "gpsimd"), pair=lambda m0, ps, t: put_up(m0, ps, t))
        run(up_in, 1)
        t_u = norm(h, t_h, t_yn, lambda k: col("ln2_g_2", k), None, u, t_cols, then_split=True)
        top[0] = base2
        hid = buf(22 * 256, (22, 256))
        NP_ = 4
        pads = [buf(2 * 258, (2, 258)) for _ in range(NP_)]
        cv = [buf(512, (2, 256)) for _ in range(NP_)]
        t_pad = [fill(x[:, :, 0:2], 0.0, end_c) for x in pads]
        pad_free = [None] * NP_
        cv_free = [None] * NP_
        t_hid = {}
        def put_up(m0, bank, last):
            ms = [m0, m0 + 1]
            i = m0 // 2 % NP_
            pd_, cv_ = pads[i], cv[i]
            t = t_up = act(pd_[:, :, 2:258], bank, ACT.Copy, last, t_pad[i], pad_free[i], end_c)
            tl = [ts(cv_[:, j, :], pd_[:, j, 0:256], col("ffn_conv_w_2", 3 * ms[j]), ALU.mult,
                     col("ffn_conv_b_2", ms[j]), ALU.add, t, cv_free[i], end_c) for j in range(2)]
            for tap in range(1, 3):
                tl = [stt(cv_[:, j, :], pd_[:, j, tap:tap + 256], col("ffn_conv_w_2", 3 * ms[j] + tap), cv_[:, j, :],
                          ALU.mult, ALU.add, tl[j]) for j in range(2)]
            pad_free[i] = tl
            if ms[0] < 22:
                t = act(hid[:, ms[0]:ms[0] + 2, :], cv_, ACT.Silu, tl, end_c)
            else:
                o = hid[:, ms[0] - 22:ms[0] - 20, :]
                t = tt(o, o, cv_, ALU.mult, tl, t_hid[ms[0] - 22])
            cv_free[i] = t
            for m in ms:
                t_hid[m % 22] = t
            return t_up

        finish(up_in)
        flush()
        down = T["ffn_w_down_2"][0]
        abanks = [take() for _ in range(4)]
        low = ("vector", "gpsimd")
        down_end = [None] * 8
        xs_half = [xs_free[:]] * 4
        for t0 in range(0, 22, 2):
            slot, landed, s = wrows(down, t0, t0 + 2)
            at = 2 * (t0 // 2 % 4)
            t_x = split(fine["xh"][:, at:at + 2, :], fine["xl"][:, at:at + 2, :], hid[:, t0:t0 + 2, :], "gpsimd" if t0 < 4 else "vector",
                        t_hid[t0], t_hid[t0 + 1], xs_half[at // 2])
            ts_ = []
            for k in range(2):
                wh, wl, tok, wi = split_w(slot, k, 1, 1024, landed, low[k])
                ts_.append(tok)

                def products(t0=t0, k=k, wh=wh, wl=wl, tok=tok, wi=wi, at=at, t_x=t_x):
                    for m in range(8):
                        b, bank, free = abanks[m // 2]
                        for i, (w, x) in enumerate(((wh, "xh"), (wh, "xl"), (wl, "xh"))):
                            last = mm(bank[:, (m % 2) * 256:(m % 2) * 256 + 256], w[:, 0, m * P:m * P + P],
                                      fine[x][:, at + k, :], t0 + k == 0 and i == 0 and m % 2 == 0,
                                      t0 + k == 21 and i == 2, free, tok, t_x, skip=True)
                        down_end[m] = last
                    w_free[wi] = xs_half[at // 2] = xs_free[0] = last
                defer(products)
            ring_free[s] = ts_
        flush()
        last = xs_free[0]
        t_h = []
        for m in range(8):
            o = abanks[m // 2][1][:, (m % 2) * 256:(m % 2) * 256 + 256]
            t = tt(h[:, m, :], o, h[:, m, :], ALU.add, down_end[m | 1])
            t_h.append(t)
            bank_free[abanks[m // 2][0]] = t

        t_u = norm(h, t_h, None, lambda k: col("final_g_2", k), None, u, last, t_cols)
        outs = []
        for tc in range(2):
            for g in range(2):
                b, bank, free = take()
                for j in range(4):
                    last = tp(bank[:, j * P:j * P + P], u[:, 4 * g + j, tc * P:tc * P + P], ident, free, t_u)
                o = xT[:, tc, 512 * g:512 * g + 512]
                t = copy(o, bank[:, :], last)
                bank_free[b] = t
                outs.append(dma(out[0, tc * P:tc * P + P, 512 * g:512 * g + 512], o, t))
        op("sync", None, outs, t_rep_out)

        def key_of(w):
            return (w.key, w.at) if isinstance(w, Tok) else (w.sem, w.value)

        def needed(eng):
            seen, outer = {}, None
            for fn, waits, tok, sem in queue[eng]:
                best = {}
                for w in waits:
                    key, val = key_of(w)
                    if seen.get(key, -1) < val:
                        seen[key] = val
                        best[key] = w
                yield fn, list(best.values()), tok, sem
                if isinstance(fn, tuple):
                    if fn[0] == "if":
                        outer = dict(seen)
                    else:
                        seen = outer

        plan = {e: list(needed(e)) for e in engines}
        for e in engines:
            for _, waits, _, _ in plan[e]:
                for w in waits:
                    if isinstance(w, Tok):
                        w.used = True
        for e in engines:
            n = [0, 0]
            for _, _, tok, _ in plan[e]:
                n[tok.region] += tok.used
                tok.count = n[tok.region]

        block = ctx.enter_context(nc.Block())

        def emit(eng, e):
            guard = None
            for fn, waits, tok, sem in plan[eng]:
                for w in waits:
                    if isinstance(w, Tok):
                        e.wait_ge(done[w.key], w.count)
                    else:
                        e.wait_ge(w.sem, w.value)
                if fn is None:
                    continue
                if isinstance(fn, tuple):
                    if fn[0] == "if":
                        reg = e.alloc_register()
                        e.reg_load(reg, fn[1])
                        guard = e.If_ne(reg, 0)
                        guard.__enter__()
                    else:
                        guard.__exit__(None, None, None)
                    continue
                ins = fn(e)
                if sem is not None:
                    ins.then_inc(sem, 16)
                elif tok.used:
                    ins.then_inc(done[tok.key], 1)

        @block.sync
        def _(e):
            emit("sync", e)

        @block.gpsimd
        def _(e):
            emit("gpsimd", e)

        @block.scalar
        def _(e):
            emit("scalar", e)

        @block.vector
        def _(e):
            emit("vector", e)

        @block.tensor
        def _(e):
            emit("tensor", e)


DIRECT = ["x", "w_ada", "w_in", "w_conv_pw", "w_gla_o", "w_out", "w1", "w3", "w2", "w_ada_f", "w_in_2", "w_a_2", "pool_w_2", "w_b_2", "w_c_2", "w_o_2",
          "ffn_w_up_2", "ffn_w_down_2"]


def lay_columns(inputs):
    def fcol(v):
        return v.reshape(-1, P).T

    def taps(v):
        return v.reshape(v.shape[0], -1, P).transpose(2, 1, 0).reshape(P, -1)

    def pad(v):
        return np.concatenate([v, np.zeros((P - v.shape[0], v.shape[1]), np.float32)])

    def tiles(v):
        return v.reshape(-1, P, v.shape[1]).transpose(1, 0, 2).reshape(P, -1)

    def rows(v):
        return np.broadcast_to(v.reshape(1, -1), (P, v.size))

    a = {k: np.asarray(v) for k, v in inputs.items()}
    parts = {
        "w_dw": taps(a["w_dw"][0]), "ssd_conv_w_2": taps(a["ssd_conv_w_2"][0]),
        "ffn_conv_w_2": taps(a["ffn_conv_w_2"][0]),
        "ssd_d_2": fcol(np.repeat(a["ssd_d_2"][0], 64)),
        "router_b": rows(np.concatenate([a["b_router_g"][0], a["b_router_e"][0]])),
        "dt_bias": rows(a["ssd_dt_bias_2"][0]), "a_log": rows(a["ssd_a_log_2"][0]),
        "eps": np.full((P, 1), 1e-6, np.float32),
        "rtab": pad(np.concatenate([a["rel_bias_2"], np.ones((1, 18), np.float32)])),
        "w_a2": pad(np.concatenate([a["w_a2"][0], a["b_a2"]])),
        "w_a1": tiles(a["w_in"][0][:, IN1["a1"]:IN1["a1"] + 16]),
        "w_dt": tiles(a["w_in_2"][0][:, IN2["dt"]:IN2["dt"] + 16]),
        "w_r": tiles(np.concatenate([a["w_router_g"][0], a["w_router_e"][0]], 1)),
    }
    out = []
    for name, n in COLS:
        v = parts[name] if name in parts else fcol(a[name])
        assert v.shape == (P, n), (name, v.shape)
        out.append(v)
    return np.ascontiguousarray(np.concatenate(out, 1).astype(np.float32, copy=False))


def kernel(**inputs):
    import concourse.bacc as bacc
    from concourse.bass_utils import run_bass_kernel_spmd as run

    nc = bacc.Bacc("TRN2", target_bir_lowering=False, num_devices=1)
    arrays = {n: np.ascontiguousarray(np.asarray(inputs[n])) for n in DIRECT}
    arrays["cols"] = lay_columns(inputs)
    arrays["consts"] = constants()
    T, feed = {}, {}
    for n, a in arrays.items():
        feed["in_" + n] = a
        T[n] = nc.dram_tensor("in_" + n, a.shape, F32, kind="ExternalInput").ap()
    out = nc.dram_tensor("out_0", (1, S, D), F32, kind="ExternalOutput").ap()
    scratch = nc.dram_tensor("scratch", ((P + 1) * 18 * 384,), F32, kind="Internal").ap()
    build(nc, T, out, scratch)
    res = run(nc, [feed], core_ids=[0])
    return res.results[0]["out_0"]
```
